# Optimizing a Trainium2 kernel written in Bass

```python
import math
import jax, jax.numpy as jnp
from jax import lax
import numpy as np

D_MODEL = 1024
BATCH = 1
SEQ = 1024
DEPTH = 1
DEC_BATCH = 8
DEC_SEQ = 8
PAST_LEN = 1024
PAGE_SIZE = 128

N_MIXERS = 4
GROUP_WIDTH = D_MODEL // N_MIXERS
GROUP_HEADS = 4
HEAD_DIM = GROUP_WIDTH // GROUP_HEADS
HG_DK = HEAD_DIM
HG_DV = HEAD_DIM
GLA_DK = HEAD_DIM // 2
GLA_DV = HEAD_DIM
GLA_GATE_RANK = 16
GLA_GATE_NORM = 16.0
GLA_CHUNK = 32
RW_DECAY_RANK = 32
RW_A_RANK = 32
RW_GATE_RANK = 64
RW_PROJ = 3 * GROUP_WIDTH + RW_DECAY_RANK + RW_A_RANK + RW_GATE_RANK
RW_GN_EPS = 64e-5
SB_BLOCK = 128
SB_BIAS_INIT = -6.0
D_FF = 4 * D_MODEL
RMS_EPS = 1e-6
IN_WIDTHS = (GROUP_WIDTH, GROUP_WIDTH, GROUP_WIDTH, GROUP_WIDTH,
             RW_PROJ,
             GROUP_WIDTH, GROUP_WIDTH, GROUP_WIDTH,
             GROUP_HEADS * GLA_DK, GROUP_HEADS * GLA_DK, GROUP_WIDTH, GLA_GATE_RANK, GROUP_WIDTH)
IN_COLS = sum(IN_WIDTHS)
F32 = jnp.float32

kernel_name = 'hymba_style_hgrn2_rwkv7_stickbreak_gla_step'

def _rms(x, g):
    xf = x.astype(F32)
    y = xf * lax.rsqrt(jnp.mean(xf * xf, axis=-1, keepdims=True) + RMS_EPS)
    return (y * g.astype(F32)).astype(x.dtype)

def _split(a, widths):
    return jnp.split(a, np.cumsum(widths)[:-1].tolist(), axis=-1)

def _chunked_gla(q, k, v, log_g, s0):
    q, k, v, log_g = (t.astype(F32) for t in (q, k, v, log_g))
    B, T, H, _ = q.shape
    dv = v.shape[-1]
    C = math.gcd(GLA_CHUNK, T)
    n = T // C

    def to_chunks(a):
        return a.reshape(B, n, C, H, a.shape[-1]).transpose(1, 0, 3, 2, 4)

    causal = jnp.tril(jnp.ones((C, C), dtype=bool))

    def step(S, inp):
        qi, ki, vi, gi = inp
        b = jnp.cumsum(gi, axis=-2)
        diff = b[..., :, None, :] - b[..., None, :, :]
        decay = jnp.exp(jnp.where(causal[:, :, None], diff, -jnp.inf))
        att = jnp.einsum('bhtd,bhsd,bhtsd->bhts', qi, ki, decay)
        o = jnp.einsum('bhts,bhse->bhte', att, vi) + jnp.einsum('bhtd,bhde->bhte', qi * jnp.exp(b), S)
        b_last = b[..., -1, :]
        S = S * jnp.exp(b_last)[..., None] + jnp.einsum('bhsd,bhse->bhde', ki * jnp.exp(b_last[..., None, :] - b), vi)
        return S, o

    S, o = lax.scan(step, s0.astype(F32), (to_chunks(q), to_chunks(k), to_chunks(v), to_chunks(log_g)))
    o = o.transpose(1, 0, 3, 2, 4).reshape(B, T, H, dv)
    return o, S

def _hgrn2(hq, hf, hi, hg, lb, norm_w, s0):
    B, T, _ = hq.shape
    heads = lambda t: t.reshape(B, T, GROUP_HEADS, -1)
    hf = hf.astype(F32)
    q = jax.nn.silu(hq.astype(F32))
    log_f = jnp.logaddexp(jnp.log(lb), jnp.log1p(-lb) + jax.nn.log_sigmoid(hf))
    k = (1.0 - lb) * jax.nn.sigmoid(-hf)
    o, S = _chunked_gla(heads(q), heads(k), heads(hi), heads(log_f), s0)
    o = _rms(o, norm_w) * jax.nn.silu(heads(hg.astype(F32)))
    return o.reshape(B, T, GROUP_WIDTH), S

def _gla(gq, gk, gv, ga, gg, a2, a_b, norm_w, s0):
    B, T, _ = gq.shape
    heads = lambda t: t.reshape(B, T, GROUP_HEADS, -1)
    log_a = jax.nn.log_sigmoid(ga.astype(F32) @ a2.astype(F32) + a_b.astype(F32)) / GLA_GATE_NORM
    q = heads(gq.astype(F32)) * GLA_DK ** -0.5
    o, S = _chunked_gla(q, heads(gk), heads(gv), heads(log_a), s0)
    o = _rms(o, norm_w) * jax.nn.silu(heads(gg.astype(F32)))
    return o.reshape(B, T, GROUP_WIDTH), S

def _rwkv7(p, shift0, s0, mu, w0, w2, a0, a2, g2, k_k, k_a, r_k, ln_w, ln_b):
    B, T, _ = p.shape
    p = p.astype(F32)
    prev = jnp.concatenate([shift0.astype(F32)[:, None], p[:, :-1]], axis=1)
    xs = p + (prev - p) * mu.astype(F32)
    r, k, v, w_in, a_in, g_in = _split(xs, (GROUP_WIDTH, GROUP_WIDTH, GROUP_WIDTH, RW_DECAY_RANK, RW_A_RANK, RW_GATE_RANK))
    w = -jax.nn.softplus(-(w0.astype(F32) + jnp.tanh(w_in) @ w2.astype(F32))) - 0.5
    decay = jnp.exp(-jnp.exp(w))
    a = jax.nn.sigmoid(a0.astype(F32) + a_in @ a2.astype(F32))
    g = jax.nn.sigmoid(g_in) @ g2.astype(F32)
    heads = lambda t: t.reshape(B, T, GROUP_HEADS, HEAD_DIM)
    kk = heads(k * k_k.astype(F32))
    kk = kk / jnp.maximum(jnp.sqrt(jnp.sum(kk * kk, axis=-1, keepdims=True)), 1e-12)
    k = k * (1.0 + (a - 1.0) * k_a.astype(F32))
    r, k, v, a, decay = heads(r), heads(k), heads(v), heads(a), heads(decay)

    def step(S, inp):
        r_t, w_t, k_t, v_t, kk_t, a_t = inp
        sa = jnp.einsum('bhij,bhj->bhi', S, -kk_t)
        S = S * w_t[:, :, None, :] + sa[..., None] * (kk_t * a_t)[:, :, None, :] + v_t[..., None] * k_t[:, :, None, :]
        return S, jnp.einsum('bhij,bhj->bhi', S, r_t)

    tm = lambda t: jnp.moveaxis(t, 1, 0)
    S, y = lax.scan(step, s0.astype(F32), (tm(r), tm(decay), tm(k), tm(v), tm(kk), tm(a)))
    y = jnp.moveaxis(y, 0, 1)
    mean = jnp.mean(y, axis=-1, keepdims=True)
    var = jnp.mean(jnp.square(y - mean), axis=-1, keepdims=True)
    y = (y - mean) * lax.rsqrt(var + RW_GN_EPS) * ln_w.astype(F32).reshape(GROUP_HEADS, HEAD_DIM) \
        + ln_b.astype(F32).reshape(GROUP_HEADS, HEAD_DIM)
    y = y + jnp.sum(r * k * r_k.astype(F32), axis=-1, keepdims=True) * v
    out = y.reshape(B, T, GROUP_WIDTH) * g
    return out, S, p[:, -1].astype(shift0.dtype)

def _stick_breaking(q, k, v, q_pos0, bias):
    Tq, Tk = q.shape[1], k.shape[1]
    z = jnp.einsum('bqhd,bkhd->bhqk', q.astype(F32), k.astype(F32)) * HEAD_DIM ** -0.5 \
        + bias.astype(F32)[None, :, None, None]
    qpos = q_pos0 + jnp.arange(Tq)
    kpos = jnp.arange(Tk)
    mask = kpos[None, :] < qpos[:, None]
    log_1m = jnp.where(mask, jax.nn.log_sigmoid(-z), 0.0)
    between = lax.cumsum(log_1m, axis=3, reverse=True) - log_1m
    weights = jnp.exp(jnp.where(mask, jax.nn.log_sigmoid(z) + between, -jnp.inf))
    return jnp.einsum('bhqk,bkhd->bqhd', weights, v.astype(F32))

def _sb_blocks(q, k_all, v_all, pos0, bias):
    T = q.shape[1]
    outs = []
    for b0 in range(0, T, SB_BLOCK):
        b1 = min(b0 + SB_BLOCK, T)
        n_keys = pos0 + b1
        outs.append(_stick_breaking(q[:, b0:b1], k_all[:, :n_keys], v_all[:, :n_keys], pos0 + b0, bias))
    return jnp.concatenate(outs, axis=1)

def _layer(x, pos0, lb, hg_s0, rw_s0, rw_shift0, gla_s0, past_k, past_v, P):
    B, T, _ = x.shape
    h = _rms(x, P['norm_mix_pre'])
    proj = jnp.einsum('btd,dc->btc', h, P['w_in'])
    hq, hf, hi, hg, rw, sq, sk, sv, gq, gk, gv, ga, gg = _split(proj, IN_WIDTHS)
    o_hg, hg_S = _hgrn2(hq, hf, hi, hg, lb, P['hg_norm'], hg_s0)
    o_rw, rw_S, rw_shift = _rwkv7(rw, rw_shift0, rw_s0, P['rw_mu'], P['rw_w0'], P['rw_w2'], P['rw_a0'], P['rw_a2'],
                                  P['rw_g2'], P['rw_k_k'], P['rw_k_a'], P['rw_r_k'], P['rw_ln_w'], P['rw_ln_b'])
    q_h = sq.reshape(B, T, GROUP_HEADS, HEAD_DIM)
    k_h = sk.reshape(B, T, GROUP_HEADS, HEAD_DIM)
    v_h = sv.reshape(B, T, GROUP_HEADS, HEAD_DIM)
    if past_k is None:
        k_all, v_all = k_h, v_h
    else:
        k_all = jnp.concatenate([past_k.astype(k_h.dtype), k_h], axis=1)
        v_all = jnp.concatenate([past_v.astype(v_h.dtype), v_h], axis=1)
    o_sb = _sb_blocks(q_h, k_all, v_all, pos0, P['sb_bias']).reshape(B, T, GROUP_WIDTH)
    o_gla, gla_S = _gla(gq, gk, gv, ga, gg, P['gla_a2'], P['gla_a_b'], P['gla_norm'], gla_s0)
    mix = jnp.concatenate([o_hg, o_rw, o_sb, o_gla], axis=-1).astype(x.dtype)
    x = x + _rms(jnp.einsum('btc,cd->btd', mix, P['w_out']), P['norm_mix_post'])
    h2 = _rms(x, P['norm_ffn_pre'])
    u = jnp.square(jax.nn.relu(jnp.einsum('btd,df->btf', h2, P['w_up'])))
    x = x + _rms(jnp.einsum('btf,fd->btd', u, P['w_down']), P['norm_ffn_post'])
    return (x, k_h, v_h, hg_S.astype(hg_s0.dtype), rw_S.astype(rw_s0.dtype), rw_shift, gla_S.astype(gla_s0.dtype))

def setup_inputs(seed: int = 0) -> dict:
    key = jax.random.key(seed)
    ks = iter(jax.random.split(key, 48))
    nrm = lambda shape, s: jax.random.normal(next(ks), shape, jnp.float32) * s
    n_pages = PAST_LEN // PAGE_SIZE
    n_used = DEC_BATCH * n_pages
    n_pool = n_used + max(1, n_used // 4)
    H = GROUP_HEADS
    x_prompt = nrm((BATCH, SEQ, D_MODEL), 1.0)
    x_sample = nrm((DEC_BATCH, DEC_SEQ, D_MODEL), 1.0)
    cache_sb_k = nrm((DEPTH, n_pool, PAGE_SIZE, H, HEAD_DIM), 1.0)
    cache_sb_v = nrm((DEPTH, n_pool, PAGE_SIZE, H, HEAD_DIM), 1.0)
    page_table = jax.random.permutation(next(ks), n_pool)[:n_used].reshape(DEC_BATCH, n_pages).astype(jnp.int32)
    state_hgrn = nrm((DEPTH, DEC_BATCH, H, HG_DK, HG_DV), 0.5)
    state_rwkv = nrm((DEPTH, DEC_BATCH, H, HEAD_DIM, HEAD_DIM), 0.5)
    state_rwkv_shift = nrm((DEPTH, DEC_BATCH, RW_PROJ), 1.0)
    state_gla = nrm((DEPTH, DEC_BATCH, H, GLA_DK, GLA_DV), 0.5)
    gain = lambda shape: 1.0 + nrm(shape, 0.05)
    return {
        'x_prompt': x_prompt, 'x_sample': x_sample,
        'cache_sb_k': cache_sb_k, 'cache_sb_v': cache_sb_v, 'page_table': page_table,
        'state_hgrn': state_hgrn, 'state_rwkv': state_rwkv, 'state_rwkv_shift': state_rwkv_shift, 'state_gla': state_gla,
        'norm_mix_pre': gain((DEPTH, D_MODEL)), 'norm_mix_post': gain((DEPTH, D_MODEL)),
        'norm_ffn_pre': gain((DEPTH, D_MODEL)), 'norm_ffn_post': gain((DEPTH, D_MODEL)),
        'w_in': nrm((DEPTH, D_MODEL, IN_COLS), D_MODEL ** -0.5),
        'w_out': nrm((DEPTH, D_MODEL, D_MODEL), D_MODEL ** -0.5),
        'w_up': nrm((DEPTH, D_MODEL, D_FF), D_MODEL ** -0.5),
        'w_down': nrm((DEPTH, D_FF, D_MODEL), D_FF ** -0.5),
        'hg_lb': nrm((DEPTH, GROUP_WIDTH), 1.0),
        'hg_norm': gain((DEPTH, HG_DV)),
        'rw_mu': jax.random.uniform(next(ks), (DEPTH, RW_PROJ), jnp.float32),
        'rw_w0': jax.random.uniform(next(ks), (DEPTH, GROUP_WIDTH), jnp.float32, -6.0, 0.0),
        'rw_w2': nrm((DEPTH, RW_DECAY_RANK, GROUP_WIDTH), 0.1),
        'rw_a0': nrm((DEPTH, GROUP_WIDTH), 0.1),
        'rw_a2': nrm((DEPTH, RW_A_RANK, GROUP_WIDTH), 0.5 * RW_A_RANK ** -0.5),
        'rw_g2': nrm((DEPTH, RW_GATE_RANK, GROUP_WIDTH), RW_GATE_RANK ** -0.5),
        'rw_k_k': gain((DEPTH, GROUP_WIDTH)),
        'rw_k_a': gain((DEPTH, GROUP_WIDTH)),
        'rw_r_k': nrm((DEPTH, GROUP_HEADS, HEAD_DIM), 0.1),
        'rw_ln_w': gain((DEPTH, GROUP_WIDTH)),
        'rw_ln_b': nrm((DEPTH, GROUP_WIDTH), 0.01),
        'sb_bias': SB_BIAS_INIT + nrm((DEPTH, GROUP_HEADS), 0.1),
        'gla_a2': nrm((DEPTH, GLA_GATE_RANK, GROUP_HEADS * GLA_DK), GLA_GATE_RANK ** -0.5),
        'gla_a_b': nrm((DEPTH, GROUP_HEADS * GLA_DK), 0.1),
        'gla_norm': gain((DEPTH, GLA_DV)),
    }

def reference(x_prompt, x_sample, cache_sb_k, cache_sb_v, page_table, state_hgrn, state_rwkv, state_rwkv_shift,
              state_gla, norm_mix_pre, norm_mix_post, norm_ffn_pre, norm_ffn_post, w_in, w_out, w_up, w_down,
              hg_lb, hg_norm, rw_mu, rw_w0, rw_w2, rw_a0, rw_a2, rw_g2, rw_k_k, rw_k_a, rw_r_k, rw_ln_w, rw_ln_b,
              sb_bias, gla_a2, gla_a_b, gla_norm):
    lb_all = jnp.cumsum(jax.nn.softmax(hg_lb.astype(F32), axis=0), axis=0)
    lb_all = lb_all - lb_all[0:1]
    n_seq_p = x_prompt.shape[0]
    n_seq_s, n_pages = page_table.shape
    xp, xs = x_prompt, x_sample
    sbk_p, sbv_p, sbk_s, sbv_s = [], [], [], []
    hg_p, hg_s, rw_p, rw_s, sh_p, sh_s, gl_p, gl_s = [], [], [], [], [], [], [], []
    for l in range(DEPTH):
        P = {'norm_mix_pre': norm_mix_pre[l], 'norm_mix_post': norm_mix_post[l], 'norm_ffn_pre': norm_ffn_pre[l],
             'norm_ffn_post': norm_ffn_post[l], 'w_in': w_in[l], 'w_out': w_out[l], 'w_up': w_up[l],
             'w_down': w_down[l], 'hg_norm': hg_norm[l], 'rw_mu': rw_mu[l], 'rw_w0': rw_w0[l], 'rw_w2': rw_w2[l],
             'rw_a0': rw_a0[l], 'rw_a2': rw_a2[l], 'rw_g2': rw_g2[l], 'rw_k_k': rw_k_k[l], 'rw_k_a': rw_k_a[l],
             'rw_r_k': rw_r_k[l], 'rw_ln_w': rw_ln_w[l], 'rw_ln_b': rw_ln_b[l], 'sb_bias': sb_bias[l],
             'gla_a2': gla_a2[l], 'gla_a_b': gla_a_b[l], 'gla_norm': gla_norm[l]}
        lb = lb_all[l]
        xp, k_p, v_p, hS_p, rS_p, shf_p, gS_p = _layer(
            xp, 0, lb,
            jnp.zeros((n_seq_p, GROUP_HEADS, HG_DK, HG_DV), F32),
            jnp.zeros((n_seq_p, GROUP_HEADS, HEAD_DIM, HEAD_DIM), F32),
            jnp.zeros((n_seq_p, RW_PROJ), xp.dtype),
            jnp.zeros((n_seq_p, GROUP_HEADS, GLA_DK, GLA_DV), F32),
            None, None, P)
        past_k = cache_sb_k[l][page_table].reshape(n_seq_s, n_pages * PAGE_SIZE, GROUP_HEADS, HEAD_DIM)
        past_v = cache_sb_v[l][page_table].reshape(n_seq_s, n_pages * PAGE_SIZE, GROUP_HEADS, HEAD_DIM)
        xs, k_s, v_s, hS_s, rS_s, shf_s, gS_s = _layer(
            xs, n_pages * PAGE_SIZE, lb, state_hgrn[l], state_rwkv[l], state_rwkv_shift[l], state_gla[l],
            past_k, past_v, P)
        sbk_p.append(k_p); sbv_p.append(v_p); sbk_s.append(k_s); sbv_s.append(v_s)
        hg_p.append(hS_p); hg_s.append(hS_s); rw_p.append(rS_p); rw_s.append(rS_s)
        sh_p.append(shf_p); sh_s.append(shf_s); gl_p.append(gS_p); gl_s.append(gS_s)
    y_prompt, y_sample = xp, xs
    sb_k_prompt = jnp.stack(sbk_p, 0)
    sb_v_prompt = jnp.stack(sbv_p, 0)
    sb_k_sample = jnp.stack(sbk_s, 0)
    sb_v_sample = jnp.stack(sbv_s, 0)
    hgrn_prompt = jnp.stack(hg_p, 0)
    hgrn_sample = jnp.stack(hg_s, 0)
    rwkv_prompt = jnp.stack(rw_p, 0)
    rwkv_sample = jnp.stack(rw_s, 0)
    rwkv_shift_prompt = jnp.stack(sh_p, 0)
    rwkv_shift_sample = jnp.stack(sh_s, 0)
    gla_prompt = jnp.stack(gl_p, 0)
    gla_sample = jnp.stack(gl_s, 0)
    return (y_prompt, y_sample, sb_k_prompt, sb_v_prompt, sb_k_sample, sb_v_sample, hgrn_prompt, hgrn_sample,
            rwkv_prompt, rwkv_sample, rwkv_shift_prompt, rwkv_shift_sample, gla_prompt, gla_sample)


_drawn_inputs = setup_inputs


def setup_inputs(seed=0):
    import zlib

    import numpy as np

    out = dict(_drawn_inputs(seed))
    spreads = {}
    factors = {'rw_ln_b': 8.0, 'sb_bias': 8.0}
    for name, (base, spread) in spreads.items():
        noise = np.random.default_rng([zlib.crc32(name.encode()), seed]).standard_normal(out[name].shape)
        drawn = base * np.exp(spread * noise) if base else spread * noise
        out[name] = __import__('jax').numpy.asarray(drawn.astype(out[name].dtype))
    for name, factor in factors.items():
        out[name] = (out[name] * factor).astype(out[name].dtype)
    return out
```

```python
import math
from contextlib import ExitStack

import concourse.bass as bass
from concourse import mybir

F32 = mybir.dt.float32
U32 = mybir.dt.uint32
I32 = mybir.dt.int32
ALU = mybir.AluOpType
ACT = mybir.ActivationFunctionType
AX = mybir.AxisListType.X

P = 128
D = 1024
T = 1024
NB, NS = 8, 8
SMP = NB * NS
TOK = T + SMP
KD = D // P
NT = T // P + 1
FF = 4 * D
H, HD = 4, 64
GW = H * HD
EPS = 1e-6
RW_GN_EPS = 64e-5
TG = ((0, 512), (512, 512), (T, SMP))
RWT = 7
PADW = 1 + T + NB * (1 + NS)
LEVELS = (64, 32, 16, 8, 4, 2, 1)

COL = {}
_c = 0
for _n, _w in (("hq", 256), ("hf", 256), ("hi", 256), ("hg", 256), ("rr", 256), ("rk", 256), ("rv", 256),
               ("rx", 128), ("sq", 256), ("sk", 256), ("sv", 256), ("gq", 128), ("gk", 128), ("gv", 256),
               ("ga", 16), ("gg", 256)):
    COL[_n] = _c
    _c += _w
IN_COLS = _c

GROUPS = (("rr", COL["rr"], 256, True, False), ("rk", COL["rk"], 256, True, False),
          ("rv", COL["rv"], 256, True, False), ("rx", COL["rx"], 128, True, False),
          ("sq", COL["sq"], 256, True, False), ("sk", COL["sk"], 256, True, True),
          ("sv", COL["sv"], 256, False, True), ("hq", COL["hq"], 256, True, False),
          ("hf", COL["hf"], 256, True, False), ("hi", COL["hi"], 256, False, True),
          ("hg", COL["hg"], 256, False, True), ("gqk", COL["gq"], 256, True, False),
          ("ga", COL["ga"], 16, True, False), ("gv", COL["gv"], 256, False, True),
          ("gg", COL["gg"], 256, False, True))
WSLOTS = 4


def rows(i):
    return P if i < NT - 1 else SMP


def projection_jobs():
    jobs = []
    for g, (name, c0, w, as_t, as_n) in enumerate(GROUPS):
        if as_t:
            for ct in range(max(1, w // P)):
                for tg in range(3):
                    jobs.append((g, "T", ct, tg))
        if as_n:
            for i in range(NT):
                jobs.append((g, "N", i, None))
    return jobs


def build(nc, A, O):
    JOBS = projection_jobs()
    PBANKS = 6

    ctx = ExitStack()
    with ctx:
        sems = {}

        def S(name):
            if name not in sems:
                sems[name] = ctx.enter_context(nc.semaphore(name))
            return sems[name]

        NWORDS = 53200
        arena = ctx.enter_context(nc.sbuf_tensor("arena", [P, NWORDS], F32))
        ps = ctx.enter_context(nc.psum_tensor("ps", [P, 8, 512], F32))
        used = [0]

        def at(off, *dims):
            n = 1
            for d in dims:
                n *= d
            v = arena[:, off:off + n]
            assert off + n <= NWORDS, (off, n)
            if len(dims) == 1:
                return v
            names = "abcd"[:len(dims)]
            return v.rearrange("p (" + " ".join(names) + ") -> p " + " ".join(names),
                               **{names[i]: dims[i] for i in range(1, len(dims))})

        def take(*dims):
            n = 1
            for d in dims:
                n *= d
            v = at(used[0], *dims)
            used[0] += n
            return v

        ident = take(P)
        headones = take(P)
        up_mask = take(7, P)
        low_eq = take(7, P)
        upper = take(P)
        upper_eq = take(P)
        upper8 = take(P)
        upper8_eq = take(P)
        neg_tri = take(P)
        neg_ones = take(P)
        neg_big = take(P)
        neg_big8 = take(SMP)
        seqmask = take(NB)
        gain_pre = take(KD)
        gain_ffn = take(KD)
        eps_col = take(1)
        one_col = take(1)
        page_ids = take(64).bitcast(I32)
        ssq = take(NT)
        rs = take(NT)
        par = take(40)
        sb_bias = take(H)
        w2all = take(GW)
        gla_a2 = take(P)
        CONST_END = used[0]

        hT = at(used[0], KD, TOK)
        mixT = hT
        used[0] += KD * TOK
        PR = used[0]
        sqT = take(2, TOK)
        skT = take(2, TOK)
        hqT = take(2, TOK)
        hfT = take(2, TOK)
        rwP = take(RWT, PADW)
        gqT = take(TOK)
        gkT = take(TOK)
        gaT = take(TOK)
        NR = used[0]
        hi_n = take(NT, GW)
        hg_n = take(NT, GW)
        sv_n = take(NT, GW)
        gv_n = take(NT, GW)
        gg_n = take(NT, GW)
        WR = used[0]
        wring = at(WR, WSLOTS, KD, 256)
        sk_stage = gg_n
        xin = at(PR, 3, D)
        xh = at(PR + 3 * D, 2, D)
        sq_junk = at(PR + 5 * D, D)
        shift_in = at(PR + 6 * D, RWT * P)
        nat_dst = {"hi": hi_n, "hg": hg_n, "sv": sv_n, "gv": gv_n, "gg": gg_n, "sk": sk_stage}

        PAR = {}
        PAR_SRC = (("mu", "rw_mu", 7), ("w0", "rw_w0", 2), ("a0", "rw_a0", 2), ("k_k", "rw_k_k", 2),
                   ("k_a", "rw_k_a", 2), ("r_k", "rw_r_k", 2), ("ln_w", "rw_ln_w", 2), ("ln_b", "rw_ln_b", 2),
                   ("gla_ab", "gla_a_b", 1))
        o = 0
        for n, src, w in PAR_SRC:
            PAR[n] = par[:, o:o + w]
            o += w
        PAR["hg_norm"] = par[:, o:o + 1]
        PAR["gla_norm"] = par[:, o + 1:o + 2]
        PAR["one_k_a"] = par[:, o + 2:o + 4]

        own = {}

        def did(engine):
            own[engine] = own.get(engine, 0) + 1
            return S(engine + "_own"), 1

        def so_far(engine):
            return S(engine + "_own"), own[engine]

        def chain(eng, engine):
            def step(ins):
                ins.then_inc(*did(engine))
                eng.wait_ge(*so_far(engine))
            return step

        def x_rows(i):
            return (A["x_prompt"][0, i * P:(i + 1) * P, :] if i < NT - 1
                    else A["x_sample"].rearrange("b t d -> (b t) d"))

        block = ctx.enter_context(nc.Block())

        N_PAR_DMA = 2 + len(PAR_SRC) + 4 + 1 + 3 + 1 + 1

        def load_parameters(act):
            def put(dst, src):
                act.dma_start(dst, src, allow_slow_non_contiguous=True).then_inc(S("params"), 16)
            put(gain_pre, A["norm_mix_pre"].rearrange("o (k p) -> p (o k)", p=P))
            put(gain_ffn, A["norm_ffn_pre"].rearrange("o (k p) -> p (o k)", p=P))
            for n, src, w in PAR_SRC:
                s = A[src].rearrange("o h d -> o (h d)") if src == "rw_r_k" else A[src]
                put(PAR[n], s.rearrange("o (k p) -> p (o k)", p=P))
            for j in range(2):
                put(PAR["hg_norm"][64 * j:64 * j + 64, :], A["hg_norm"].rearrange("o p -> p o"))
                put(PAR["gla_norm"][64 * j:64 * j + 64, :], A["gla_norm"].rearrange("o p -> p o"))
            put(sb_bias, A["sb_bias"][0].partition_broadcast(P))
            put(w2all[0:32, :], A["rw_w2"][0])
            put(w2all[32:64, :], A["rw_a2"][0])
            put(w2all[64:128, :], A["rw_g2"][0])
            put(gla_a2[0:16, :], A["gla_a2"][0])
            put(shift_in[0:NB, :], A["state_rwkv_shift"][0])

        def make_constants(pool):
            step = chain(pool, "pool")
            step(pool.memset(ident, 0.0))
            step(pool.affine_select(out=ident, in_=ident, compare_op=ALU.not_equal, fill=1.0, base=0,
                                    pattern=[[-1, P]], channel_multiplier=1))
            step(pool.memset(one_col, 1.0))
            pool.memset(eps_col, EPS).then_inc(S("ident"), 1)
            step(pool.memset(headones, 0.0))
            step(pool.memset(headones[0:64, 0:64], 1.0))
            step(pool.memset(headones[64:128, 64:128], 1.0))
            step(pool.memset(up_mask, 0.0))
            for lv, m in enumerate(LEVELS):
                v = up_mask[:, lv, :].rearrange("p (j h i) -> p j h i", h=2, i=m)[:, :, 1, :]
                step(pool.memset(v, 1.0))
                nb = P // (2 * m)
                step(pool.affine_select(out=v, in_=v, compare_op=ALU.is_ge, fill=0.0, base=0,
                                        pattern=[[-2 * m, nb], [0, m]], channel_multiplier=1))
                step(pool.affine_select(out=v, in_=v, compare_op=ALU.is_ge, fill=0.0, base=m - 1,
                                        pattern=[[2 * m, nb], [0, m]], channel_multiplier=-1))
            step(pool.memset(low_eq, 0.0))
            for lv, m in enumerate(LEVELS):
                v = low_eq[:, lv, :].rearrange("p (j h i) -> p j h i", h=2, i=m)[:, :, 0, :]
                step(pool.memset(v, 1.0))
                nb = P // (2 * m)
                step(pool.affine_select(out=v, in_=v, compare_op=ALU.is_ge, fill=0.0, base=-m,
                                        pattern=[[-2 * m, nb], [0, m]], channel_multiplier=1))
                step(pool.affine_select(out=v, in_=v, compare_op=ALU.is_ge, fill=0.0, base=2 * m - 1,
                                        pattern=[[2 * m, nb], [0, m]], channel_multiplier=-1))
                step(pool.tensor_tensor(low_eq[:, lv, :], low_eq[:, lv, :], ident, ALU.add))
            step(pool.memset(upper, 1.0))
            step(pool.affine_select(out=upper, in_=upper, compare_op=ALU.is_ge, fill=0.0, base=-1,
                                    pattern=[[1, P]], channel_multiplier=-1))
            step(pool.memset(upper_eq, 1.0))
            step(pool.affine_select(out=upper_eq, in_=upper_eq, compare_op=ALU.is_ge, fill=0.0, base=0,
                                    pattern=[[1, P]], channel_multiplier=-1))
            step(pool.memset(neg_tri, -1.0))
            step(pool.affine_select(out=neg_tri, in_=neg_tri, compare_op=ALU.is_ge, fill=0.0, base=0,
                                    pattern=[[-1, P]], channel_multiplier=1))
            step(pool.memset(neg_ones, -1.0))
            step(pool.memset(neg_big, 0.0))
            step(pool.affine_select(out=neg_big, in_=neg_big, compare_op=ALU.is_ge, fill=-3.0e4, base=-1,
                                    pattern=[[1, P]], channel_multiplier=-1))
            step(pool.memset(seqmask, 1.0))
            step(pool.affine_select(out=seqmask, in_=seqmask, compare_op=ALU.is_ge, fill=0.0, base=0,
                                    pattern=[[-NS, NB]], channel_multiplier=1))
            step(pool.affine_select(out=seqmask, in_=seqmask, compare_op=ALU.is_ge, fill=0.0, base=NS - 1,
                                    pattern=[[NS, NB]], channel_multiplier=-1))
            step(pool.tensor_tensor(upper8, up_mask[:, 4, :], up_mask[:, 5, :], ALU.add))
            step(pool.tensor_tensor(upper8, upper8, up_mask[:, 6, :], ALU.add))
            step(pool.tensor_tensor(upper8_eq, upper8, ident, ALU.add))
            pool.tensor_scalar(neg_big8, upper8[:, 0:SMP], 3.0e4, -3.0e4, ALU.mult, ALU.add)\
                .then_inc(S("consts"), 1)

        def norm_in_sync(sp):
            for i in range(NT):
                if i >= 3:
                    sp.wait_ge(S("xh"), i - 2)
                sp.dma_start(xin[0:rows(i), i % 3, :], x_rows(i)).then_inc(S(f"x_in{i % 3}"), 16)

        def norm_in_act(act):
            act.preload_act_table_set("natural_log_exp_and_others")
            act.wait_ge(S("ident"), 1)
            for i in range(NT):
                r = rows(i)
                act.wait_ge(S(f"x_in{i % 3}"), 16 * (i // 3 + 1))
                act.activation(sq_junk[0:r, :], xin[0:r, i % 3, :], ACT.Square,
                               accum_out=ssq[0:r, i:i + 1]).then_inc(*did("act"))
                act.wait_ge(*so_far("act"))
                act.activation(ssq[0:r, i:i + 1], ssq[0:r, i:i + 1], ACT.Ln, scale=1.0 / D,
                               bias=eps_col[0:r, :]).then_inc(*did("act"))
                act.wait_ge(*so_far("act"))
                act.activation(rs[0:r, i:i + 1], ssq[0:r, i:i + 1], ACT.Exp, scale=-0.5).then_inc(S("rs"), 1)

        def norm_in_vector(dve):
            def evac(i):
                r = rows(i)
                for half in range(2):
                    n = 2 * i + half
                    dve.wait_ge(S("xT"), n + 1)
                    src = ps[:, n % 4, :].rearrange("p (k t) -> p k t", k=4)[:, :, 0:r]
                    g = gain_pre[:, 4 * half:4 * half + 4].unsqueeze(2).broadcast_to([P, 4, r])
                    dve.tensor_tensor(hT[:, 4 * half:4 * half + 4, i * P:i * P + r], src, g,
                                      ALU.mult).then_inc(S("hT"), 1)
            for i in range(NT):
                r = rows(i)
                dve.wait_ge(S("rs"), i + 1)
                if i >= 2:
                    dve.wait_ge(S("xT"), 2 * (i - 1))
                dve.tensor_scalar(xh[0:r, i % 2, :], xin[0:r, i % 3, :], rs[0:r, i:i + 1], None,
                                  ALU.mult).then_inc(S("xh"), 1)
                if i == 0:
                    dve.wait_ge(S("params"), 16 * N_PAR_DMA)
                if i >= 1:
                    evac(i - 1)
            evac(NT - 1)

        def norm_in_tensor(pe):
            pe.wait_ge(S("ident"), 1)
            for i in range(NT):
                r = rows(i)
                pe.wait_ge(S("xh"), i + 1)
                for half in range(2):
                    n = 2 * i + half
                    if n >= 4:
                        pe.wait_ge(S("hT"), n - 3)
                    for k in range(4):
                        c = (4 * half + k) * P
                        ins = pe.transpose(ps[:, n % 4, k * P:k * P + r], xh[0:r, i % 2, c:c + P],
                                           ident[0:r, 0:r])
                    ins.then_inc(S("xT"), 1)
            pe.wait_ge(S("params"), 16 * N_PAR_DMA)
            for ct in range(RWT):
                ins = pe.transpose(ps[:, 6, ct * NB:(ct + 1) * NB], shift_in[0:NB, ct * P:(ct + 1) * P],
                                   ident[0:NB, 0:NB])
            ins.then_inc(S("shiftT"), 1)

        def project_sync(sp):
            last = -1
            for g, (name, c0, w, as_t, as_n) in enumerate(GROUPS):
                if g >= WSLOTS:
                    last = max(n for n, j in enumerate(JOBS) if j[0] == g - WSLOTS)
                    sp.wait_ge(S("proj_ps"), last + 1)
                sp.dma_start(wring[:, g % WSLOTS, :, 0:w],
                             A["w_in"][0].rearrange("(k p) c -> p k c", p=P)[:, :, c0:c0 + w])\
                    .then_inc(S(f"w_in{g % WSLOTS}"), 16)

        def project_tensor(pe):
            pe.wait_ge(S("hT"), 2 * NT)
            seen = -1
            for n, (g, kind, a, tg) in enumerate(JOBS):
                w = GROUPS[g][2]
                if g != seen:
                    pe.wait_ge(S(f"w_in{g % WSLOTS}"), 16 * (g // WSLOTS + 1))
                    seen = g
                if n >= PBANKS:
                    pe.wait_ge(S("proj_out"), n - PBANKS + 1)
                bank = ps[:, n % PBANKS, :]
                for k in range(KD):
                    if kind == "T":
                        t0, tw = TG[tg]
                        cw = min(w, P)
                        ins = pe.matmul(bank[0:cw, 0:tw], wring[:, g % WSLOTS, k, a * P:a * P + cw],
                                        hT[:, k, t0:t0 + tw], start=(k == 0), stop=(k == KD - 1))
                    else:
                        r = rows(a)
                        ins = pe.matmul(bank[0:r, 0:256], hT[:, k, a * P:a * P + r],
                                        wring[:, g % WSLOTS, k, :], start=(k == 0), stop=(k == KD - 1))
                ins.then_inc(S("proj_ps"), 1)

        def project_act(act):
            act.wait_ge(S("hT"), 2 * NT)
            act.wait_ge(S("shiftT"), 1)
            for n, (g, kind, a, tg) in enumerate(JOBS):
                name, w = GROUPS[g][0], GROUPS[g][2]
                act.wait_ge(S("proj_ps"), n + 1)
                bank = ps[:, n % PBANKS, :]
                if kind == "N":
                    r = rows(a)
                    if name == "gg" and a == 0:
                        act.wait_ge(S("sk_out"), 32)
                    fn = ACT.Silu if name in ("hg", "gg") else ACT.Copy
                    act.activation(nat_dst[name][0:r, a, :], bank[0:r, 0:256], fn).then_inc(S("proj_out"), 1)
                    continue
                t0, tw = TG[tg]
                cw = min(w, P)
                src = bank[0:cw, 0:tw]
                if name in ("rr", "rk", "rv", "rx"):
                    ct = {"rr": 0, "rk": 2, "rv": 4, "rx": 6}[name] + a
                    if tg < 2:
                        dst = rwP[:, ct, 1 + t0:1 + t0 + tw]
                    else:
                        dst = rwP[:, ct, 1 + T:].rearrange("p (b t) -> p b t", b=NB)[:, :, 1:]
                        src = src.rearrange("p (b t) -> p b t", b=NB)
                elif name == "gqk":
                    dst = (gqT, gkT)[a][:, t0:t0 + tw]
                elif name == "ga":
                    dst = gaT[0:cw, t0:t0 + tw]
                else:
                    dst = {"sq": sqT, "sk": skT, "hq": hqT, "hf": hfT}[name][:, a, t0:t0 + tw]
                fn = ACT.Silu if name == "hq" else ACT.Copy
                scale = HD ** -0.5 if name == "sq" else 32 ** -0.5 if (name, a) == ("gqk", 0) else 1.0
                act.activation(dst, src, fn, scale=scale).then_inc(S("proj_out"), 1)

        def project_vector(dve):
            dve.memset(rwP[:, :, 0:1], 0.0).then_inc(*did("dve"))
            dve.wait_ge(S("shiftT"), 1)
            dve.tensor_copy(rwP[:, :, 1 + T:].rearrange("p c (b t) -> p c b t", b=NB)[:, :, :, 0],
                            ps[:, 6, 0:RWT * NB].rearrange("p (c b) -> p c b", c=RWT)).then_inc(*did("dve"))

        def job_of(name, kind):
            return 1 + max(n for n, j in enumerate(JOBS) if GROUPS[j[0]][0] == name and j[1] == kind)

        def caches_out_gpsimd(pool):
            for name, first in (("sk", sk_stage), ("sv", sv_n)):
                pool.wait_ge(S("proj_out"), job_of(name, "N"))
                kv = "k" if name == "sk" else "v"
                done = S("sk_out") if name == "sk" else S("sv_out")
                pool.dma_start(O[f"sb_{kv}_prompt"][0, 0].rearrange("(i p) h d -> p i (h d)", p=P),
                               first[:, 0:NT - 1, :]).then_inc(done, 16)
                pool.dma_start(O[f"sb_{kv}_sample"][0].rearrange("b t h d -> (b t) (h d)"),
                               first[0:SMP, NT - 1, :]).then_inc(done, 16)


        SB_BLOCKS = [(h, G, kt) for h in range(H) for G in range(2) for kt in range(4 * G + 3, -1, -1)]
        SBN = len(SB_BLOCKS)
        SB_DIAG = sum(b[2] >= 4 * b[1] for b in SB_BLOCKS)
        sb_zc = at(WR, 3, 512)
        sb_sp = at(WR + 1536, 3, 512)
        sb_w = at(WR + 3072, 3, 512)
        sb_sum = at(WR + 4608, 2, 512)

        def sb_geometry(n):
            h, G, kt = SB_BLOCKS[n]
            base = 64 * (h % 2)
            q0 = max(kt * P, 512 * G)
            return h, G, kt, slice(base, base + 64), q0, 512 * (G + 1) - q0, q0 - 512 * G, 2 * h + G

        def sb_tensor(pe):
            pe.wait_ge(S("proj_out"), len(JOBS))
            pe.wait_ge(S("consts"), 1)
            NBLK = len(SB_BLOCKS)

            def scores(n):
                h, G, kt, rws, q0, w, c0, hg = sb_geometry(n)
                if n >= 3:
                    pe.wait_ge(S("sb_sp"), n - 2)
                pe.matmul(ps[:, n % 3, 0:w], skT[rws, h // 2, kt * P:kt * P + P], sqT[rws, h // 2, q0:q0 + w],
                          start=True, stop=True).then_inc(S("sb_z"), 1)

            def exponents(n):
                h, G, kt, rws, q0, w, c0, hg = sb_geometry(n)
                bank = ps[:, 3 + n % 2, 0:w]
                if n >= 2:
                    pe.wait_ge(S("sb_w"), n - 1)
                pe.matmul(bank, skT[rws, h // 2, kt * P:kt * P + P], sqT[rws, h // 2, q0:q0 + w],
                          start=True, stop=False, skip_group_check=True)
                if kt >= 4 * G:
                    pe.matmul(bank[:, 0:P], ident, neg_big, start=False, stop=False, skip_group_check=True)
                    pe.wait_ge(S("sb_spm"), sum(b[2] >= 4 * b[1] for b in SB_BLOCKS[:n + 1]))
                pe.wait_ge(S("sb_sp"), n + 1)
                if kt < 4 * G + 3:
                    pe.wait_ge(S("sb_sum"), n)
                    pe.matmul(bank, neg_ones, sb_sum[:, (n - 1) % 2, c0:512], start=False, stop=False,
                              skip_group_check=True)
                pe.matmul(bank, neg_tri, sb_sp[:, n % 3, 0:w], start=False, stop=True,
                          skip_group_check=True).then_inc(S("sb_x"), 1)

            def outputs(n):
                h, G, kt, rws, q0, w, c0, hg = sb_geometry(n)
                pe.wait_ge(S("sb_w"), n + 1)
                if kt == 4 * G + 3 and hg >= 2:
                    pe.wait_ge(S("sb_o"), hg - 1)
                pe.matmul(ps[rws, 5 + hg % 2, c0:512], sv_n[:, kt, h * HD:(h + 1) * HD], sb_w[:, n % 3, 0:w],
                          start=(kt == 4 * G + 3), stop=(kt == 0), skip_group_check=True)\
                    .then_inc(S("sb_pv"), 1)

            scores(0)
            scores(1)
            for n in range(NBLK):
                if n + 2 < NBLK:
                    scores(n + 2)
                exponents(n)
                if n >= 1:
                    outputs(n - 1)
            outputs(NBLK - 1)

        def sb_vector(dve):
            diag = 0
            dve.wait_ge(S("params"), 16 * N_PAR_DMA)
            for n in range(len(SB_BLOCKS)):
                h, G, kt, rws, q0, w, c0, hg = sb_geometry(n)
                dve.wait_ge(S("sb_z"), n + 1)
                dve.tensor_scalar(sb_zc[:, n % 3, 0:w], ps[:, n % 3, 0:w], sb_bias[:, h:h + 1], 40.0,
                                  ALU.add, ALU.min).then_inc(S("sb_zc"), 1)
                if n >= 1:
                    diag = softplus(dve, n - 1, diag)
            softplus(dve, len(SB_BLOCKS) - 1, diag)

        def softplus(dve, n, diag):
            h, G, kt, rws, q0, w, c0, hg = sb_geometry(n)
            dve.wait_ge(S("sb_l"), n + 1)
            if n >= 3:
                dve.wait_ge(S("sb_x"), n - 2)
                dve.wait_ge(S("sb_sum"), n - 2)
            dve.scalar_tensor_tensor(sb_sp[:, n % 3, 0:w], ps[:, n % 3, 0:w], sb_bias[:, h:h + 1],
                                     sb_zc[:, n % 3, 0:w], ALU.add, ALU.max).then_inc(S("sb_sp"), 1)
            if kt >= 4 * G:
                diag += 1
                dve.wait_ge(S("sb_sp"), n + 1)
                dve.tensor_tensor(sb_sp[:, n % 3, 0:P], sb_sp[:, n % 3, 0:P], upper, ALU.mult)\
                    .then_inc(S("sb_spm"), 1)
            return diag

        def sb_act(act):
            act.preload_act_table_set("natural_log_exp_and_others")

            def weights(n):
                h, G, kt, rws, q0, w, c0, hg = sb_geometry(n)
                act.wait_ge(S("sb_x"), n + 1)
                if n >= 3:
                    act.wait_ge(S("sb_pv"), n - 2)
                act.activation(sb_w[:, n % 3, 0:w], ps[:, 3 + n % 2, 0:w], ACT.Exp,
                               bias=sb_bias[:, h:h + 1]).then_inc(S("sb_w"), 1)
                if kt == 0:
                    act.wait_ge(S("sb_pv"), n + 1)
                    act.activation(mixT[rws, 4 + h // 2, 512 * G:512 * G + 512], ps[rws, 5 + hg % 2, :],
                                   ACT.Copy).then_inc(S("sb_o"), 1)
            for n in range(len(SB_BLOCKS)):
                w = sb_geometry(n)[5]
                zc = sb_zc[:, n % 3, 0:w]
                act.wait_ge(S("sb_zc"), n + 1)
                act.activation(zc, zc, ACT.Exp).then_inc(*did("act"))
                act.wait_ge(*so_far("act"))
                act.activation(zc, zc, ACT.Ln, bias=one_col).then_inc(S("sb_l"), 1)
                if n >= 1:
                    weights(n - 1)
            weights(len(SB_BLOCKS) - 1)

        def sb_gpsimd(pool):
            diag = 0
            for n in range(len(SB_BLOCKS)):
                h, G, kt, rws, q0, w, c0, hg = sb_geometry(n)
                if kt == 4 * G + 3:
                    if n >= 1:
                        pool.wait_ge(S("sb_x"), n)
                        pool.wait_ge(S("sb_sum"), n)
                    pool.wait_ge(S("proj_out"), len(JOBS))
                    pool.memset(sb_sum, 0.0).then_inc(*did("pool"))
                    pool.wait_ge(*so_far("pool"))
                pool.wait_ge(S("sb_sp"), n + 1)
                if kt >= 4 * G:
                    diag += 1
                    pool.wait_ge(S("sb_spm"), diag)
                if n >= 1:
                    pool.wait_ge(S("sb_x"), n)
                    pool.wait_ge(S("sb_sum"), n)
                pool.tensor_tensor(sb_sum[:, n % 2, c0:512], sb_sum[:, (n - 1) % 2, c0:512],
                                   sb_sp[:, n % 3, 0:w], ALU.add).then_inc(S("sb_sum"), 1)

        QC = H * SMP
        NPG = 8
        k_half = at(WR, 2, 4, GW)
        v_page = at(WR + 2048, 2, NB, GW)
        kT_page = at(WR + 6144, NB, 2, P)
        dsb = [mixT[:, 2 + i // 4, 256 * (i % 4):256 * (i % 4) + 256] for i in range(8)]
        q_diag = dsb[0].rearrange("p (a c t) -> p a c t", a=2, c=2)
        d_z, d_l, d_w = dsb[1], dsb[2], dsb[3]
        d_sp, d_sum = (dsb[4], dsb[5]), (dsb[6], dsb[7])

        def decode_rows(j):
            return SMP if j == 0 else P

        def decode_load_sync(sp):
            sp.dma_start(page_ids[0:1, :], A["page_table"].rearrange("(o b) n -> o (b n)", o=1))\
                .then_inc(S("page_ids"), 16)
            sp.wait_ge(S("page_ids"), 16)
            sp.wait_ge(S("sb_pv"), len(SB_BLOCKS))
            sp.wait_ge(S("sb_sum"), len(SB_BLOCKS))
            def page_id(b, j):
                n = b * NPG + NPG - j
                return sp.value_load(page_ids[0:1, n:n + 1], min_val=0, max_val=A["cache_sb_k"].shape[1] - 1)

            for j in range(1, NPG + 1):
                for b in range(NB):
                    half = 2 * (j - 1) + b // 4
                    if b % 4 == 0 and half >= 2:
                        sp.wait_ge(S("d_kt"), 2 * (half - 1))
                    sp.dma_start(k_half[:, half % 2, b % 4, :],
                                 A["cache_sb_k"][0][bass.ds(page_id(b, j), 1)].rearrange("n t h d -> t (n h d)"))\
                        .then_inc(S(f"d_k{half % 2}"), 16)
                if j >= 3:
                    sp.wait_ge(S("sb_pv"), SBN + j - 1)
                for b in range(NB):
                    sp.dma_start(v_page[:, j % 2, b, :],
                                 A["cache_sb_v"][0][bass.ds(page_id(b, j), 1)].rearrange("n t h d -> t (n h d)"))\
                        .then_inc(S(f"d_v{j % 2}"), 16)

        def decode_tensor(pe):
            def transposes(j):
                for g in range(4):
                    half = 2 * (j - 1) + g // 2
                    n = 4 * (j - 1) + g
                    if g % 2 == 0:
                        pe.wait_ge(S(f"d_k{half % 2}"), 64 * (half // 2 + 1))
                    if n >= 2:
                        pe.wait_ge(S("d_kT"), n - 1)
                    for i in range(4):
                        b, pr = 2 * g + i // 2, i % 2
                        ins = pe.transpose(ps[:, n % 2, i * P:(i + 1) * P],
                                           k_half[:, half % 2, b % 4, pr * P:(pr + 1) * P], ident)
                    ins.then_inc(S("d_kt"), 1)

            def scores(j):
                bank = ps[:, 2, 0:QC]
                if j >= 1:
                    pe.wait_ge(S("d_z"), j)
                if j == 0:
                    pe.wait_ge(S("d_q"), 4)
                    for pr in range(2):
                        ins = pe.matmul(bank[0:SMP, pr * P:(pr + 1) * P], skT[:, pr, T:TOK],
                                        q_diag[:, pr, :, :], start=(pr == 0), stop=True, skip_group_check=True)
                else:
                    pe.wait_ge(S("d_kT"), 4 * j)
                    out = bank.rearrange("p (a c t) -> p a c t", a=2, c=2)
                    for b in range(NB):
                        for pr in range(2):
                            cols = slice(b * NS, (b + 1) * NS)
                            ins = pe.matmul(out[:, pr, :, cols], kT_page[:, b, pr, :], q_diag[:, pr, :, cols],
                                            start=(b == 0 and pr == 0), stop=True, skip_group_check=True)
                ins.then_inc(S("sb_z"), 1)

            def exponents(j):
                r = decode_rows(j)
                bank = ps[0:r, 3, 0:QC]
                pe.wait_ge(S("d_z"), j + 1)
                if j >= 1:
                    pe.wait_ge(S("sb_w"), SBN + j)
                pe.matmul(bank, ident[0:r, 0:r], d_z[0:r, :], start=True, stop=False, skip_group_check=True)
                if j == 0:
                    for h in range(H):
                        pe.matmul(bank[:, h * SMP:(h + 1) * SMP], ident[0:r, 0:r], neg_big8[0:r, :],
                                  start=False, stop=False, skip_group_check=True)
                    pe.wait_ge(S("sb_spm"), SB_DIAG + 1)
                else:
                    pe.wait_ge(S("d_sum"), j)
                    pe.matmul(bank, neg_ones, d_sum[(j - 1) % 2], start=False, stop=False, skip_group_check=True)
                pe.wait_ge(S("sb_sp"), SBN + j + 1)
                pe.matmul(bank, neg_tri[0:r, 0:r], d_sp[j % 2][0:r, :], start=False, stop=True,
                          skip_group_check=True).then_inc(S("sb_x"), 1)

            def outputs(j):
                pe.wait_ge(S("sb_w"), SBN + j + 1)
                out = ps[:, 4, 0:QC].rearrange("p (a c t) -> p a c t", a=2, c=2)
                w = d_w.rearrange("p (a c t) -> p a c t", a=2, c=2)
                if j == 0:
                    for pr in range(2):
                        ins = pe.matmul(out[:, pr, :, :], sv_n[0:SMP, NT - 1, pr * P:(pr + 1) * P],
                                        w[0:SMP, pr, :, :], start=(pr == 0), stop=False, skip_group_check=True)
                else:
                    pe.wait_ge(S(f"d_v{j % 2}"), 128 * ((j + 1) // 2))
                    for b in range(NB):
                        for pr in range(2):
                            cols = slice(b * NS, (b + 1) * NS)
                            ins = pe.matmul(out[:, pr, :, cols], v_page[:, j % 2, b, pr * P:(pr + 1) * P],
                                            w[:, pr, :, cols], start=False, stop=(j == NPG), skip_group_check=True)
                ins.then_inc(S("sb_pv"), 1)

            scores(0)
            transposes(1)
            for j in range(NPG + 1):
                exponents(j)
                if j < NPG:
                    scores(j + 1)
                    if j + 1 < NPG:
                        transposes(j + 2)
                outputs(j)

        def decode_vector(dve):
            dve.wait_ge(S("sb_pv"), len(SB_BLOCKS))
            dve.memset(dsb[0], 0.0).then_inc(S("d_q"), 1)
            dve.memset(d_sum[1], 0.0).then_inc(S("d_q"), 1)
            dve.wait_ge(S("d_q"), 2)
            for c in range(2):
                rws = slice(64 * c, 64 * c + 64)
                dve.tensor_copy(q_diag[rws, :, c, :], sqT[rws, :, T:TOK]).then_inc(S("d_q"), 1)
            for j in range(NPG + 1):
                r = decode_rows(j)
                heads = lambda t: t[0:r, :].rearrange("p (h t) -> p h t", h=H)
                dve.wait_ge(S("sb_z"), SBN + j + 1)
                if j >= 1:
                    dve.wait_ge(S("sb_x"), SBN + j)
                dve.tensor_tensor(heads(d_z), heads(ps[:, 2, 0:QC]),
                                  sb_bias[0:r, :].unsqueeze(2).broadcast_to([r, H, SMP]), ALU.add)\
                    .then_inc(S("d_z"), 1)
                dve.wait_ge(S("d_z"), j + 1)
                dve.tensor_scalar(d_l[0:r, :], d_z[0:r, :], 40.0, None, ALU.min).then_inc(S("sb_zc"), 1)
                dve.wait_ge(S("sb_l"), SBN + j + 1)
                if j >= 2:
                    dve.wait_ge(S("d_sum"), j - 1)
                dve.tensor_tensor(d_sp[j % 2][0:r, :], d_z[0:r, :], d_l[0:r, :], ALU.max).then_inc(S("sb_sp"), 1)
                dve.wait_ge(S("sb_sp"), SBN + j + 1)
                if j == 0:
                    dve.tensor_tensor(heads(d_sp[0]), heads(d_sp[0]),
                                      upper8[0:r, 0:SMP].unsqueeze(1).broadcast_to([r, H, SMP]), ALU.mult)\
                        .then_inc(S("sb_spm"), 1)
                    dve.wait_ge(S("sb_spm"), SB_DIAG + 1)
                    dve.tensor_copy(d_sum[0], d_sum[1]).then_inc(*did("dve"))
                    dve.wait_ge(*so_far("dve"))
                    dve.tensor_copy(d_sum[0][0:r, :], d_sp[0][0:r, :]).then_inc(S("d_sum"), 1)
                else:
                    dve.wait_ge(S("d_sum"), j)
                    dve.tensor_tensor(d_sum[j % 2], d_sum[(j - 1) % 2], d_sp[j % 2], ALU.add)\
                        .then_inc(S("d_sum"), 1)

        def decode_act(act):
            def weights(j):
                r = decode_rows(j)
                act.wait_ge(S("sb_x"), SBN + j + 1)
                if j >= 1:
                    act.wait_ge(S("sb_pv"), SBN + j)
                act.activation(d_w[0:r, :], ps[0:r, 3, 0:QC], ACT.Exp).then_inc(S("sb_w"), 1)

            def evacuate(j):
                for g in range(4):
                    n = 4 * (j - 1) + g
                    act.wait_ge(S("d_kt"), n + 1)
                    if g == 0 and j >= 2:
                        act.wait_ge(S("sb_z"), SBN + j)
                    act.activation(kT_page[:, 2 * g:2 * g + 2, :, :],
                                   ps[:, n % 2, :].rearrange("p (b a t) -> p b a t", b=2, a=2), ACT.Copy)\
                        .then_inc(S("d_kT"), 1)
            evacuate(1)
            for j in range(NPG + 1):
                r = decode_rows(j)
                act.wait_ge(S("sb_zc"), SBN + j + 1)
                act.activation(d_l[0:r, :], d_l[0:r, :], ACT.Exp).then_inc(*did("act"))
                act.wait_ge(*so_far("act"))
                act.activation(d_l[0:r, :], d_l[0:r, :], ACT.Ln, bias=one_col[0:r, :]).then_inc(S("sb_l"), 1)
                if j >= 1 and j < NPG:
                    evacuate(j + 1)
                weights(j)
            act.wait_ge(S("sb_pv"), SBN + NPG + 1)
            for c in range(2):
                rws = slice(64 * c, 64 * c + 64)
                act.activation(mixT[rws, 4:6, T:TOK],
                               ps[rws, 4, 0:QC].rearrange("p (a c t) -> p a c t", a=2, c=2)[:, :, c, :],
                               ACT.Copy).then_inc(S("d_o"), 1)


        class Mixer:

            def __init__(self, dk, q, k, b, v, gate, gscale, kt0, norm, state, s0, out_p, out_s):
                self.dk, self.q, self.k, self.b, self.v, self.gate = dk, q, k, b, v, gate
                self.gscale, self.kt0, self.norm, self.state, self.s0 = gscale, kt0, norm, state, s0
                self.out_p, self.out_s = out_p, out_s
                self.nd = H * dk // P

            def head(self, h):
                per = P // self.dk
                return h // per, slice(self.dk * (h % per), self.dk * (h % per) + self.dk)

        la_b = at(PR, 3, TOK)
        la_reset = at(PR + 3 * TOK, TOK)
        la_g = at(WR, 3, TOK)
        la_tmp = at(WR + 3 * TOK, 3, TOK)
        la_x = at(WR, 2, 9, 2 * P)
        la_att = at(WR + 4608, 2, H, P)
        la_kn = at(WR + 5632, 2, GW)
        la_o_sq = at(WR + 6144, GW)
        la_o_n = at(WR + 6400, 2, GW)
        hg_state = at(WR + 6912, GW)
        gla_state = at(WR + 7168, GW)
        la_ss = at(WR + 7424, 2, H)
        la_gl = at(WR + 7432, 2 * NB)
        la_big = at(WR + 7448, NB, HD)
        la_inter = at(WR + 7960, GW)
        la_dlast = at(WR + 8216, 2, 2)
        hg_s0 = at(NR + 2 * NT * GW, 2, NB, HD)
        gla_s0 = at(NR + 2 * NT * GW + 1024, 1, NB, HD)

        HG = Mixer(HD, hqT, hfT, la_b[:, 0:2, :], hi_n, hg_n, 1.0, 0, PAR["hg_norm"], hg_state, hg_s0,
                   O["hgrn_prompt"], O["hgrn_sample"])
        GL = Mixer(32, gqT.unsqueeze(1), gkT.unsqueeze(1), la_b[:, 2:3, :], gv_n, gg_n, 1.0 / 16.0, 6,
                   PAR["gla_norm"], gla_state, gla_s0, O["gla_prompt"], O["gla_sample"])
        MIX = (HG, GL)
        LT = 2 * NT

        def la_tile(n):
            i = n % NT
            return MIX[n // NT], i, rows(i), i * P, i == NT - 1


        def la_prep_tensor(pe):
            pe.wait_ge(S("d_o"), 2)
            for tg, (t0, tw) in enumerate(TG):
                ins = pe.matmul(ps[:, tg, 0:tw], gla_a2[0:16, :], gaT[0:16, t0:t0 + tw], start=True, stop=True)
            ins.then_inc(S("gla_logit"), 1)

        def la_prep_act(act):
            act.wait_ge(S("gla_logit"), 1)
            for tg, (t0, tw) in enumerate(TG):
                ins = act.activation(la_g[:, 2, t0:t0 + tw], ps[:, tg, 0:tw], ACT.Identity, bias=PAR["gla_ab"])
            ins.then_inc(S("gla_x"), 1)
            for a in range(3):
                act.wait_ge(S("g_clip"), a + 1)
                act.activation(la_tmp[:, a, :], la_tmp[:, a, :], ACT.Exp, scale=-1.0).then_inc(*did("act"))
                act.wait_ge(*so_far("act"))
                act.activation(la_tmp[:, a, :], la_tmp[:, a, :], ACT.Ln, bias=one_col).then_inc(S("g_l"), 1)
            for a in range(2):
                act.wait_ge(S("g_kx"), a + 1)
                act.activation(hfT[:, a, :], hfT[:, a, :], ACT.Exp).then_inc(S("hg_k"), 1)

        def la_prep_vector(dve):
            dve.wait_ge(S("d_o"), 2)
            dve.memset(la_reset, 1.0).then_inc(*did("dve"))
            dve.wait_ge(*so_far("dve"))
            dve.memset(la_reset[:, 0:T].rearrange("p (i t) -> p i t", t=P)[:, :, 0:1], 0.0)\
                .then_inc(*did("dve"))
            dve.memset(la_reset[:, T:TOK].rearrange("p (i t) -> p i t", t=NS)[:, :, 0:1], 0.0)\
                .then_inc(*did("dve"))
            x = (hfT[:, 0, :], hfT[:, 1, :], la_g[:, 2, :])
            for a in range(3):
                if a == 2:
                    dve.wait_ge(S("gla_x"), 1)
                dve.tensor_scalar(la_tmp[:, a, :], x[a], -40.0, None, ALU.max).then_inc(S("g_clip"), 1)
            for a in range(3):
                dve.wait_ge(S("g_l"), a + 1)
                dve.scalar_tensor_tensor(la_g[:, a, :], la_tmp[:, a, :], -1.0, x[a], ALU.mult, ALU.min)\
                    .then_inc(*did("dve"))
                dve.wait_ge(*so_far("dve"))
                dve.wait_ge(*so_far("dve"))
                dve.tensor_tensor_scan(la_b[:, a, :], la_reset, la_g[:, a, :], 0.0, ALU.mult, ALU.add)\
                    .then_inc(*did("dve"))
                if a < 2:
                    dve.tensor_tensor(hfT[:, a, :], la_g[:, a, :], hfT[:, a, :], ALU.subtract)\
                        .then_inc(S("g_kx"), 1)
            dve.wait_ge(*so_far("dve"))
            dve.wait_ge(S("g_kx"), 2)
            dve.memset(la_att, 0.0).then_inc(S("la_zero"), 1)
            dve.memset(hg_state, 0.0).then_inc(S("la_zero"), 1)
            dve.memset(gla_state, 0.0).then_inc(S("la_zero"), 1)

        def la_load_sync(sp):
            sp.wait_ge(S("sv_out"), 32)
            sp.wait_ge(S("d_o"), 2)
            for a in range(2):
                for c in range(2):
                    sp.dma_start(hg_s0[64 * c:64 * c + 64, a, :, :],
                                 A["state_hgrn"][0, :, 2 * a + c, :, :].rearrange("b d e -> d b e"))\
                        .then_inc(S("la_s0"), 16)
            for h in range(H):
                sp.dma_start(gla_s0[32 * h:32 * h + 32, 0, :, :],
                             A["state_gla"][0, :, h, :, :].rearrange("b d e -> d b e")).then_inc(S("la_s0"), 16)

        def la_halves(m, t):
            return t.rearrange("p a (j h i) -> p a j h i", h=2, i=m)

        def la_levels(smp):
            return [(lv, m) for lv, m in enumerate(LEVELS) if not smp or m < NS]

        def la_diffs(eng, n, half, done):
            M, i, r, c0, smp = la_tile(n)
            b = M.b[:, :, c0:c0 + r]
            eng.wait_ge(S("la_zero"), 3)
            if n >= 2:
                eng.wait_ge(S("la_o"), n - 1)
                eng.wait_ge(S("la_kT"), n - 1)
            for lv, m in la_levels(smp):
                v, x = la_halves(m, b), la_halves(m, la_x[:, n % 2, lv, 0:M.nd * r].rearrange(
                    "p (a t) -> p a t", a=M.nd))
                for a in range(M.nd):
                    mid = v[:, a, :, 0, m - 1:m].broadcast_to([P, r // (2 * m), m])
                    if half == 1:
                        ins = eng.tensor_tensor(x[:, a, :, 1, :], v[:, a, :, 1, :], mid, ALU.subtract)
                    else:
                        ins = eng.tensor_tensor(x[:, a, :, 0, :], mid, v[:, a, :, 0, :], ALU.subtract)
            if half == 1:
                L = NS if smp else P
                for a in range(M.nd):
                    bb = b[:, a, :].rearrange("p (j t) -> p j t", t=L)
                    last = bb[:, :, L - 1:L].broadcast_to([P, r // L, L])
                    ins = eng.tensor_tensor(la_x[:, n % 2, 8, a * r:(a + 1) * r].rearrange(
                        "p (j t) -> p j t", t=L), last, bb, ALU.subtract)
            ins.then_inc(S(done), 1)

        def la_exp(act, n):
            M, i, r, c0, smp = la_tile(n)
            w = M.nd * r
            act.wait_ge(S("la_xr"), n + 1)
            act.wait_ge(S("la_xl"), n + 1)
            lv0 = la_levels(smp)[0][0]
            act.activation(la_x[:, n % 2, lv0:7, 0:w], la_x[:, n % 2, lv0:7, 0:w], ACT.Exp, scale=M.gscale)
            act.activation(la_x[:, n % 2, 8, 0:w], la_x[:, n % 2, 8, 0:w], ACT.Exp, scale=M.gscale)
            if smp:
                if n >= NT:
                    act.wait_ge(S("la_snew"), H)
                act.activation(la_gl[:, 0:M.nd * NB].rearrange("p (a b) -> p a b", a=M.nd),
                               M.b[:, :, c0 + NS - 1:c0 + r:NS], ACT.Exp, scale=M.gscale)
            act.activation(la_x[:, n % 2, 7, 0:w].rearrange("p (a t) -> p a t", a=M.nd),
                           M.b[:, :, c0:c0 + r], ACT.Exp, scale=M.gscale).then_inc(S("la_exp"), 1)

        def la_times(eng, n, half, done):
            M, i, r, c0, smp = la_tile(n)
            eng.wait_ge(S("la_exp"), n + 1)
            if n == 0:
                eng.wait_ge(S("hg_k"), 2)
            y = (M.q if half == 1 else M.k)[:, :, c0:c0 + r]
            for lv, m in la_levels(smp):
                x = la_halves(m, la_x[:, n % 2, lv, 0:M.nd * r].rearrange("p (a t) -> p a t", a=M.nd))
                for a in range(M.nd):
                    ins = eng.tensor_tensor(x[:, a, :, half, :], x[:, a, :, half, :],
                                            la_halves(m, y)[:, a, :, half, :], ALU.mult)
            x = la_x[:, n % 2, 7 if half == 1 else 8, 0:M.nd * r].rearrange("p (a t) -> p a t", a=M.nd)
            eng.tensor_tensor(x, x, y, ALU.mult).then_inc(S(done), 1)

        def la_group(smp, g):
            return ([(0, 64), (1, 32), (2, 16), (3, 8)], [(4, 4), (5, 2), (6, 1), (None, 0)])[g]

        def la_attD_count(n):
            return sum(1 if la_tile(j)[4] else 2 for j in range(n + 1))

        def la_tensor(pe):
            def key_transposes(n):
                M, i, r, c0, smp = la_tile(n)
                pe.wait_ge(S("la_tl"), n + 1)
                if n >= 1:
                    pe.wait_ge(S("la_kn"), n)
                if n == NT:
                    pe.wait_ge(S("la_snew"), H)
                for a in range(M.nd):
                    ins = pe.transpose(ps[0:r, 4, a * P:(a + 1) * P], la_x[:, n % 2, 8, a * r:(a + 1) * r], ident)
                ins.then_inc(S("la_kT"), 1)

            def outputs(n):
                M, i, r, c0, smp = la_tile(n)
                pe.wait_ge(S("la_attD"), la_attD_count(n))
                if not smp:
                    pe.wait_ge(S("la_attA"), sum(not la_tile(j)[4] for j in range(n + 1)))
                if n >= 1:
                    pe.wait_ge(S("la_on"), n)
                    pe.wait_ge(S("la_S"), n)
                o = ps[0:r, 5, 0:GW]
                if not smp:
                    for a in range(M.nd):
                        w = GW // M.nd
                        pe.matmul(o[:, a * w:(a + 1) * w], la_x[:, n % 2, 7, a * r:(a + 1) * r],
                                  M.state[:, a * w:(a + 1) * w], start=(a == 0), stop=False,
                                  skip_group_check=True)
                for h in range(H):
                    ins = pe.matmul(o[:, h * HD:(h + 1) * HD], la_att[0:r, n % 2, h, 0:r],
                                    M.v[0:r, i, h * HD:(h + 1) * HD], start=(smp and h == 0), stop=True,
                                    skip_group_check=True)
                ins.then_inc(S("la_o"), 1)
                pe.wait_ge(S("la_kn"), n + 1)
                if not smp:
                    for a in range(M.nd):
                        w = GW // M.nd
                        ins = pe.matmul(ps[:, 6, a * w:(a + 1) * w], la_kn[0:r, n % 2, a * P:(a + 1) * P],
                                        M.v[0:r, i, a * w:(a + 1) * w], start=(a == 0), stop=True,
                                        skip_group_check=True)
                    ins.then_inc(S("la_s"), 1)

            def output_transposes(n):
                M, i, r, c0, smp = la_tile(n)
                pe.wait_ge(S("la_on"), n + 1)
                if n >= 1:
                    pe.wait_ge(S("la_mix"), n)
                for a in range(2):
                    ins = pe.transpose(ps[:, 7, a * P:a * P + r], la_o_n[0:r, n % 2, a * P:(a + 1) * P],
                                       ident[0:r, 0:r])
                ins.then_inc(S("la_oT"), 1)

            def sample_states(n):
                M, i, r, c0, smp = la_tile(n)
                k = MIX.index(M)
                pe.wait_ge(S("la_s0"), 16 * 8)
                for h in range(H):
                    c = H * k + h
                    a, rws = M.head(h)
                    if c >= 1:
                        pe.wait_ge(S("la_bigr"), c)
                    pe.matmul(ps[0:r, 6, :], la_x[rws, n % 2, 7, a * r:(a + 1) * r],
                              M.s0[rws, a, :, :], start=True, stop=True).then_inc(S("la_bigi"), 1)
                    pe.wait_ge(S("la_vexp"), c + 1)
                    if c >= 1:
                        pe.wait_ge(S("la_snew"), c)
                    kc = a * P + rws.start
                    pe.matmul(ps[rws, 4, :], la_kn[0:r, n % 2, kc:kc + M.dk], la_big[0:r, :, :],
                              start=True, stop=True).then_inc(S("la_bigs"), 1)

            for n in range(LT):
                smp = la_tile(n)[4]
                if not smp:
                    la_scores(pe, n, 0)
                key_transposes(n)
                if n >= 1:
                    output_transposes(n - 1)
                la_scores(pe, n, 1)
                if smp:
                    pe.wait_ge(S("la_kn"), n + 1)
                    sample_states(n)
                outputs(n)
            output_transposes(LT - 1)

        def la_scores(pe, n, g):
            M, i, r, c0, smp = la_tile(n)
            pe.wait_ge(S("la_tr"), n + 1)
            pe.wait_ge(S("la_tl"), n + 1)
            before = la_attD_count(n - 1) + (1 if g == 1 and not smp else 0)
            if before:
                pe.wait_ge(S("la_attD"), before)
            full = sum(not la_tile(j)[4] for j in range(n + (g == 1)))
            if full:
                pe.wait_ge(S("la_attA"), full)
            for slot, (lv, m) in enumerate(la_group(smp, g)):
                for h in range(H):
                    a, rws = M.head(h)
                    out = ps[:, h, slot * P:slot * P + P]
                    if lv is None:
                        ins = pe.matmul(out[0:r, 0:r], M.k[rws, a, c0:c0 + r], M.q[rws, a, c0:c0 + r],
                                        start=True, stop=True, skip_group_check=True)
                        continue
                    x = la_x[rws, n % 2, lv, a * r:(a + 1) * r]
                    if m >= 32:
                        for j in range(P // (2 * m)):
                            s0 = 2 * m * j
                            ins = pe.matmul(out[s0:s0 + m, s0 + m:s0 + 2 * m], x[:, s0:s0 + m],
                                            x[:, s0 + m:s0 + 2 * m], start=True, stop=True,
                                            skip_group_check=True)
                    else:
                        ins = pe.matmul(out[0:r, 0:r], x, x, start=True, stop=True, skip_group_check=True)
            ins.then_inc(S("la_att"), 1)

        def la_att_count(n, g):
            return la_attD_count(n - 1) + (1 if la_tile(n)[4] else g + 1)

        def la_mask(dve, step, n, g):
            M, i, r, c0, smp = la_tile(n)
            dve.wait_ge(S("la_att"), la_att_count(n, g))
            if n >= 2 and (g == 0 or smp):
                dve.wait_ge(S("la_o"), n - 1)
            if smp:
                step(dve.memset(la_att[:, n % 2, :, :], 0.0))
            elif g == 0:
                dve.wait_ge(S("la_attA"), sum(not la_tile(j)[4] for j in range(n + 1)))
            for slot, (lv, m) in enumerate(la_group(smp, g)):
                if m >= 32:
                    continue
                mask = ident if lv is None else up_mask[:, lv, :]
                step(dve.copy_predicated(la_att[0:r, n % 2, :, 0:r],
                                         mask[0:r, 0:r].bitcast(U32).unsqueeze(1).broadcast_to([r, H, r]),
                                         ps[0:r, 0:H, slot * P:slot * P + r]))
            dve.nop().then_inc(S("la_attD"), 1)

        def la_state(dve, n):
            M, i, r, c0, smp = la_tile(n)
            if smp:
                return
            dve.wait_ge(S("la_s"), sum(not la_tile(j)[4] for j in range(n + 1)))
            dve.wait_ge(S("la_o"), n + 1)
            dve.wait_ge(S("la_exp"), n + 1)
            dve.wait_ge(S("la_dl"), sum(not la_tile(j)[4] for j in range(n + 1)))
            for h in range(H):
                a, rws = M.head(h)
                blk = M.state[rws, h * HD:(h + 1) * HD]
                ins = dve.scalar_tensor_tensor(blk, blk, la_dlast[rws, n % 2, a:a + 1],
                                               ps[rws, 6, h * HD:(h + 1) * HD], ALU.mult, ALU.add)
            ins.then_inc(S("la_S"), 1)

        def la_normalise(dve, n):
            M, i, r, c0, smp = la_tile(n)
            o = ps[0:r, 5, 0:GW]
            if smp:
                dve.wait_ge(S("la_o"), n + 1)
                dve.tensor_tensor(la_inter[0:r, :], o, la_inter[0:r, :], ALU.add).then_inc(S("la_osum"), 1)
                o = la_inter[0:r, :]
            dve.wait_ge(S("la_sq"), n + 1)
            dve.tensor_reduce(la_ss[0:r, n % 2, :], la_o_sq[0:r, :].rearrange("p (h e) -> p h e", h=H), AX,
                              ALU.add).then_inc(S("la_ss"), 1)
            if smp:
                dve.wait_ge(S("la_osum"), n // NT + 1)
            else:
                dve.wait_ge(S("la_o"), n + 1)
            if n >= 2:
                dve.wait_ge(S("la_oT"), n - 1)
            on = la_o_n[0:r, n % 2, :]
            dve.tensor_tensor(on, o, M.gate[0:r, i, :], ALU.mult).then_inc(*did("dve"))
            dve.wait_ge(*so_far("dve"))
            dve.wait_ge(S("la_rs"), n + 1)
            dve.tensor_tensor(on.rearrange("p (h e) -> p h e", h=H), on.rearrange("p (h e) -> p h e", h=H),
                              la_ss[0:r, n % 2, :].unsqueeze(2).broadcast_to([r, H, HD]), ALU.mult)\
                .then_inc(S("la_on"), 1)

        def la_sample_vector(dve, n):
            M, i, r, c0, smp = la_tile(n)
            k = MIX.index(M)
            sm = seqmask[0:r, :].unsqueeze(2).broadcast_to([r, NB, HD])
            for h in range(H):
                c = H * k + h
                a, rws = M.head(h)
                dve.wait_ge(S("la_bigi"), c + 1)
                if c >= 1:
                    dve.wait_ge(S("la_bigs"), c)
                if h == 0 and k == 1:
                    dve.wait_ge(*so_far("dve"))
                dve.tensor_tensor(la_big[0:r, :, :], ps[0:r, 6, :].rearrange("p (b e) -> p b e", b=NB), sm,
                                  ALU.mult).then_inc(*did("dve"))
                dve.wait_ge(*so_far("dve"))
                dve.tensor_reduce(la_inter[0:r, h * HD:(h + 1) * HD],
                                  la_big[0:r, :, :].rearrange("p b e -> p e b"), AX, ALU.add)\
                    .then_inc(S("la_bigr"), 1)
                dve.wait_ge(S("la_bigr"), c + 1)
                dve.tensor_tensor(la_big[0:r, :, :],
                                  M.v[0:r, i, h * HD:(h + 1) * HD].unsqueeze(1).broadcast_to([r, NB, HD]), sm,
                                  ALU.mult).then_inc(S("la_vexp"), 1)
                gl = la_gl[rws, a * NB:(a + 1) * NB].unsqueeze(2).broadcast_to([M.dk, NB, HD])
                dve.wait_ge(S("la_exp"), n + 1)
                dve.wait_ge(S("la_bigs"), c + 1)
                dve.tensor_tensor(M.s0[rws, a, :, :], M.s0[rws, a, :, :], gl, ALU.mult)\
                    .then_inc(*did("dve"))
                dve.wait_ge(*so_far("dve"))
                dve.tensor_tensor(M.s0[rws, a, :, :], M.s0[rws, a, :, :],
                                  ps[rws, 4, :].rearrange("p (b e) -> p b e", b=NB), ALU.add)\
                    .then_inc(S("la_snew"), 1)

        def la_vector(dve):
            step = chain(dve, "dve")
            la_diffs(dve, 0, 1, "la_xr")
            la_times(dve, 0, 1, "la_tr")
            for n in range(LT):
                smp = la_tile(n)[4]
                if n + 1 < LT:
                    la_diffs(dve, n + 1, 1, "la_xr")
                if not smp:
                    la_mask(dve, step, n, 0)
                if n + 1 < LT:
                    la_times(dve, n + 1, 1, "la_tr")
                la_mask(dve, step, n, 1)
                if smp:
                    la_sample_vector(dve, n)
                    dve.nop().then_inc(S("la_S"), 1)
                la_state(dve, n)
                la_normalise(dve, n)

        def la_gpsimd(pool):
            la_diffs(pool, 0, 0, "la_xl")
            la_times(pool, 0, 0, "la_tl")
            for n in range(LT):
                if n + 1 < LT:
                    la_diffs(pool, n + 1, 0, "la_xl")
                    la_times(pool, n + 1, 0, "la_tl")
                if la_tile(n)[1] == NT - 2:
                    M = la_tile(n)[0]
                    pool.wait_ge(S("la_S"), n + 1)
                    for h in range(H):
                        a, rws = M.head(h)
                        pool.dma_start(M.out_p[0, 0, h], M.state[rws, h * HD:(h + 1) * HD])\
                            .then_inc(S("states_out"), 16)
            for M in MIX:
                pool.wait_ge(S("la_snew"), H * (MIX.index(M) + 1))
                for h in range(H):
                    a, rws = M.head(h)
                    pool.dma_start(M.out_s[0, :, h].rearrange("b d e -> d b e"), M.s0[rws, a, :, :])\
                        .then_inc(S("states_out"), 16)

        def la_act(act):
            def last_decay(n):
                M, i, r, c0, smp = la_tile(n)
                if smp:
                    return
                if n >= 2:
                    act.wait_ge(S("la_S"), n - 1)
                act.activation(la_dlast[:, n % 2, 0:M.nd].unsqueeze(2), M.b[:, :, c0 + r - 1:c0 + r], ACT.Exp,
                               scale=M.gscale).then_inc(S("la_dl"), 1)

            def direct(n):
                M, i, r, c0, smp = la_tile(n)
                if smp:
                    return
                act.wait_ge(S("la_att"), la_att_count(n, 0))
                if n >= 2:
                    act.wait_ge(S("la_o"), n - 1)
                act.wait_ge(S("la_zero"), 3)
                for slot, m in ((0, 64), (1, 32)):
                    for j in range(P // (2 * m)):
                        s0 = 2 * m * j
                        ins = act.activation(la_att[s0:s0 + m, n % 2, :, s0 + m:s0 + 2 * m],
                                             ps[s0:s0 + m, 0:H, slot * P + s0 + m:slot * P + s0 + 2 * m], ACT.Copy)
                ins.then_inc(S("la_attA"), 1)

            def mix_out(n):
                M, i, r, c0, smp = la_tile(n)
                act.wait_ge(S("la_oT"), n + 1)
                act.activation(mixT[:, M.kt0:M.kt0 + 2, c0:c0 + r],
                               ps[:, 7, 0:GW].rearrange("p (a t) -> p a t", a=2)[:, :, 0:r], ACT.Copy,
                               scale=M.norm).then_inc(S("la_mix"), 1)

            la_exp(act, 0)
            for n in range(LT):
                M, i, r, c0, smp = la_tile(n)
                if n + 1 < LT:
                    la_exp(act, n + 1)
                last_decay(n)
                direct(n)
                act.wait_ge(S("la_kT"), n + 1)
                if n >= 2:
                    act.wait_ge(S("la_o"), n - 1)
                    act.wait_ge(S("la_S"), n - 1)
                act.activation(la_kn[0:r, n % 2, 0:M.nd * P], ps[0:r, 4, 0:M.nd * P], ACT.Copy)\
                    .then_inc(S("la_kn"), 1)
                if n >= 1:
                    mix_out(n - 1)
                if smp:
                    act.wait_ge(S("la_osum"), n // NT + 1)
                act.wait_ge(S("la_o"), n + 1)
                if n >= 1:
                    act.wait_ge(S("la_ss"), n)
                act.activation(la_o_sq[0:r, :], la_inter[0:r, :] if smp else ps[0:r, 5, 0:GW], ACT.Square)\
                    .then_inc(S("la_sq"), 1)
                act.wait_ge(S("la_ss"), n + 1)
                ss = la_ss[0:r, n % 2, :]
                act.activation(ss, ss, ACT.Ln, scale=1.0 / HD, bias=eps_col[0:r, :]).then_inc(*did("act"))
                act.wait_ge(*so_far("act"))
                act.activation(ss, ss, ACT.Exp, scale=-0.5).then_inc(S("la_rs"), 1)
            mix_out(LT - 1)


        rwR, rwK, rwV = at(NR, 2, TOK), at(NR + 2 * TOK, 2, TOK), at(NR + 4 * TOK, 2, TOK)
        rwX = at(NR + 6 * TOK, TOK)
        rw_bonus = at(NR + 7 * TOK, 2, TOK)
        _o = NR + 9 * TOK
        rw_state = at(_o, GW)
        rw_stmp = at(_o + 256, GW)
        rw_inter = at(_o + 512, 2, GW)
        rw_big = at(_o + 1024, NB, HD)
        RP = PR + 8 * TOK
        rwKQ, rwAH, rwLW = at(RP, 2, TOK), at(RP + 2 * TOK, 2, TOK), at(RP + 4 * TOK, 2, TOK)
        rw_s0 = at(RP + 6 * TOK, 2, NB, HD)
        rwB, rwA = at(PR, 2, TOK), at(PR + 2 * TOK, 2, TOK)
        rwT1, rwT2 = at(PR + 4 * TOK, 2, TOK), at(PR + 6 * TOK, 2, TOK)
        rw_d = at(PR, 2, PADW)
        GR = RP + RWT * PADW
        rw_reset = at(GR, TOK)
        rw_s0_in = at(GR + TOK, 2, NB, P)
        rw_mats = at(WR, 4, 4, H, P)
        rw_sh9 = at(WR + 8192, RWT, 1 + NB)
        rw_pc = at(WR + 8256, 2, NT - 1 + NB)
        rw_col = at(WR + 8288, 8)
        rw_ms = at(WR + 8296, 2, H)
        rw_x = at(PR, 2, H, P)
        rw_t = at(PR + 1024, 2, H, P)
        rw_xt = at(PR + 2048, 4, H, P)
        rw_nat = at(PR + 4096, 4, 3, GW)
        rw_rh = at(PR + 7168, GW)
        rw_u = at(PR + 7424, GW)
        rw_yc = at(PR + 7680, GW)
        rw_sq = at(PR + 7936, GW)
        rw_mz = at(PR + 8192, GW)
        rw_shift_out = at(GR + TOK, RWT * P)
        LOG_DECAY = -math.exp(-0.5)
        LN_SCALE = 2.0 ** 30

        def rw_shifted(ct):
            return (rwR, rwR, rwK, rwK, rwV, rwV)[ct][:, ct % 2, :] if ct < 6 else rwX

        SHIFT_ORDER = (6, 2, 3, 0, 1, 4, 5)

        def rw_prep_vector(dve):
            step = chain(dve, "dve")
            dve.wait_ge(S("la_mix"), LT)
            dve.wait_ge(S("states_out"), 16 * 16)
            step(dve.tensor_copy(rw_sh9[:, :, 0:1], rwP[:, :, T:T + 1]))
            smp_view = rwP[:, :, 1 + T:].rearrange("p c (b t) -> p c b t", b=NB)
            dve.tensor_copy(rw_sh9[:, :, 1:].unsqueeze(3), smp_view[:, :, :, NS:NS + 1])\
                .then_inc(S("rw_sh9"), 1)
            step(dve.memset(rw_reset, 1.0))
            step(dve.memset(rw_reset[:, 0:T].rearrange("p (i t) -> p i t", t=P)[:, :, 0:1], 0.0))
            step(dve.memset(rw_reset[:, T:TOK].rearrange("p (i t) -> p i t", t=NS)[:, :, 0:1], 0.0))
            step(dve.memset(rw_col[:, 0:1], 0.5 * math.log(LN_SCALE)))
            step(dve.memset(rw_col[:, 1:2], RW_GN_EPS))
            dve.tensor_scalar(PAR["one_k_a"], PAR["k_a"], -1.0, 1.0, ALU.mult, ALU.add)\
                .then_inc(*did("dve"))
            for n, ct in enumerate(SHIFT_ORDER):
                d, dst, mu = rw_d[:, n % 2, 0:PADW - 1], rw_shifted(ct), PAR["mu"][:, ct:ct + 1]
                step(dve.tensor_tensor(d, rwP[:, ct, 0:PADW - 1], rwP[:, ct, 1:PADW], ALU.subtract))
                dve.scalar_tensor_tensor(dst[:, 0:T], d[:, 0:T], mu, rwP[:, ct, 1:1 + T], ALU.mult, ALU.add)
                tail = lambda t: t.rearrange("p (b t) -> p b t", b=NB)
                dve.scalar_tensor_tensor(tail(dst[:, T:TOK]), tail(d[:, T:PADW - 1])[:, :, 1:], mu,
                                         tail(rwP[:, ct, 1 + T:PADW])[:, :, 1:], ALU.mult, ALU.add)\
                    .then_inc(S("rw_xs"), 1)
            dve.wait_ge(S("rw_xs"), RWT)
            dve.wait_ge(*so_far("dve"))
            for a in range(2):
                step(dve.tensor_scalar(rwT1[:, a, :], rwK[:, a, :], PAR["k_k"][:, a:a + 1], None, ALU.mult))
                dve.tensor_tensor(rwT2[:, a, :], rwT1[:, a, :], rwT1[:, a, :], ALU.mult).then_inc(S("rw_kk2"), 1)
            dve.wait_ge(S("rw_gate"), 6)
            for a in range(2):
                step(dve.tensor_scalar(rwLW[:, a, :], rwLW[:, a, :], LOG_DECAY, None, ALU.mult))
                dve.tensor_tensor_scan(rwB[:, a, :], rw_reset, rwLW[:, a, :], 0.0, ALU.mult, ALU.add)\
                    .then_inc(*did("dve"))
            for q in range(6):
                a, (t0, tw) = q // 3, TG[q % 3]
                dve.wait_ge(S("rw_q"), 18 + q + 1)
                dve.tensor_scalar(rwT2[:, a, t0:t0 + tw], ps[:, q, 0:tw], 1e-24, None, ALU.max)\
                    .then_inc(S("rw_ss"), 1)
            dve.wait_ge(S("rw_gate"), 12)
            for a in range(2):
                step(dve.tensor_scalar(rwKQ[:, a, :], rwA[:, a, :], PAR["k_a"][:, a:a + 1],
                                       PAR["one_k_a"][:, a:a + 1], ALU.mult, ALU.add))
                step(dve.tensor_tensor(rwK[:, a, :], rwK[:, a, :], rwKQ[:, a, :], ALU.mult))
                dve.scalar_tensor_tensor(rwAH[:, a, :], rwR[:, a, :], PAR["r_k"][:, a:a + 1], rwK[:, a, :],
                                         ALU.mult, ALU.mult).then_inc(S("rw_rkrk"), 1)
            for q in range(6):
                a, (t0, tw) = q // 3, TG[q % 3]
                dve.wait_ge(S("rw_q"), 24 + q + 1)
                dve.tensor_tensor(rw_bonus[:, a, t0:t0 + tw], ps[:, q, 0:tw], rwV[:, a, t0:t0 + tw], ALU.mult)\
                    .then_inc(*did("dve"))
            dve.wait_ge(S("rw_rn"), 2)
            dve.wait_ge(*so_far("dve"))
            for a in range(2):
                step(dve.tensor_tensor(rwT1[:, a, :], rwT1[:, a, :], rwT2[:, a, :], ALU.mult))
                dve.tensor_tensor(rwT2[:, a, :], rwB[:, a, :], rwLW[:, a, :], ALU.subtract)\
                    .then_inc(S("rw_bprev"), 1)
            for a in range(2):
                step(dve.tensor_tensor(rwAH[:, a, :], rwT1[:, a, :], rwA[:, a, :], ALU.mult))
                dve.wait_ge(S("rw_e"), 3 * a + 1)
                dve.scalar_tensor_tensor(rwKQ[:, a, :], rwT1[:, a, :], -1.0, rwT2[:, a, :], ALU.mult, ALU.mult)
                dve.wait_ge(S("rw_e"), 3 * a + 2)
                dve.tensor_tensor(rwAH[:, a, :], rwAH[:, a, :], rwLW[:, a, :], ALU.mult)
                dve.tensor_tensor(rwK[:, a, :], rwK[:, a, :], rwLW[:, a, :], ALU.mult)
                dve.wait_ge(S("rw_e"), 3 * a + 3)
                dve.tensor_copy(rw_pc[:, a, 0:NT - 1], rwB[:, a, P - 1:T:P])
                dve.tensor_copy(rw_pc[:, a, NT - 1:], rwB[:, a, T + NS - 1:TOK:NS])
                dve.tensor_tensor(rwR[:, a, :], rwR[:, a, :], rwB[:, a, :], ALU.mult).then_inc(S("rw_ready"), 1)
            dve.memset(rw_state, 0.0).then_inc(*did("dve"))
            dve.wait_ge(S("rw_ready"), 2)
            dve.wait_ge(*so_far("dve"))

        def rw_prep_act(act):
            act.wait_ge(S("rw_shp"), 1)
            act.activation(rw_shift_out[0:1 + NB, 0:512], ps[0:1 + NB, 6, :], ACT.Copy)
            act.activation(rw_shift_out[0:1 + NB, 512:RWT * P], ps[0:1 + NB, 7, 0:RWT * P - 512], ACT.Copy)\
                .then_inc(S("rw_shout"), 1)
            act.wait_ge(S("rw_xs"), 1)
            act.activation(rwX[0:32, :], rwX[0:32, :], ACT.Tanh).then_inc(S("rw_lr"), 1)
            act.activation(rwX[64:128, :], rwX[64:128, :], ACT.Sigmoid).then_inc(S("rw_lr"), 1)
            act.wait_ge(S("rw_xs"), RWT)
            for q in range(18):
                kind, a, (t0, tw) = q // 6, q % 6 // 3, TG[q % 3]
                act.wait_ge(S("rw_q"), q + 1)
                src = ps[:, q % 6, 0:tw]
                if kind == 0:
                    ins = act.activation(rwLW[:, a, t0:t0 + tw], src, ACT.Sigmoid, bias=PAR["w0"][:, a:a + 1])
                elif kind == 1:
                    ins = act.activation(rwA[:, a, t0:t0 + tw], src, ACT.Sigmoid, bias=PAR["a0"][:, a:a + 1])
                else:
                    ins = act.activation(mixT[:, 2 + a, t0:t0 + tw], src, ACT.Copy)
                ins.then_inc(S("rw_gate"), 1)
            act.preload_act_table_set("natural_log_exp_and_others")
            act.wait_ge(S("rw_ss"), 6)
            for a in range(2):
                act.activation(rwT2[:, a, :], rwT2[:, a, :], ACT.Ln, scale=LN_SCALE).then_inc(*did("act"))
                act.wait_ge(*so_far("act"))
                act.activation(rwT2[:, a, :], rwT2[:, a, :], ACT.Exp, scale=-0.5, bias=rw_col[:, 0:1])\
                    .then_inc(S("rw_rn"), 1)
            act.wait_ge(S("rw_bprev"), 2)
            for a in range(2):
                act.activation(rwT2[:, a, :], rwT2[:, a, :], ACT.Exp).then_inc(S("rw_e"), 1)
                act.activation(rwLW[:, a, :], rwB[:, a, :], ACT.Exp, scale=-1.0).then_inc(S("rw_e"), 1)
                act.activation(rwB[:, a, :], rwB[:, a, :], ACT.Exp).then_inc(S("rw_e"), 1)

        def rw_prep_tensor(pe):
            pe.wait_ge(S("la_mix"), LT)
            pe.wait_ge(S("rw_sh9"), 1)
            for ct in range(RWT):
                ins = pe.transpose(ps[0:1 + NB, 6 + ct // 4, (ct % 4) * P:(ct % 4) * P + P], rw_sh9[:, ct, :],
                                   ident)
            ins.then_inc(S("rw_shp"), 1)
            for q in range(30):
                kind, a, (t0, tw) = q // 6, q % 6 // 3, TG[q % 3]
                if kind == 0:
                    pe.wait_ge(S("rw_lr"), 1)
                    lhs, rhs = w2all[0:32, a * P:(a + 1) * P], rwX[0:32, t0:t0 + tw]
                elif kind == 1:
                    pe.wait_ge(S("rw_gate"), q - 5)
                    lhs, rhs = w2all[32:64, a * P:(a + 1) * P], rwX[32:64, t0:t0 + tw]
                elif kind == 2:
                    pe.wait_ge(S("rw_gate"), q - 5)
                    pe.wait_ge(S("rw_lr"), 2)
                    lhs, rhs = w2all[64:128, a * P:(a + 1) * P], rwX[64:128, t0:t0 + tw]
                elif kind == 3:
                    pe.wait_ge(S("rw_gate"), q - 5)
                    pe.wait_ge(S("rw_kk2"), a + 1)
                    lhs, rhs = headones, rwT2[:, a, t0:t0 + tw]
                else:
                    pe.wait_ge(S("rw_ss"), q - 23)
                    pe.wait_ge(S("rw_rkrk"), a + 1)
                    lhs, rhs = headones, rwAH[:, a, t0:t0 + tw]
                pe.matmul(ps[:, q % 6, 0:tw], lhs, rhs, start=True, stop=True).then_inc(S("rw_q"), 1)
            pe.wait_ge(S("rw_s0_in"), 64)
            pe.wait_ge(S("rw_shout"), 1)
            for a in range(2):
                for b in range(NB):
                    ins = pe.transpose(ps[:, 6 + a, b * HD:(b + 1) * HD], rw_s0_in[0:HD, a, b, :],
                                       ident[0:HD, 0:HD])
            ins.then_inc(S("rw_s0p"), 1)

        def rw_gpsimd(pool):
            pool.wait_ge(S("la_mix"), LT)
            pool.wait_ge(S("states_out"), 16 * 16)
            for sl in range(4):
                pool.memset(rw_mats[:, sl, :, :, :], 0.0).then_inc(S("rw_m0"), 1)
            pool.wait_ge(S("rw_m0"), 4)
            for sl in range(4):
                pool.tensor_copy(rw_mats[:, sl, 0, :, :], ident.unsqueeze(1).broadcast_to([P, H, P]))\
                    .then_inc(S("rw_m0"), 1)
            pool.wait_ge(S("rw_shout"), 1)
            pool.dma_start(O["rwkv_shift_prompt"][0], rw_shift_out[0:1, :]).then_inc(S("shift_out"), 16)
            pool.dma_start(O["rwkv_shift_sample"][0], rw_shift_out[1:1 + NB, :]).then_inc(S("shift_out"), 16)
            pool.wait_ge(S("shift_out"), 32)
            for h in range(H):
                c = h % 2
                pool.dma_start(rw_s0_in[0:HD, h // 2, :, 64 * c:64 * c + 64],
                               A["state_rwkv"][0, :, h, :, :].rearrange("b v k -> v b k"))\
                    .then_inc(S("rw_s0_in"), 16)
            pool.wait_ge(S("rw_fin_p"), 1)
            for h in range(H):
                c, a = h % 2, h // 2
                pool.dma_start(O["rwkv_prompt"][0, 0, h],
                               rw_stmp[64 * c:64 * c + 64, a * P + 64 * c:a * P + 64 * c + 64])\
                    .then_inc(S("rw_states_out"), 16)
            pool.wait_ge(S("rw_fin_s"), 4)
            for h in range(H):
                c = h % 2
                pool.dma_start(O["rwkv_sample"][0, :, h, :, :].rearrange("b v k -> v b k"),
                               rw_s0_in[0:HD, h // 2, :, 64 * c:64 * c + 64]).then_inc(S("rw_states_out"), 16)

        def rw_schedule():
            items = []
            pairs = [(0, 1), (2, 3), (4, 5), (6, 7), (NT - 1,)]
            for p, pair in enumerate(pairs):
                prev = pairs[p - 1] if p else ()
                fill = [(k, prev[j]) for k, j in (("rhs", 0), ("solve", 0), ("out", 0), ("rhs", 1), ("turn", 0),
                                                  ("solve", 1), ("out", 1), ("turn", 1))] if p else []
                items += [("front", n) for n in pair]
                for lv in range(6, -1, -1) if len(pair) == 2 else (6, 5, 4):
                    items += [("join_a", n, lv) for n in pair]
                    items += [fill.pop(0)] if fill else []
                    items += [("join_b", n, lv) for n in pair]
                    if len(fill) > 6 or len(pair) == 1:
                        items += [fill.pop(0)] if fill else []
                items += fill
            return items

        RW_ITEMS = rw_schedule()

        def rw_upto(kind, *key):
            last = max(j for j, it in enumerate(RW_ITEMS) if it[0] == kind and it[1:1 + len(key)] == key)
            return sum(it[0] == kind for it in RW_ITEMS[:last + 1])

        def rw_last_level(n):
            return 4 if n == NT - 1 else 0

        def rw_before(kind, at_item):
            return sum(it[0] == kind for it in RW_ITEMS[:RW_ITEMS.index(at_item)])

        def rw_tensor(pe):
            for item in RW_ITEMS:
                kind, n = item[0], item[1]
                r, c0 = rows(n), n * P
                cols = slice(c0, c0 + r)
                sl, e = n % 4, n % 2
                nat = rw_nat[0:r, sl, :, :]
                if kind == "front":
                    if n == 0:
                        pe.wait_ge(S("rw_ready"), 2)
                    else:
                        pe.wait_ge(S("rw_mats"), n)
                        pe.wait_ge(S("rw_nat"), n)
                        if rw_before("join_b", item):
                            pe.wait_ge(S("rw_xx"), rw_before("join_b", item))
                    for h in range(H):
                        a, rws = h // 2, slice(64 * (h % 2), 64 * (h % 2) + 64)
                        for ty, (lhs, rhs) in enumerate(((rwAH, rwKQ), (rwK, rwKQ), (rwAH, rwR), (rwK, rwR))):
                            ins = pe.matmul(ps[0:r, h, ty * P:ty * P + r], lhs[rws, a, cols], rhs[rws, a, cols],
                                            start=True, stop=True, skip_group_check=True)
                    ins.then_inc(S("rw_mp"), 1)
                    for y, src in enumerate((rwK, rwAH, rwV)):
                        for a in range(2):
                            ins = pe.transpose(ps[0:r, 4 + y // 2, (y % 2) * GW + a * P:(y % 2) * GW + (a + 1) * P],
                                               src[:, a, cols], ident)
                    ins.then_inc(S("rw_np"), 1)
                elif kind == "join_a":
                    lv = item[2]
                    first = lv == 6
                    if first:
                        pe.wait_ge(S("rw_mats"), n + 1)
                        pe.wait_ge(S("rw_nat"), min(NT, (n // 2) * 2 + 2))
                        pe.wait_ge(S("rw_mats"), min(NT, (n // 2) * 2 + 2))
                    else:
                        pe.wait_ge(S("rw_xx"), rw_upto("join_b", n, lv + 1))
                    for h in range(H):
                        x = ident[0:r, 0:r] if first else (rw_t if lv == 5 else rw_x)[0:r, e, h, 0:r]
                        ins = pe.matmul(ps[0:r, 3 * e, h * P:h * P + r], rw_mats[0:r, sl, 0, h, 0:r], x,
                                        start=(h == 0), stop=True, skip_group_check=True)
                    ins.then_inc(S("rw_ja"), 1)
                elif kind == "join_b":
                    lv = item[2]
                    pe.wait_ge(S("rw_t1"), rw_upto("join_a", n, lv))
                    for h in range(H):
                        t1 = rw_t[0:r, e, h, 0:r]
                        if lv != 6 and lv != rw_last_level(n):
                            pe.matmul(ps[0:r, 3 * e + 1, h * P:h * P + r], rw_xt[0:r, sl, h, 0:r], t1,
                                      start=(h == 0), stop=True, skip_group_check=True)
                        xt = ident[0:r, 0:r] if lv == 6 else rw_xt[0:r, sl, h, 0:r]
                        ins = pe.matmul(ps[0:r, 3 * e + 2, h * P:h * P + r], t1, xt, start=(h == 0), stop=True,
                                        skip_group_check=True)
                    ins.then_inc(S("rw_jb"), 1)
                elif kind == "rhs":
                    pe.wait_ge(S("rw_nat"), n + 1)
                    if n >= 1:
                        pe.wait_ge(S("rw_S"), n)
                        pe.wait_ge(S("rw_u"), n)
                    else:
                        pe.wait_ge(S("rw_s0"), 1)
                    for a in range(2):
                        pe.matmul(ps[0:r, 6, a * P:(a + 1) * P], rwKQ[:, a, cols], rw_state[:, a * P:(a + 1) * P],
                                  start=(a == 0), stop=False, skip_group_check=True)
                    for h in range(H):
                        hc = slice(h * HD, (h + 1) * HD)
                        ins = pe.matmul(ps[0:r, 6, hc], rw_mats[0:r, sl, 1, h, 0:r], nat[:, 2, hc], start=False,
                                        stop=True, skip_group_check=True)
                    ins.then_inc(S("rw_c1"), 1)
                elif kind == "solve":
                    pe.wait_ge(S("rw_rh"), n + 1)
                    pe.wait_ge(S("rw_xx"), rw_upto("join_b", n, rw_last_level(n)))
                    for h in range(H):
                        hc = slice(h * HD, (h + 1) * HD)
                        ins = pe.matmul(ps[0:r, 6, GW + h * HD:GW + (h + 1) * HD], rw_xt[0:r, sl, h, 0:r],
                                        rw_rh[0:r, hc], start=(h == 0), stop=True, skip_group_check=True)
                    ins.then_inc(S("rw_c2"), 1)
                elif kind == "out":
                    pe.wait_ge(S("rw_u"), n + 1)
                    if n >= 1:
                        pe.wait_ge(S("rw_mz"), n)
                    for a in range(2):
                        pe.matmul(ps[0:r, 7, a * P:(a + 1) * P], rwR[:, a, cols], rw_state[:, a * P:(a + 1) * P],
                                  start=(a == 0), stop=False, skip_group_check=True)
                    for h in range(H):
                        hc = slice(h * HD, (h + 1) * HD)
                        pe.matmul(ps[0:r, 7, hc], rw_mats[0:r, sl, 2, h, 0:r], rw_u[0:r, hc], start=False,
                                  stop=False, skip_group_check=True)
                        pe.matmul(ps[0:r, 7, hc], rw_mats[0:r, sl, 3, h, 0:r], nat[:, 2, hc], start=False,
                                  stop=True, skip_group_check=True)
                    for a in range(2):
                        ac = slice(a * P, (a + 1) * P)
                        pe.matmul(ps[:, 7, GW + a * P:GW + (a + 1) * P], nat[:, 1, ac], rw_u[0:r, ac],
                                  start=False, stop=False, skip_group_check=True)
                        ins = pe.matmul(ps[:, 7, GW + a * P:GW + (a + 1) * P], nat[:, 0, ac], nat[:, 2, ac],
                                        start=False, stop=True, skip_group_check=True)
                    ins.then_inc(S("rw_c3"), 1)
                elif kind == "turn":
                    pe.wait_ge(S("rw_yn"), n + 1)
                    pe.wait_ge(S("rw_S"), n + 1)
                    for a in range(2):
                        ins = pe.transpose(ps[:, 7, a * P:a * P + r], rw_yc[0:r, a * P:(a + 1) * P],
                                           ident[0:r, 0:r])
                    ins.then_inc(S("rw_c6"), 1)

        def rw_vector(dve):
            step = chain(dve, "dve")
            dve.wait_ge(S("rw_m0"), 8)
            for item in RW_ITEMS:
                kind, n = item[0], item[1]
                r, c0 = rows(n), n * P
                cols = slice(c0, c0 + r)
                sl, e = n % 4, n % 2
                if kind == "front":
                    smp = n == NT - 1
                    if n >= 4:
                        dve.wait_ge(S("rw_c3"), n - 3)
                    if smp:
                        step(dve.memset(rw_mats[0:r, sl, :, :, 0:r], 0.0))
                        step(dve.tensor_copy(rw_mats[0:r, sl, 0, :, 0:r],
                                             ident[0:r, 0:r].unsqueeze(1).broadcast_to([r, H, r])))
                    dve.wait_ge(S("rw_mp"), n + 1)
                    for ty in range(4):
                        mask = ((upper8 if smp else upper) if ty < 2 else (upper8_eq if smp else upper_eq))
                        ins = dve.copy_predicated(rw_mats[0:r, sl, ty, :, 0:r],
                                                  mask[0:r, 0:r].bitcast(U32).unsqueeze(1).broadcast_to([r, H, r]),
                                                  ps[0:r, 0:H, ty * P:ty * P + r])
                    ins.then_inc(S("rw_mats"), 1)
                elif kind == "join_a":
                    lv = item[2]
                    dve.wait_ge(S("rw_ja"), rw_upto("join_a", n, lv))
                    heads = lambda t: t.rearrange("p (h t) -> p h t", h=H)[:, :, 0:r]
                    dve.tensor_tensor(rw_t[0:r, e, :, 0:r], heads(ps[0:r, 3 * e, :]),
                                      low_eq[0:r, lv, 0:r].unsqueeze(1).broadcast_to([r, H, r]), ALU.mult)\
                        .then_inc(S("rw_t1"), 1)
                elif kind == "out":
                    dve.wait_ge(S("rw_c3"), n + 1)
                    y = ps[0:r, 7, 0:GW].rearrange("p (h e) -> p h e", h=H)
                    step(dve.tensor_tensor(rw_stmp, rw_state, ps[:, 7, GW:2 * GW], ALU.add))
                    for a in range(2):
                        ac = slice(a * P, (a + 1) * P)
                        ins = dve.scalar_tensor_tensor(rw_state[:, ac], rw_stmp[:, ac], rw_pc[:, a, n:n + 1],
                                                       headones, ALU.mult, ALU.mult)
                    ins.then_inc(S("rw_S"), 1)
                    rw_norm(dve, step, n, r, y)
                elif kind == "turn":
                    rw_mix(dve, step, n, r, cols)

        def rw_norm(dve, step, n, r, y):
            step(dve.tensor_reduce(rw_ms[0:r, 0, :], y, AX, ALU.add))
            if n >= 1:
                dve.wait_ge(S("rw_c6"), n)
            yc = rw_yc[0:r, :].rearrange("p (h e) -> p h e", h=H)
            dve.scalar_tensor_tensor(yc, rw_ms[0:r, 0, :].unsqueeze(2).broadcast_to([r, H, HD]), -1.0 / HD, y,
                                     ALU.mult, ALU.add).then_inc(S("rw_yc"), 1)
            dve.wait_ge(S("rw_ysq"), n + 1)
            dve.tensor_reduce(rw_ms[0:r, 1, :], rw_sq[0:r, :].rearrange("p (h e) -> p h e", h=H), AX,
                              ALU.add).then_inc(S("rw_var"), 1)
            dve.wait_ge(S("rw_yrs"), n + 1)
            dve.tensor_tensor(yc, yc, rw_ms[0:r, 1, :].unsqueeze(2).broadcast_to([r, H, HD]), ALU.mult)\
                .then_inc(S("rw_yn"), 1)

        def rw_mix(dve, step, n, r, cols):
            dve.wait_ge(S("rw_mz"), n + 1)
            z = rw_mz.rearrange("p (a t) -> p a t", a=2)[:, :, 0:r]
            step(dve.tensor_tensor(z, z, rw_bonus[:, :, cols], ALU.add))
            dve.tensor_tensor(mixT[:, 2:4, cols], z, mixT[:, 2:4, cols], ALU.mult).then_inc(S("rw_done"), 1)

        def rw_act_norm(act, n, r):
            act.wait_ge(S("rw_yc"), n + 1)
            act.activation(rw_sq[0:r, :], rw_yc[0:r, :], ACT.Square).then_inc(S("rw_ysq"), 1)
            act.wait_ge(S("rw_var"), n + 1)
            v = rw_ms[0:r, 1, :]
            act.activation(v, v, ACT.Ln, scale=1.0 / HD, bias=rw_col[0:r, 1:2]).then_inc(*did("act"))
            act.wait_ge(*so_far("act"))
            act.activation(v, v, ACT.Exp, scale=-0.5).then_inc(S("rw_yrs"), 1)

        def rw_act_turn(act, n, r):
            act.wait_ge(S("rw_c6"), n + 1)
            if n >= 1:
                act.wait_ge(S("rw_done"), n)
            for a in range(2):
                ins = act.activation(rw_mz[:, a * P:a * P + r], ps[:, 7, a * P:a * P + r], ACT.Identity,
                                     scale=PAR["ln_w"][:, a:a + 1], bias=PAR["ln_b"][:, a:a + 1])
            ins.then_inc(S("rw_mz"), 1)

        def rw_act(act):
            act.wait_ge(S("rw_s0p"), 1)
            act.activation(rw_s0.rearrange("p a b e -> p a (b e)"), ps[:, 6:8, :], ACT.Copy)\
                .then_inc(S("rw_s0"), 1)
            act.wait_ge(S("rw_ready"), 2)
            for item in RW_ITEMS:
                kind, n = item[0], item[1]
                r = rows(n)
                sl, e = n % 4, n % 2
                if kind == "front":
                    act.wait_ge(S("rw_np"), n + 1)
                    if n >= 4:
                        act.wait_ge(S("rw_c3"), n - 3)
                    act.activation(rw_nat[0:r, sl, 0:2, :],
                                   ps[0:r, 4, :].rearrange("p (y c) -> p y c", y=2), ACT.Copy)
                    act.activation(rw_nat[0:r, sl, 2, :], ps[0:r, 5, 0:GW], ACT.Copy).then_inc(S("rw_nat"), 1)
                elif kind == "join_b":
                    lv = item[2]
                    act.wait_ge(S("rw_jb"), rw_upto("join_b", n, lv))
                    heads = lambda t: t.rearrange("p (h t) -> p h t", h=H)[:, :, 0:r]
                    if lv != 6 and lv != rw_last_level(n):
                        act.activation(rw_x[0:r, e, :, 0:r], heads(ps[0:r, 3 * e + 1, :]), ACT.Copy)
                    act.activation(rw_xt[0:r, sl, :, 0:r], heads(ps[0:r, 3 * e + 2, :]), ACT.Copy)\
                        .then_inc(S("rw_xx"), 1)
                elif kind == "rhs":
                    act.wait_ge(S("rw_c1"), n + 1)
                    if n >= 1:
                        act.wait_ge(S("rw_c2"), n)
                    act.activation(rw_rh[0:r, :], ps[0:r, 6, 0:GW], ACT.Copy).then_inc(S("rw_rh"), 1)
                elif kind == "solve":
                    act.wait_ge(S("rw_c2"), n + 1)
                    if n >= 1:
                        act.wait_ge(S("rw_c3"), n)
                    act.activation(rw_u[0:r, :], ps[0:r, 6, GW:2 * GW], ACT.Copy).then_inc(S("rw_u"), 1)
                elif kind == "out":
                    rw_act_norm(act, n, r)
                elif kind == "turn":
                    rw_act_turn(act, n, r)

        def rws_tensor(pe):
            n, r, cols = NT - 1, SMP, slice(T, TOK)
            sl = n % 4
            nat = rw_nat[0:r, sl, :, :]
            pe.wait_ge(S("rw_mz"), NT - 1)
            pe.wait_ge(S("rw_u"), NT - 1)
            for c in range(2 * H):
                h = c % H
                rws = slice(64 * (h % 2), 64 * (h % 2) + 64)
                if c >= 2:
                    pe.wait_ge(S("rws_sel"), c - 1)
                pe.matmul(ps[0:r, 6 + c % 2, :], (rwKQ, rwR)[c // H][rws, h // 2, cols],
                          rw_s0[rws, h // 2, :, :], start=True, stop=True).then_inc(S("rws_big"), 1)
            pe.wait_ge(S("rws_sel"), 2 * H)
            pe.wait_ge(S("rw_nat"), NT)
            for h in range(H):
                hc = slice(h * HD, (h + 1) * HD)
                ins = pe.matmul(ps[0:r, 6, hc], rw_mats[0:r, sl, 1, h, 0:r], nat[:, 2, hc], start=(h == 0),
                                stop=True, skip_group_check=True)
            ins.then_inc(S("rws_c1"), 1)
            pe.wait_ge(S("rws_rh"), 1)
            pe.wait_ge(S("rw_xx"), rw_upto("join_b", n, rw_last_level(n)))
            for h in range(H):
                hc = slice(h * HD, (h + 1) * HD)
                ins = pe.matmul(ps[0:r, 6, GW + h * HD:GW + (h + 1) * HD], rw_xt[0:r, sl, h, 0:r], rw_rh[0:r, hc],
                                start=(h == 0), stop=True, skip_group_check=True)
            ins.then_inc(S("rws_c2"), 1)
            pe.wait_ge(S("rws_u"), 1)
            for h in range(H):
                hc = slice(h * HD, (h + 1) * HD)
                pe.matmul(ps[0:r, 7, hc], rw_mats[0:r, sl, 2, h, 0:r], rw_u[0:r, hc], start=(h == 0), stop=False,
                          skip_group_check=True)
                ins = pe.matmul(ps[0:r, 7, hc], rw_mats[0:r, sl, 3, h, 0:r], nat[:, 2, hc], start=False,
                                stop=True, skip_group_check=True)
            ins.then_inc(S("rws_y"), 1)
            for h in range(H):
                rws = slice(64 * (h % 2), 64 * (h % 2) + 64)
                for y in range(2):
                    pe.wait_ge(S("rws_exp"), 2 * h + y + 1)
                    pe.matmul(ps[rws, h, :], nat[:, 1 - y, h * HD:(h + 1) * HD], rw_big[0:r, :, :],
                              start=(y == 0), stop=(y == 1)).then_inc(S("rws_inc"), 1)
            pe.wait_ge(S("rw_yn"), NT)
            for a in range(2):
                ins = pe.transpose(ps[:, 7, a * P:a * P + r], rw_yc[0:r, a * P:(a + 1) * P], ident[0:r, 0:r])
            ins.then_inc(S("rw_c6"), 1)
            pe.wait_ge(S("rw_S"), NT - 1)
            for a in range(2):
                ins = pe.transpose(ps[:, 6, a * P:(a + 1) * P], rw_state[:, a * P:(a + 1) * P], ident)
            ins.then_inc(S("rw_finp"), 1)
            for g in range(4):
                pe.wait_ge(S("rws_new"), H)
                for j in range(4):
                    b = 4 * (g % 2) + j
                    ins = pe.transpose(ps[0:HD, g, j * P:(j + 1) * P], rw_s0[:, g // 2, b, :], ident)
                ins.then_inc(S("rw_fins"), 1)

        def rws_vector(dve):
            n, r, cols = NT - 1, SMP, slice(T, TOK)
            step = chain(dve, "dve")
            sm = seqmask[0:r, :].unsqueeze(2).broadcast_to([r, NB, HD])
            for c in range(2 * H):
                h = c % H
                dve.wait_ge(S("rws_big"), c + 1)
                if c >= 1:
                    dve.wait_ge(S("rws_sel"), c)
                step(dve.tensor_tensor(rw_big[0:r, :, :], ps[0:r, 6 + c % 2, :].rearrange(
                    "p (b e) -> p b e", b=NB), sm, ALU.mult))
                dve.tensor_reduce(rw_inter[0:r, c // H, h * HD:(h + 1) * HD],
                                  rw_big[0:r, :, :].rearrange("p b e -> p e b"), AX, ALU.add)\
                    .then_inc(S("rws_sel"), 1)
            dve.wait_ge(S("rws_sel"), 2 * H)
            dve.wait_ge(S("rws_c1"), 1)
            dve.wait_ge(S("rw_c2"), NT - 1)
            dve.tensor_tensor(rw_rh[0:r, :], ps[0:r, 6, 0:GW], rw_inter[0:r, 0, :], ALU.add)\
                .then_inc(S("rws_rh"), 1)
            dve.wait_ge(S("rws_y"), 1)
            step(dve.tensor_tensor(rw_inter[0:r, 1, :], ps[0:r, 7, 0:GW], rw_inter[0:r, 1, :], ALU.add))
            for h in range(H):
                rws, a = slice(64 * (h % 2), 64 * (h % 2) + 64), h // 2
                for y, src in enumerate((rw_u[0:r, :], rw_nat[0:r, n % 4, 2, :])):
                    if h or y:
                        dve.wait_ge(S("rws_inc"), 2 * h + y)
                    dve.tensor_tensor(rw_big[0:r, :, :],
                                      src[:, h * HD:(h + 1) * HD].unsqueeze(1).broadcast_to([r, NB, HD]), sm,
                                      ALU.mult).then_inc(S("rws_exp"), 1)
                dve.wait_ge(S("rws_inc"), 2 * h + 2)
                step(dve.tensor_tensor(rw_s0[rws, a, :, :], rw_s0[rws, a, :, :],
                                       ps[rws, h, :].rearrange("p (b e) -> p b e", b=NB), ALU.add))
                dve.tensor_tensor(rw_s0[rws, a, :, :], rw_s0[rws, a, :, :],
                                  rw_pc[rws, a, NT - 1:].unsqueeze(2).broadcast_to([64, NB, HD]), ALU.mult)\
                    .then_inc(S("rws_new"), 1)
            rw_norm(dve, step, n, r, rw_inter[0:r, 1, :].rearrange("p (h e) -> p h e", h=H))
            rw_mix(dve, step, n, r, cols)

        def rws_act(act):
            n, r = NT - 1, SMP
            act.wait_ge(S("rws_c2"), 1)
            act.wait_ge(S("rw_c3"), NT - 1)
            act.activation(rw_u[0:r, :], ps[0:r, 6, GW:2 * GW], ACT.Copy).then_inc(S("rws_u"), 1)
            rw_act_norm(act, n, r)
            rw_act_turn(act, n, r)
            act.wait_ge(S("rw_finp"), 1)
            act.activation(rw_stmp, ps[:, 6, 0:GW], ACT.Copy).then_inc(S("rw_fin_p"), 1)
            for g in range(4):
                act.wait_ge(S("rw_fins"), g + 1)
                act.activation(rw_s0_in[0:HD, g // 2, 4 * (g % 2):4 * (g % 2) + 4, :],
                               ps[0:HD, g, :].rearrange("p (b k) -> p b k", b=4), ACT.Copy)\
                    .then_inc(S("rw_fin_s"), 1)


        CH = 512
        NCH = FF // CH
        FT = CH // P
        uT = at(CONST_END, FT, TOK)
        x1 = at(PR, NT, D)
        h2T = at(PR + NT * D, KD, TOK)
        y_acc = at(PR + NT * D + KD * TOK, NT, D)
        w_out = at(PR + NT * D + KD * TOK, KD, D)
        _o = PR + 2 * NT * D + KD * TOK
        wu = at(_o, 2, KD, 256)
        wd = at(_o + 4096, 2, 2, D)
        post_gain = at(_o + 8192, D)
        x_again = at(_o + 4096, 2, D)
        h2 = at(_o + 6144, 2, D)
        d_junk = at(_o + 9216 + 2 * NT, D)
        d_ss = at(_o + 9216, 2 * NT)

        W_LOADS = [(len(GROUPS) + WSLOTS - 1 - g) // WSLOTS for g in range(WSLOTS)]

        def mlp_out_sync(sp):
            sp.wait_ge(S("rw_done"), NT)
            sp.wait_ge(S("rw_fin_s"), 4)
            sp.wait_ge(S("rw_states_out"), 16 * 8)
            sp.wait_ge(S("shift_out"), 32)
            for half in range(2):
                sp.dma_start(w_out[:, :, half * 512:half * 512 + 512],
                             A["w_out"][0].rearrange("(k p) c -> p k c", p=P)[:, :, half * 512:half * 512 + 512])\
                    .then_inc(S("params"), 16)
            sp.dma_start(post_gain, A["norm_mix_post"][0].partition_broadcast(P)).then_inc(S("params"), 16)
            for i in range(NT):
                if i >= 2:
                    sp.wait_ge(S("m_x1"), i - 1)
                sp.dma_start(x_again[0:rows(i), i % 2, :], x_rows(i)).then_inc(S(f"x_in{i % 2}"), 16)
                if i == 2:
                    for g in range(2):
                        load_up(sp, 0, g)
            sp.wait_ge(S("m_x1"), NT)
            sp.dma_start(post_gain, A["norm_ffn_post"][0].partition_broadcast(P)).then_inc(S("params"), 16)
            sp.wait_ge(S("hT"), 2 * NT + 2 * NT)
            for g in range(2):
                load_down(sp, 0, g)
            with sp.Fori(1, NCH) as c:
                for g in range(2):
                    sp.wait_ge(S("up_ps"), c * (3 * FT) + (g - 1) * (3 * FT // 2))
                    load_up(sp, c, g)
                sp.wait_ge(S("dn_ps"), c * (2 * NT))
                for g in range(2):
                    load_down(sp, c, g)

        def load_up(sp, c, g):
            sp.dma_start(wu[:, g, :, :], A["w_up"][0].rearrange("(k p) (n f) -> p k n f", p=P, f=256)
                         [:, :, bass.ds(c * 2 + g, 1), :].rearrange("p k n f -> p k (n f)"))\
                .then_inc(S(f"w_in{g}"), 16)

        def load_down(sp, c, g):
            sp.dma_start(wd[:, g, :, :], A["w_down"][0].rearrange("(n k p) c -> p n k c", p=P, k=2)
                         [:, bass.ds(c * 2 + g, 1), :, :].rearrange("p n k c -> p (n k) c"))\
                .then_inc(S(f"w_in{2 + g}"), 16)

        def out_tensor(pe):
            def transposes(i):
                r = rows(i)
                pe.wait_ge(S("xh"), NT + i + 1)
                if i >= 1:
                    pe.wait_ge(S("hT"), 2 * NT + 2 * i)
                for half in range(2):
                    for k in range(4):
                        c = (4 * half + k) * P
                        ins = pe.transpose(ps[:, 4 + half, k * P:k * P + r], h2[0:r, i % 2, c:c + P],
                                           ident[0:r, 0:r])
                    ins.then_inc(S("xT"), 1)
            pe.wait_ge(S("params"), 16 * (N_PAR_DMA + 3))
            pe.wait_ge(S("rw_done"), NT)
            pe.wait_ge(S("rw_fin_s"), 4)
            for i in range(NT):
                r = rows(i)
                if i >= 2:
                    pe.wait_ge(S("m_x1"), i - 1)
                for half in range(2):
                    for k in range(KD):
                        ins = pe.matmul(ps[0:r, 2 * (i % 2) + half, :], mixT[:, k, i * P:i * P + r],
                                        w_out[:, k, half * 512:half * 512 + 512], start=(k == 0),
                                        stop=(k == KD - 1))
                ins.then_inc(S("m_o"), 1)
                if i >= 1:
                    transposes(i - 1)
            transposes(NT - 1)

        def out_act(act):
            def rms(col, src, r, want, n):
                s = d_ss[0:r, col:col + 1]
                act.wait_ge(S(want), n)
                act.activation(d_junk[0:r, :], src, ACT.Square, accum_out=s).then_inc(*did("act"))
                act.wait_ge(*so_far("act"))
                act.activation(s, s, ACT.Ln, scale=1.0 / D, bias=eps_col[0:r, :]).then_inc(*did("act"))
                act.wait_ge(*so_far("act"))
                return act.activation(s, s, ACT.Exp, scale=-0.5)
            for i in range(NT):
                r = rows(i)
                rms(2 * i, ps[0:r, 2 * (i % 2):2 * (i % 2) + 2, :].rearrange("p a c -> p (a c)"), r, "m_o",
                    i + 1 if i < NT - 1 else NT).then_inc(S("rs"), 1)
                rms(2 * i + 1, x1[0:r, i, :], r, "m_x1", i + 1).then_inc(S("m_rs2"), 1)

        def out_vector(dve):
            def evac(i):
                r = rows(i)
                for half in range(2):
                    dve.wait_ge(S("xT"), 2 * NT + 2 * i + half + 1)
                    src = ps[:, 4 + half, :].rearrange("p (k t) -> p k t", k=4)[:, :, 0:r]
                    g = gain_ffn[:, 4 * half:4 * half + 4].unsqueeze(2).broadcast_to([P, 4, r])
                    dve.tensor_tensor(h2T[:, 4 * half:4 * half + 4, i * P:i * P + r], src, g,
                                      ALU.mult).then_inc(S("hT"), 1)
            step = chain(dve, "dve")
            for i in range(NT):
                r = rows(i)
                dve.wait_ge(S("rs"), NT + i + 1)
                o = ps[0:r, 2 * (i % 2):2 * (i % 2) + 2, :].rearrange("p a c -> p (a c)")
                step(dve.scalar_tensor_tensor(x1[0:r, i, :], o, d_ss[0:r, 2 * i:2 * i + 1], post_gain[0:r, :],
                                              ALU.mult, ALU.mult))
                dve.wait_ge(S(f"x_in{i % 2}"), 16 * (3 + i // 2 + 1))
                dve.tensor_tensor(x1[0:r, i, :], x1[0:r, i, :], x_again[0:r, i % 2, :], ALU.add)\
                    .then_inc(S("m_x1"), 1)
                if i >= 1:
                    evac(i - 1)
                dve.wait_ge(S("m_rs2"), i + 1)
                dve.tensor_scalar(h2[0:r, i % 2, :], x1[0:r, i, :], d_ss[0:r, 2 * i + 1:2 * i + 2], None,
                                  ALU.mult).then_inc(S("xh"), 1)
            evac(NT - 1)

        NUP = 3 * FT
        NDN = 2 * NT

        def mlp_tensor(pe):
            def chunk(c, first):
                for q in range(NUP):
                    ft, (t0, tw) = q // 3, TG[q % 3]
                    if q % (NUP // 2) == 0:
                        pe.wait_ge(S(f"w_in{2 * q // NUP}"), c * 16 + 16 * (W_LOADS[2 * q // NUP] + 1))
                    if not first or q >= 4:
                        pe.wait_ge(S("up_out"), c * NUP + (q - 3))
                    for k in range(KD):
                        ins = pe.matmul(ps[:, q % 4, 0:tw], wu[:, ft // 2, k, (ft % 2) * P:(ft % 2) * P + P],
                                        h2T[:, k, t0:t0 + tw], start=(k == 0), stop=(k == KD - 1))
                    ins.then_inc(S("up_ps"), 1)
                for q in range(NDN):
                    i, half = q // 2, q % 2
                    r = rows(i)
                    if q == 0:
                        pe.wait_ge(S("up_out"), c * NUP + NUP)
                        pe.wait_ge(S("w_in2"), c * 16 + 16 * (W_LOADS[2] + 1))
                        pe.wait_ge(S("w_in3"), c * 16 + 16 * (W_LOADS[3] + 1))
                    if not first or q >= 3:
                        pe.wait_ge(S("dn_out"), c * NDN + (q - 2))
                    for k in range(FT):
                        ins = pe.matmul(ps[0:r, 4 + q % 3, :], uT[:, k, i * P:i * P + r],
                                        wd[:, k // 2, k % 2, half * 512:half * 512 + 512], start=(k == 0),
                                        stop=(k == FT - 1))
                    ins.then_inc(S("dn_ps"), 1)
            pe.wait_ge(S("hT"), 2 * NT + 2 * NT)
            pe.wait_ge(S("m_x1"), NT)
            chunk(0, True)
            with pe.Fori(1, NCH) as c:
                chunk(c, False)

        def mlp_act(act):
            def chunk(c, first):
                for q in range(NUP):
                    ft, (t0, tw) = q // 3, TG[q % 3]
                    act.wait_ge(S("up_ps"), c * NUP + (q + 1))
                    if not first and q == 0:
                        act.wait_ge(S("dn_ps"), c * NDN)
                    u = uT[:, ft, t0:t0 + tw]
                    act.activation(u, ps[:, q % 4, 0:tw], ACT.Relu).then_inc(S("up_relu"), 1)
                    act.wait_ge(S("up_relu"), c * NUP + (q + 1))
                    act.activation(u, u, ACT.Square).then_inc(S("up_out"), 1)
            chunk(0, True)
            with act.Fori(1, NCH) as c:
                chunk(c, False)
            for i in range(NT):
                r = rows(i)
                s = d_ss[0:r, 2 * i:2 * i + 1]
                act.wait_ge(S("dn_out"), (NCH - 1) * NDN + 2 * i + 2)
                act.activation(d_junk[0:r, :], y_acc[0:r, i, :], ACT.Square, accum_out=s).then_inc(*did("act"))
                act.wait_ge(*so_far("act"))
                act.activation(s, s, ACT.Ln, scale=1.0 / D, bias=eps_col[0:r, :]).then_inc(*did("act"))
                act.wait_ge(*so_far("act"))
                act.activation(s, s, ACT.Exp, scale=-0.5).then_inc(S("y_rs"), 1)

        def mlp_vector(dve):
            def chunk(c, first, last=False):
                for q in range(NDN):
                    i, half = q // 2, q % 2
                    r = rows(i)
                    y = y_acc[0:r, i, half * 512:half * 512 + 512]
                    p = ps[0:r, 4 + q % 3, :]
                    dve.wait_ge(S("dn_ps"), c * NDN + (q + 1))
                    if first:
                        dve.tensor_copy(y, p).then_inc(S("dn_out"), 1)
                    else:
                        if q == 0:
                            dve.wait_ge(S("dn_out"), c * NDN)
                        dve.tensor_tensor(y, y, p, ALU.add).then_inc(S("dn_out"), 1)
            chunk(0, True)
            with dve.Fori(1, NCH) as c:
                chunk(c, False)
            dve.wait_ge(S("params"), 16 * (N_PAR_DMA + 4))
            step = chain(dve, "dve")
            for i in range(NT):
                r = rows(i)
                dve.wait_ge(S("y_rs"), i + 1)
                y = y_acc[0:r, i, :]
                step(dve.scalar_tensor_tensor(y, y, d_ss[0:r, 2 * i:2 * i + 1], post_gain[0:r, :], ALU.mult,
                                              ALU.mult))
                dve.tensor_tensor(y, y, x1[0:r, i, :], ALU.add).then_inc(S("y_ready"), 1)

        def y_out_sync(sp):
            for i in range(NT):
                sp.wait_ge(S("y_ready"), i + 1)
                dst = (O["y_prompt"][0, i * P:(i + 1) * P, :] if i < NT - 1
                       else O["y_sample"].rearrange("b t d -> (b t) d"))
                sp.dma_start(dst, y_acc[0:rows(i), i, :]).then_inc(S("y_out"), 16)
            sp.wait_ge(S("y_out"), 16 * NT)

        @block.sync
        def _(sp):
            norm_in_sync(sp)
            project_sync(sp)
            decode_load_sync(sp)
            la_load_sync(sp)
            mlp_out_sync(sp)
            y_out_sync(sp)

        @block.scalar
        def _(act):
            load_parameters(act)
            norm_in_act(act)
            project_act(act)
            sb_act(act)
            decode_act(act)
            la_prep_act(act)
            la_act(act)
            rw_prep_act(act)
            rw_act(act)
            rws_act(act)
            out_act(act)
            mlp_act(act)

        @block.gpsimd
        def _(pool):
            make_constants(pool)
            caches_out_gpsimd(pool)
            sb_gpsimd(pool)
            la_gpsimd(pool)
            rw_gpsimd(pool)
            pool.wait_ge(S("rw_states_out"), 16 * 8)
            pool.wait_ge(S("states_out"), 16 * 4 * 4)
            pool.wait_ge(S("sk_out"), 32)
            pool.wait_ge(S("sv_out"), 32)

        @block.tensor
        def _(pe):
            norm_in_tensor(pe)
            project_tensor(pe)
            sb_tensor(pe)
            decode_tensor(pe)
            la_prep_tensor(pe)
            la_tensor(pe)
            rw_prep_tensor(pe)
            rw_tensor(pe)
            rws_tensor(pe)
            out_tensor(pe)
            mlp_tensor(pe)

        @block.vector
        def _(dve):
            norm_in_vector(dve)
            project_vector(dve)
            sb_vector(dve)
            decode_vector(dve)
            la_prep_vector(dve)
            la_vector(dve)
            rw_prep_vector(dve)
            rw_vector(dve)
            rws_vector(dve)
            out_vector(dve)
            mlp_vector(dve)


INPUTS = ("x_prompt", "x_sample", "cache_sb_k", "cache_sb_v", "page_table", "state_hgrn", "state_rwkv",
          "state_rwkv_shift", "state_gla", "norm_mix_pre", "norm_mix_post", "norm_ffn_pre", "norm_ffn_post",
          "w_in", "w_out", "w_up", "w_down", "hg_norm", "rw_mu", "rw_w0", "rw_w2", "rw_a0", "rw_a2",
          "rw_g2", "rw_k_k", "rw_k_a", "rw_r_k", "rw_ln_w", "rw_ln_b", "sb_bias", "gla_a2", "gla_a_b", "gla_norm")
OUTPUTS = (("y_prompt", (1, T, D)), ("y_sample", (NB, NS, D)),
           ("sb_k_prompt", (1, 1, T, H, HD)), ("sb_v_prompt", (1, 1, T, H, HD)),
           ("sb_k_sample", (1, NB, NS, H, HD)), ("sb_v_sample", (1, NB, NS, H, HD)),
           ("hgrn_prompt", (1, 1, H, HD, HD)), ("hgrn_sample", (1, NB, H, HD, HD)),
           ("rwkv_prompt", (1, 1, H, HD, HD)), ("rwkv_sample", (1, NB, H, HD, HD)),
           ("rwkv_shift_prompt", (1, 1, 896)), ("rwkv_shift_sample", (1, NB, 896)),
           ("gla_prompt", (1, 1, H, 32, HD)), ("gla_sample", (1, NB, H, 32, HD)))


def kernel(**inputs):
    import numpy as np
    from concourse import bacc
    from concourse.bass_utils import run_bass_kernel_spmd

    nc = bacc.Bacc("TRN2", target_bir_lowering=False, num_devices=1)
    arrays, A, O = {}, {}, {}
    for name in INPUTS:
        a = np.ascontiguousarray(inputs[name])
        arrays[f"in_{name}"] = a
        A[name] = nc.dram_tensor(f"in_{name}", a.shape, mybir.dt.from_np(a.dtype), kind="ExternalInput").ap()
    for name, shape in OUTPUTS:
        O[name] = nc.dram_tensor(f"out_{name}", shape, F32, kind="ExternalOutput").ap()
    build(nc, A, O)
    r = run_bass_kernel_spmd(nc, [arrays], core_ids=[0])
    return tuple(r.results[0][f"out_{name}"] for name, _ in OUTPUTS)
```

```python
import itertools
import math
from contextlib import ExitStack

import concourse.bass as bass
from concourse import mybir

F32 = mybir.dt.float32
F32R = mybir.dt.float32r
BF16 = mybir.dt.bfloat16
U32 = mybir.dt.uint32
I32 = mybir.dt.int32
ALU = mybir.AluOpType
ACT = mybir.ActivationFunctionType
AX = mybir.AxisListType.X

P = 128
D = 1024
T = 1024
NB, NS = 8, 8
SMP = NB * NS
TOK = T + SMP
KD = D // P
NT = T // P + 1
FF = 4 * D
H, HD = 4, 64
GW = H * HD
EPS = 1e-6
RW_GN_EPS = 64e-5
TG = ((0, 512), (512, 512), (T, SMP))
EG = tuple((3 * P * n, min(3 * P, TOK - 3 * P * n)) for n in range(3))
RWT = 7
PADW = 1 + T + NB * (1 + NS)
LEVELS = (64, 32, 16, 8, 4, 2, 1)

COL = {}
_c = 0
for _n, _w in (("hq", 256), ("hf", 256), ("hi", 256), ("hg", 256), ("rr", 256), ("rk", 256), ("rv", 256),
               ("rx", 128), ("sq", 256), ("sk", 256), ("sv", 256), ("gq", 128), ("gk", 128), ("gv", 256),
               ("ga", 16), ("gg", 256)):
    COL[_n] = _c
    _c += _w
IN_COLS = _c

T_GROUPS = (("rr", 256), ("rk", 256), ("rv", 256), ("rx", 128), ("sq", 256), ("sk", 256), ("hq", 256),
            ("hf", 256), ("gq", 128), ("gk", 128), ("ga", 16))
N_GROUPS = ("sk", "sv", "hi", "hg", "gv", "gg")
T_UNITS = [(n, a, min(w, P)) for n, w in T_GROUPS for a in range(max(1, w // P))]
WSLOTS = 4
RSLOTS = 3


def rows(i):
    return P if i < NT - 1 else SMP


def projection_jobs():
    return ([(name, "T", a, tg) for name, a, _ in T_UNITS for tg in range(3)]
            + [(name, "N", i, None) for name in N_GROUPS for i in range(NT)])


def build(nc, A, O):
    JOBS = projection_jobs()
    PBANKS = 6

    ctx = ExitStack()
    with ctx:
        sems = {}

        def S(name):
            if name not in sems:
                sems[name] = ctx.enter_context(nc.semaphore(name))
            return sems[name]

        NWORDS = 53208
        with nc.sbuf_tensor("arena", [P, NWORDS], F32) as arena_tensor:
            arena = arena_tensor
        ps = ctx.enter_context(nc.psum_tensor("ps", [P, 8, 512], F32))
        used = [0]

        def at(off, *dims):
            n = 1
            for d in dims:
                n *= d
            v = arena[:, off:off + n]
            assert off + n <= NWORDS, (off, n)
            if len(dims) == 1:
                return v
            names = "abcd"[:len(dims)]
            return v.rearrange("p (" + " ".join(names) + ") -> p " + " ".join(names),
                               **{names[i]: dims[i] for i in range(1, len(dims))})

        def take(*dims):
            n = 1
            for d in dims:
                n *= d
            v = at(used[0], *dims)
            used[0] += n
            return v

        gain_pre = take(KD)
        gain_ffn = take(KD)
        eps_col = take(1)
        one_col = take(1)
        ssq = take(NT)
        rs = take(NT)
        MIXER_CONSTS = used[0]
        ident = take(P)
        headones = take(P)
        up_mask = take(7, P)
        low_eq = take(7, P)
        upper = take(P)
        upper_eq = take(P)
        upper8 = take(P)
        upper8_eq = take(P)
        neg_tri = take(P)
        neg_ones = take(P)
        neg_big = take(P)
        neg_big8 = take(SMP)
        seqmask = take(NB)
        page_ids = take(64).bitcast(I32)
        par = take(40)
        sb_bias = take(H)
        w2all = take(GW)
        gla_a2 = take(P)
        CONST_END = used[0]

        mixT = at(used[0], KD, TOK)
        used[0] += KD * TOK
        PR = used[0]
        sqT = take(2, TOK)
        skT = take(2, TOK)
        hqT = take(2, TOK)
        hfT = take(2, TOK)
        rwP = take(RWT, PADW)
        gqT = take(TOK)
        gkT = take(TOK)
        gaT = take(TOK)
        NR = used[0]
        hi_n = take(NT, GW)
        hg_n = take(NT, GW)
        sv_n = take(NT, GW)
        gv_n = take(NT, GW)
        gg_n = take(NT, GW)
        WR = used[0]
        sk_stage = gg_n
        xin = at(PR, 3, D)
        xh = at(PR + 3 * D, 2, D)
        sq_junk = at(PR + 5 * D, D)
        shift_in = at(PR + 6 * D, RWT * P)
        H_TMP = PR + 6 * D + RWT * P
        LO = (NR + 7) // 8 * 8
        with ExitStack() as place:
            place.enter_context(nc.sbuf_tensor("below_h_hi", [P, CONST_END], F32))
            h_hi = place.enter_context(nc.sbuf_tensor("h_hi", [P, KD, TOK], F32R))
            place.enter_context(nc.sbuf_tensor("below_h_tmp", [P, H_TMP - PR], F32))
            h_tmp = place.enter_context(nc.sbuf_tensor("h_tmp", [P, 2, 4, P], F32))
            place.enter_context(nc.sbuf_tensor("below_h_lo", [P, LO - H_TMP - 8 * P], F32))
            h_lo = place.enter_context(nc.sbuf_tensor("h_lo", [P, KD, TOK], F32R))
            w1 = place.enter_context(nc.sbuf_tensor("w1_split", [P, 2, 2, KD * P], F32R))
            w1_raw = place.enter_context(nc.sbuf_tensor("w1_raw", [P, RSLOTS, KD * P], F32))
        with ExitStack() as place:
            place.enter_context(nc.sbuf_tensor("below_hT", [P, CONST_END], F32))
            hT = place.enter_context(nc.sbuf_tensor("hT_whole", [P, KD, TOK], F32))
            between = (WR + 7) // 8 * 8 - CONST_END - KD * TOK
            place.enter_context(nc.sbuf_tensor("below_w_ring", [P, between], F32))
            wring = place.enter_context(nc.sbuf_tensor("w_ring", [P, WSLOTS, KD, 256], F32))
        nat_dst = {"hi": hi_n, "hg": hg_n, "sv": sv_n, "gv": gv_n, "gg": gg_n, "sk": sk_stage}

        PAR = {}
        PAR_SRC = (("mu", "rw_mu", 7), ("w0", "rw_w0", 2), ("a0", "rw_a0", 2), ("k_k", "rw_k_k", 2),
                   ("k_a", "rw_k_a", 2), ("r_k", "rw_r_k", 2), ("ln_w", "rw_ln_w", 2), ("ln_b", "rw_ln_b", 2),
                   ("gla_ab", "gla_a_b", 1))
        o = 0
        for n, src, w in PAR_SRC:
            PAR[n] = par[:, o:o + w]
            o += w
        PAR["hg_norm"] = par[:, o:o + 1]
        PAR["gla_norm"] = par[:, o + 1:o + 2]
        PAR["one_k_a"] = par[:, o + 2:o + 4]

        own = {}

        def did(engine):
            own[engine] = own.get(engine, 0) + 1
            return S(engine + "_own"), 1

        def so_far(engine):
            return S(engine + "_own"), own[engine]

        def chain(eng, engine):
            def step(ins):
                ins.then_inc(*did(engine))
                eng.wait_ge(*so_far(engine))
            return step

        def x_rows(i):
            return (A["x_prompt"][0, i * P:(i + 1) * P, :] if i < NT - 1
                    else A["x_sample"].rearrange("b t d -> (b t) d"))

        block = ctx.enter_context(nc.Block())

        N_PAR_DMA = len(PAR_SRC) + 4 + 1 + 3 + 1 + 1

        def parameter_loads():
            for dst, name in ((gain_pre, "norm_mix_pre"), (gain_ffn, "norm_ffn_pre")):
                yield dst, A[name].rearrange("o (k p) -> p (o k)", p=P)
            yield shift_in[0:NB, :], A["state_rwkv_shift"][0]
            for n, src, w in PAR_SRC:
                s = A[src].rearrange("o h d -> o (h d)") if src == "rw_r_k" else A[src]
                yield PAR[n], s.rearrange("o (k p) -> p (o k)", p=P)
            for j in range(2):
                yield PAR["hg_norm"][64 * j:64 * j + 64, :], A["hg_norm"].rearrange("o p -> p o")
                yield PAR["gla_norm"][64 * j:64 * j + 64, :], A["gla_norm"].rearrange("o p -> p o")
            yield sb_bias, A["sb_bias"][0].partition_broadcast(P)
            yield w2all[0:32, :], A["rw_w2"][0]
            yield w2all[32:64, :], A["rw_a2"][0]
            yield w2all[64:128, :], A["rw_g2"][0]
            yield gla_a2[0:16, :], A["gla_a2"][0]

        def load_parameters(act, loads, many):
            for dst, src in itertools.islice(loads, many):
                act.dma_start(dst, src, allow_slow_non_contiguous=True)\
                    .then_inc(S("gains" if dst is gain_pre or dst is gain_ffn else "params"), 16)

        def make_identity(pool):
            step = chain(pool, "pool")
            step(pool.memset(ident, 0.0))
            step(pool.affine_select(out=ident, in_=ident, compare_op=ALU.not_equal, fill=1.0, base=0,
                                    pattern=[[-1, P]], channel_multiplier=1))
            step(pool.memset(one_col, 1.0))
            pool.memset(eps_col, EPS).then_inc(S("ident"), 1)

        def make_constants(pool):
            step = chain(pool, "pool")
            step(pool.memset(headones, 0.0))
            step(pool.memset(headones[0:64, 0:64], 1.0))
            step(pool.memset(headones[64:128, 64:128], 1.0))
            step(pool.memset(up_mask, 0.0))
            for lv, m in enumerate(LEVELS):
                v = up_mask[:, lv, :].rearrange("p (j h i) -> p j h i", h=2, i=m)[:, :, 1, :]
                step(pool.memset(v, 1.0))
                nb = P // (2 * m)
                step(pool.affine_select(out=v, in_=v, compare_op=ALU.is_ge, fill=0.0, base=0,
                                        pattern=[[-2 * m, nb], [0, m]], channel_multiplier=1))
                step(pool.affine_select(out=v, in_=v, compare_op=ALU.is_ge, fill=0.0, base=m - 1,
                                        pattern=[[2 * m, nb], [0, m]], channel_multiplier=-1))
            step(pool.memset(low_eq, 0.0))
            for lv, m in enumerate(LEVELS):
                v = low_eq[:, lv, :].rearrange("p (j h i) -> p j h i", h=2, i=m)[:, :, 0, :]
                step(pool.memset(v, 1.0))
                nb = P // (2 * m)
                step(pool.affine_select(out=v, in_=v, compare_op=ALU.is_ge, fill=0.0, base=-m,
                                        pattern=[[-2 * m, nb], [0, m]], channel_multiplier=1))
                step(pool.affine_select(out=v, in_=v, compare_op=ALU.is_ge, fill=0.0, base=2 * m - 1,
                                        pattern=[[2 * m, nb], [0, m]], channel_multiplier=-1))
                step(pool.tensor_tensor(low_eq[:, lv, :], low_eq[:, lv, :], ident, ALU.add))
            step(pool.memset(upper, 1.0))
            step(pool.affine_select(out=upper, in_=upper, compare_op=ALU.is_ge, fill=0.0, base=-1,
                                    pattern=[[1, P]], channel_multiplier=-1))
            step(pool.memset(upper_eq, 1.0))
            step(pool.affine_select(out=upper_eq, in_=upper_eq, compare_op=ALU.is_ge, fill=0.0, base=0,
                                    pattern=[[1, P]], channel_multiplier=-1))
            step(pool.memset(neg_tri, -1.0))
            step(pool.affine_select(out=neg_tri, in_=neg_tri, compare_op=ALU.is_ge, fill=0.0, base=0,
                                    pattern=[[-1, P]], channel_multiplier=1))
            step(pool.memset(neg_ones, -1.0))
            step(pool.memset(neg_big, 0.0))
            step(pool.affine_select(out=neg_big, in_=neg_big, compare_op=ALU.is_ge, fill=-3.0e4, base=-1,
                                    pattern=[[1, P]], channel_multiplier=-1))
            step(pool.memset(seqmask, 1.0))
            step(pool.affine_select(out=seqmask, in_=seqmask, compare_op=ALU.is_ge, fill=0.0, base=0,
                                    pattern=[[-NS, NB]], channel_multiplier=1))
            step(pool.affine_select(out=seqmask, in_=seqmask, compare_op=ALU.is_ge, fill=0.0, base=NS - 1,
                                    pattern=[[NS, NB]], channel_multiplier=-1))
            step(pool.tensor_tensor(upper8, up_mask[:, 4, :], up_mask[:, 5, :], ALU.add))
            step(pool.tensor_tensor(upper8, upper8, up_mask[:, 6, :], ALU.add))
            step(pool.tensor_tensor(upper8_eq, upper8, ident, ALU.add))
            pool.tensor_scalar(neg_big8, upper8[:, 0:SMP], 3.0e4, -3.0e4, ALU.mult, ALU.add)\
                .then_inc(S("consts"), 1)

        def norm_in_sync(sp):
            for i in range(NT):
                if i >= 3:
                    sp.wait_ge(S("xh"), i - 2)
                sp.dma_start(xin[0:rows(i), i % 3, :], x_rows(i)).then_inc(S(f"x_in{i % 3}"), 16)

        def norm_in_act(act):
            loads = parameter_loads()
            load_parameters(act, loads, 2)
            act.preload_act_table_set("natural_log_exp_and_others")
            act.wait_ge(S("ident"), 1)
            for i in range(NT):
                r = rows(i)
                act.wait_ge(S(f"x_in{i % 3}"), 16 * (i // 3 + 1))
                act.activation(sq_junk[0:r, :], xin[0:r, i % 3, :], ACT.Square,
                               accum_out=ssq[0:r, i:i + 1]).then_inc(*did("act"))
                act.wait_ge(*so_far("act"))
                act.activation(ssq[0:r, i:i + 1], ssq[0:r, i:i + 1], ACT.Ln, scale=1.0 / D,
                               bias=eps_col[0:r, :]).then_inc(*did("act"))
                act.wait_ge(*so_far("act"))
                act.activation(rs[0:r, i:i + 1], ssq[0:r, i:i + 1], ACT.Exp, scale=-0.5).then_inc(S("rs"), 1)
                load_parameters(act, loads, -(-N_PAR_DMA // NT))

        def norm_in_vector(dve):
            def evac(i):
                r = rows(i)
                for half in range(2):
                    n = 2 * i + half
                    dve.wait_ge(S("xT"), n + 1)
                    src = ps[:, n % 4, :].rearrange("p (k t) -> p k t", k=4)[:, :, 0:r]
                    g = gain_pre[:, 4 * half:4 * half + 4].unsqueeze(2).broadcast_to([P, 4, r])
                    if n >= 2:
                        dve.wait_ge(S("hT"), n - 1)
                    hi = h_hi[:, 4 * half:4 * half + 4, i * P:i * P + r]
                    tmp = h_tmp[:, half, :, 0:r]
                    dve.tensor_tensor(tmp, src, g, ALU.mult).then_inc(S("h_tmp"), 1)
                    dve.wait_ge(S("h_tmp"), n + 1)
                    dve.tensor_copy(hi, tmp).then_inc(S("h_hi"), 1)
            for i in range(NT):
                r = rows(i)
                dve.wait_ge(S("rs"), i + 1)
                if i >= 2:
                    dve.wait_ge(S("xT"), 2 * (i - 1))
                dve.tensor_scalar(xh[0:r, i % 2, :], xin[0:r, i % 3, :], rs[0:r, i:i + 1], None,
                                  ALU.mult).then_inc(S("xh"), 1)
                if i == 0:
                    dve.wait_ge(S("gains"), 32)
                if i >= 1:
                    evac(i - 1)
            evac(NT - 1)

        def norm_in_gpsimd(pool):
            for n in range(2 * NT):
                i, half = n // 2, n % 2
                hi, lo = (t[:, 4 * half:4 * half + 4, i * P:i * P + rows(i)] for t in (h_hi, h_lo))
                pool.wait_ge(S("h_hi"), n + 1)
                pool.tensor_tensor(lo, h_tmp[:, half, :, 0:rows(i)], hi.bitcast(F32), ALU.subtract)\
                    .then_inc(S("hT"), 1)

        def norm_in_tensor(pe):
            pe.wait_ge(S("ident"), 1)
            for i in range(NT):
                r = rows(i)
                pe.wait_ge(S("xh"), i + 1)
                for half in range(2):
                    n = 2 * i + half
                    if n >= 4:
                        pe.wait_ge(S("h_tmp"), n - 3)
                    for k in range(4):
                        c = (4 * half + k) * P
                        ins = pe.transpose(ps[:, n % 4, k * P:k * P + r], xh[0:r, i % 2, c:c + P],
                                           ident[0:r, 0:r])
                    ins.then_inc(S("xT"), 1)
            pe.wait_ge(S("params"), 16 * N_PAR_DMA)
            for ct in range(RWT):
                ins = pe.transpose(ps[:, 6, ct * NB:(ct + 1) * NB], shift_in[0:NB, ct * P:(ct + 1) * P],
                                   ident[0:NB, 0:NB])
            ins.then_inc(S("shiftT"), 1)

        NTJ = 3 * len(T_UNITS)

        def three(pe, out, w_hi, w_lo, x_hi, x_lo, first, last):
            pe.matmul(out, w_hi, x_hi, start=first, stop=False)
            pe.matmul(out, w_hi, x_lo, start=False, stop=False)
            return pe.matmul(out, w_lo, x_hi, start=False, stop=last)

        def n_slot(g):
            return WSLOTS - 1 - g % WSLOTS

        def t_loads(slot):
            return len(range(slot, len(T_UNITS), RSLOTS)) if slot < RSLOTS else 0

        def project_sync(sp):
            w_in = A["w_in"][0].rearrange("(k p) c -> p k c", p=P)
            for u, (name, a, cw) in enumerate(T_UNITS):
                if u >= RSLOTS:
                    sp.wait_ge(S("w1_split"), u - RSLOTS + 1)
                c0 = COL[name] + a * P
                sp.dma_start(w1_raw[:, u % RSLOTS, 0:KD * cw].rearrange("p (k c) -> p k c", k=KD),
                             w_in[:, :, c0:c0 + cw]).then_inc(S(f"w_in{u % RSLOTS}"), 16)
            for g, name in enumerate(N_GROUPS):
                if g == 1:
                    sp.wait_ge(S("w1_split"), len(T_UNITS))
                if g == 2:
                    sp.wait_ge(S("proj_ps"), NTJ)
                if g >= WSLOTS:
                    sp.wait_ge(S("proj_ps"), NTJ + NT * (g - WSLOTS + 1))
                sp.dma_start(wring[:, n_slot(g), :, :], w_in[:, :, COL[name]:COL[name] + 256])\
                    .then_inc(S(f"w_in{n_slot(g)}"), 16)

        def project_tensor(pe):
            pe.wait_ge(S("hT"), 2 * NT)
            n = 0
            for u, (name, a, cw) in enumerate(T_UNITS):
                pe.wait_ge(S("w1_split"), u + 1)
                w_hi, w_lo = (w1[:, u % 2, y, 0:KD * cw].rearrange("p (k c) -> p k c", k=KD) for y in range(2))
                for t0, tw in EG:
                    if n >= PBANKS:
                        pe.wait_ge(S("proj_out"), n - PBANKS + 1)
                    for k in range(KD):
                        ins = three(pe, ps[0:cw, n % PBANKS, 0:tw], w_hi[:, k, :], w_lo[:, k, :],
                                    h_hi[:, k, t0:t0 + tw], h_lo[:, k, t0:t0 + tw], k == 0, k == KD - 1)
                    ins.then_inc(S("proj_ps"), 1)
                    n += 1
            for g, name in enumerate(N_GROUPS):
                slot = n_slot(g)
                pe.wait_ge(S(f"w_in{slot}"), 16 * (t_loads(slot) + g // WSLOTS + 1))
                for i in range(NT):
                    r = rows(i)
                    if g == 0:
                        pe.wait_ge(S("h_whole"), i + 1)
                    pe.wait_ge(S("proj_out"), n - PBANKS + 1)
                    for k in range(KD):
                        ins = pe.matmul(ps[0:r, n % PBANKS, 0:256], hT[:, k, i * P:i * P + r],
                                        wring[:, slot, k, :], start=(k == 0), stop=(k == KD - 1))
                    ins.then_inc(S("proj_ps"), 1)
                    n += 1

        def project_act(act):
            act.wait_ge(S("hT"), 2 * NT)
            act.wait_ge(S("shiftT"), 1)
            for n, (name, kind, a, tg) in enumerate(JOBS):
                act.wait_ge(S("proj_ps"), n + 1)
                bank = ps[:, n % PBANKS, :]
                if kind == "N":
                    r = rows(a)
                    if name == "gg" and a == 0:
                        act.wait_ge(S("sk_out"), 32)
                    fn = ACT.Silu if name in ("hg", "gg") else ACT.Copy
                    if (name, a) == (N_GROUPS[0], 0):
                        act.wait_ge(S("h_whole"), NT)
                    act.activation(nat_dst[name][0:r, a, :], bank[0:r, 0:256], fn).then_inc(S("proj_out"), 1)
                    continue
                t0, tw = EG[tg]
                cw = 16 if name == "ga" else P
                src = bank[0:cw, 0:tw]
                if name in ("rr", "rk", "rv", "rx"):
                    ct = {"rr": 0, "rk": 2, "rv": 4, "rx": 6}[name] + a
                    dst = rwP[:, ct, 1 + t0:1 + t0 + tw]
                    if t0 + tw > T:
                        act.activation(rwP[:, ct, 1 + T:].rearrange("p (b t) -> p b t", b=NB)[:, :, 1:],
                                       bank[:, T - t0:tw].rearrange("p (b t) -> p b t", b=NB), ACT.Copy)\
                            .then_inc(*did("act"))
                        dst, src = dst[:, 0:T - t0], src[:, 0:T - t0]
                elif name in ("gq", "gk"):
                    dst = (gqT if name == "gq" else gkT)[:, t0:t0 + tw]
                elif name == "ga":
                    dst = gaT[0:cw, t0:t0 + tw]
                else:
                    dst = {"sq": sqT, "sk": skT, "hq": hqT, "hf": hfT}[name][:, a, t0:t0 + tw]
                fn = ACT.Silu if name == "hq" else ACT.Copy
                scale = HD ** -0.5 if name == "sq" else 32 ** -0.5 if name == "gq" else 1.0
                act.activation(dst, src, fn, scale=scale).then_inc(S("proj_out"), 1)

        def project_vector(dve):
            dve.memset(rwP[:, :, 0:1], 0.0).then_inc(*did("dve"))
            dve.wait_ge(S("shiftT"), 1)
            dve.tensor_copy(rwP[:, :, 1 + T:].rearrange("p c (b t) -> p c b t", b=NB)[:, :, :, 0],
                            ps[:, 6, 0:RWT * NB].rearrange("p (c b) -> p c b", c=RWT)).then_inc(*did("dve"))
            for u, (name, a, cw) in enumerate(T_UNITS):
                raw = w1_raw[:, u % RSLOTS, 0:KD * cw]
                w_hi, w_lo = (w1[:, u % 2, y, 0:KD * cw] for y in range(2))
                dve.wait_ge(S(f"w_in{u % RSLOTS}"), 16 * (u // RSLOTS + 1))
                if u >= 2:
                    dve.wait_ge(S("proj_ps"), 3 * (u - 1))
                dve.tensor_copy(w_hi, raw).then_inc(S("w1_hi"), 1)
                dve.wait_ge(S("w1_hi"), u + 1)
                dve.tensor_tensor(w_lo, raw, w_hi.bitcast(F32), ALU.subtract).then_inc(S("w1_split"), 1)
            dve.wait_ge(S("proj_ps"), NTJ)
            for i in range(NT):
                cols = slice(i * P, i * P + rows(i))
                dve.tensor_tensor(hT[:, :, cols], h_hi[:, :, cols].bitcast(F32), h_lo[:, :, cols].bitcast(F32),
                                  ALU.add).then_inc(S("h_whole"), 1)

        def job_of(name, kind):
            return 1 + max(n for n, j in enumerate(JOBS) if j[:2] == (name, kind))

        def caches_out_gpsimd(pool):
            for name, first in (("sk", sk_stage), ("sv", sv_n)):
                pool.wait_ge(S("proj_out"), job_of(name, "N"))
                kv = "k" if name == "sk" else "v"
                done = S("sk_out") if name == "sk" else S("sv_out")
                pool.dma_start(O[f"sb_{kv}_prompt"][0, 0].rearrange("(i p) h d -> p i (h d)", p=P),
                               first[:, 0:NT - 1, :]).then_inc(done, 16)
                pool.dma_start(O[f"sb_{kv}_sample"][0].rearrange("b t h d -> (b t) (h d)"),
                               first[0:SMP, NT - 1, :]).then_inc(done, 16)


        SB_BLOCKS = [(h, G, kt) for h in range(H) for G in range(2) for kt in range(4 * G + 3, -1, -1)]
        SBN = len(SB_BLOCKS)
        SB_DIAG = sum(b[2] >= 4 * b[1] for b in SB_BLOCKS)
        sb_zc = at(WR, 3, 512)
        sb_sp = at(WR + 1536, 3, 512)
        sb_w = at(WR + 3072, 3, 512)
        sb_sum = at(WR + 4608, 2, 512)

        def sb_geometry(n):
            h, G, kt = SB_BLOCKS[n]
            base = 64 * (h % 2)
            q0 = max(kt * P, 512 * G)
            return h, G, kt, slice(base, base + 64), q0, 512 * (G + 1) - q0, q0 - 512 * G, 2 * h + G

        def sb_tensor(pe):
            pe.wait_ge(S("proj_out"), len(JOBS))
            pe.wait_ge(S("consts"), 1)
            NBLK = len(SB_BLOCKS)

            def scores(n):
                h, G, kt, rws, q0, w, c0, hg = sb_geometry(n)
                if n >= 3:
                    pe.wait_ge(S("sb_sp"), n - 2)
                pe.matmul(ps[:, n % 3, 0:w], skT[rws, h // 2, kt * P:kt * P + P], sqT[rws, h // 2, q0:q0 + w],
                          start=True, stop=True).then_inc(S("sb_z"), 1)

            def exponents(n):
                h, G, kt, rws, q0, w, c0, hg = sb_geometry(n)
                bank = ps[:, 3 + n % 2, 0:w]
                if n >= 2:
                    pe.wait_ge(S("sb_w"), n - 1)
                pe.matmul(bank, skT[rws, h // 2, kt * P:kt * P + P], sqT[rws, h // 2, q0:q0 + w],
                          start=True, stop=False, skip_group_check=True)
                if kt >= 4 * G:
                    pe.matmul(bank[:, 0:P], ident, neg_big, start=False, stop=False, skip_group_check=True)
                    pe.wait_ge(S("sb_spm"), sum(b[2] >= 4 * b[1] for b in SB_BLOCKS[:n + 1]))
                pe.wait_ge(S("sb_sp"), n + 1)
                if kt < 4 * G + 3:
                    pe.wait_ge(S("sb_sum"), n)
                    pe.matmul(bank, neg_ones, sb_sum[:, (n - 1) % 2, c0:512], start=False, stop=False,
                              skip_group_check=True)
                pe.matmul(bank, neg_tri, sb_sp[:, n % 3, 0:w], start=False, stop=True,
                          skip_group_check=True).then_inc(S("sb_x"), 1)

            def outputs(n):
                h, G, kt, rws, q0, w, c0, hg = sb_geometry(n)
                pe.wait_ge(S("sb_w"), n + 1)
                if kt == 4 * G + 3 and hg >= 2:
                    pe.wait_ge(S("sb_o"), hg - 1)
                pe.matmul(ps[rws, 5 + hg % 2, c0:512], sv_n[:, kt, h * HD:(h + 1) * HD], sb_w[:, n % 3, 0:w],
                          start=(kt == 4 * G + 3), stop=(kt == 0), skip_group_check=True)\
                    .then_inc(S("sb_pv"), 1)

            scores(0)
            scores(1)
            for n in range(NBLK):
                if n + 2 < NBLK:
                    scores(n + 2)
                exponents(n)
                if n >= 1:
                    outputs(n - 1)
            outputs(NBLK - 1)

        def sb_vector(dve):
            diag = 0
            dve.wait_ge(S("params"), 16 * N_PAR_DMA)
            for n in range(len(SB_BLOCKS)):
                h, G, kt, rws, q0, w, c0, hg = sb_geometry(n)
                dve.wait_ge(S("sb_z"), n + 1)
                dve.tensor_scalar(sb_zc[:, n % 3, 0:w], ps[:, n % 3, 0:w], sb_bias[:, h:h + 1], 40.0,
                                  ALU.add, ALU.min).then_inc(S("sb_zc"), 1)
                if n >= 1:
                    diag = softplus(dve, n - 1, diag)
            softplus(dve, len(SB_BLOCKS) - 1, diag)

        def softplus(dve, n, diag):
            h, G, kt, rws, q0, w, c0, hg = sb_geometry(n)
            dve.wait_ge(S("sb_l"), n + 1)
            if n >= 3:
                dve.wait_ge(S("sb_x"), n - 2)
                dve.wait_ge(S("sb_sum"), n - 2)
            dve.scalar_tensor_tensor(sb_sp[:, n % 3, 0:w], ps[:, n % 3, 0:w], sb_bias[:, h:h + 1],
                                     sb_zc[:, n % 3, 0:w], ALU.add, ALU.max).then_inc(S("sb_sp"), 1)
            if kt >= 4 * G:
                diag += 1
                dve.wait_ge(S("sb_sp"), n + 1)
                dve.tensor_tensor(sb_sp[:, n % 3, 0:P], sb_sp[:, n % 3, 0:P], upper, ALU.mult)\
                    .then_inc(S("sb_spm"), 1)
            return diag

        def sb_act(act):
            act.preload_act_table_set("natural_log_exp_and_others")

            def weights(n):
                h, G, kt, rws, q0, w, c0, hg = sb_geometry(n)
                act.wait_ge(S("sb_x"), n + 1)
                if n >= 3:
                    act.wait_ge(S("sb_pv"), n - 2)
                act.activation(sb_w[:, n % 3, 0:w], ps[:, 3 + n % 2, 0:w], ACT.Exp,
                               bias=sb_bias[:, h:h + 1]).then_inc(S("sb_w"), 1)
                if kt == 0:
                    act.wait_ge(S("sb_pv"), n + 1)
                    act.activation(mixT[rws, 4 + h // 2, 512 * G:512 * G + 512], ps[rws, 5 + hg % 2, :],
                                   ACT.Copy).then_inc(S("sb_o"), 1)
            for n in range(len(SB_BLOCKS)):
                w = sb_geometry(n)[5]
                zc = sb_zc[:, n % 3, 0:w]
                act.wait_ge(S("sb_zc"), n + 1)
                act.activation(zc, zc, ACT.Exp).then_inc(*did("act"))
                act.wait_ge(*so_far("act"))
                act.activation(zc, zc, ACT.Ln, bias=one_col).then_inc(S("sb_l"), 1)
                if n >= 1:
                    weights(n - 1)
            weights(len(SB_BLOCKS) - 1)

        def sb_gpsimd(pool):
            diag = 0
            for n in range(len(SB_BLOCKS)):
                h, G, kt, rws, q0, w, c0, hg = sb_geometry(n)
                if kt == 4 * G + 3:
                    if n >= 1:
                        pool.wait_ge(S("sb_x"), n)
                        pool.wait_ge(S("sb_sum"), n)
                    pool.wait_ge(S("proj_out"), len(JOBS))
                    pool.memset(sb_sum, 0.0).then_inc(*did("pool"))
                    pool.wait_ge(*so_far("pool"))
                pool.wait_ge(S("sb_sp"), n + 1)
                if kt >= 4 * G:
                    diag += 1
                    pool.wait_ge(S("sb_spm"), diag)
                if n >= 1:
                    pool.wait_ge(S("sb_x"), n)
                    pool.wait_ge(S("sb_sum"), n)
                pool.tensor_tensor(sb_sum[:, n % 2, c0:512], sb_sum[:, (n - 1) % 2, c0:512],
                                   sb_sp[:, n % 3, 0:w], ALU.add).then_inc(S("sb_sum"), 1)

        QC = H * SMP
        NPG = 8
        v_page = at(WR, 2, NB, GW)
        kT_page = at(WR + 4096, NB, 2, P)
        k_half = at(WR + 6144, 2, 4, GW)
        dsb = [mixT[:, 2 + i // 4, 256 * (i % 4):256 * (i % 4) + 256] for i in range(8)]
        q_diag = dsb[0].rearrange("p (a c t) -> p a c t", a=2, c=2)
        d_z, d_l, d_w = dsb[1], dsb[2], dsb[3]
        d_sp, d_sum = (dsb[4], dsb[5]), (dsb[6], dsb[7])

        def decode_rows(j):
            return SMP if j == 0 else P

        def page_rows(eng, name, b, j):
            n = b * NPG + NPG - j
            page = eng.value_load(page_ids[0:1, n:n + 1], min_val=0, max_val=A[name].shape[1] - 1)
            return A[name][0][bass.ds(page, 1)].rearrange("n t h d -> t (n h d)")

        def decode_load_sync(sp):
            sp.dma_start(page_ids[0:1, :], A["page_table"].rearrange("(o b) n -> o (b n)", o=1))\
                .then_inc(S("page_ids"), 16)
            sp.wait_ge(S("page_ids"), 16)
            sp.wait_ge(S("proj_ps"), len(JOBS))
            for j in range(1, NPG + 1):
                for b in range(NB):
                    half = 2 * (j - 1) + b // 4
                    if b % 4 == 0 and half >= 2:
                        sp.wait_ge(S("d_kt"), 2 * (half - 1))
                    sp.dma_start(k_half[:, half % 2, b % 4, :], page_rows(sp, "cache_sb_k", b, j))\
                        .then_inc(S(f"d_k{half % 2}"), 16)

        def decode_load_gpsimd(pool):
            pool.wait_ge(S("page_ids"), 16)
            pool.wait_ge(S("sb_x"), SBN)
            pool.wait_ge(S("sb_pv"), SBN)
            pool.wait_ge(S("sb_sum"), SBN)
            for j in range(1, NPG + 1):
                if j >= 3:
                    pool.wait_ge(S("sb_pv"), SBN + j - 1)
                for b in range(NB):
                    pool.dma_start(v_page[:, j % 2, b, :], page_rows(pool, "cache_sb_v", b, j))\
                        .then_inc(S(f"d_v{j % 2}"), 16)

        def decode_tensor(pe):
            def transposes(j):
                for g in range(4):
                    half = 2 * (j - 1) + g // 2
                    n = 4 * (j - 1) + g
                    if g % 2 == 0:
                        pe.wait_ge(S(f"d_k{half % 2}"), 64 * (half // 2 + 1))
                    if n >= 2:
                        pe.wait_ge(S("d_kT"), n - 1)
                    for i in range(4):
                        b, pr = 2 * g + i // 2, i % 2
                        ins = pe.transpose(ps[:, n % 2, i * P:(i + 1) * P],
                                           k_half[:, half % 2, b % 4, pr * P:(pr + 1) * P], ident)
                    ins.then_inc(S("d_kt"), 1)

            def scores(j):
                bank = ps[:, 2, 0:QC]
                if j >= 1:
                    pe.wait_ge(S("d_z"), j)
                if j == 0:
                    pe.wait_ge(S("d_q"), 4)
                    for pr in range(2):
                        ins = pe.matmul(bank[0:SMP, pr * P:(pr + 1) * P], skT[:, pr, T:TOK],
                                        q_diag[:, pr, :, :], start=(pr == 0), stop=True, skip_group_check=True)
                else:
                    pe.wait_ge(S("d_kT"), 4 * j)
                    out = bank.rearrange("p (a c t) -> p a c t", a=2, c=2)
                    for b in range(NB):
                        for pr in range(2):
                            cols = slice(b * NS, (b + 1) * NS)
                            ins = pe.matmul(out[:, pr, :, cols], kT_page[:, b, pr, :], q_diag[:, pr, :, cols],
                                            start=(b == 0 and pr == 0), stop=True, skip_group_check=True)
                ins.then_inc(S("sb_z"), 1)

            def exponents(j):
                r = decode_rows(j)
                bank = ps[0:r, 3, 0:QC]
                pe.wait_ge(S("d_z"), j + 1)
                if j >= 1:
                    pe.wait_ge(S("sb_w"), SBN + j)
                pe.matmul(bank, ident[0:r, 0:r], d_z[0:r, :], start=True, stop=False, skip_group_check=True)
                if j == 0:
                    for h in range(H):
                        pe.matmul(bank[:, h * SMP:(h + 1) * SMP], ident[0:r, 0:r], neg_big8[0:r, :],
                                  start=False, stop=False, skip_group_check=True)
                    pe.wait_ge(S("sb_spm"), SB_DIAG + 1)
                else:
                    pe.wait_ge(S("d_sum"), j)
                    pe.matmul(bank, neg_ones, d_sum[(j - 1) % 2], start=False, stop=False, skip_group_check=True)
                pe.wait_ge(S("sb_sp"), SBN + j + 1)
                pe.matmul(bank, neg_tri[0:r, 0:r], d_sp[j % 2][0:r, :], start=False, stop=True,
                          skip_group_check=True).then_inc(S("sb_x"), 1)

            def outputs(j):
                pe.wait_ge(S("sb_w"), SBN + j + 1)
                out = ps[:, 4, 0:QC].rearrange("p (a c t) -> p a c t", a=2, c=2)
                w = d_w.rearrange("p (a c t) -> p a c t", a=2, c=2)
                if j == 0:
                    for pr in range(2):
                        ins = pe.matmul(out[:, pr, :, :], sv_n[0:SMP, NT - 1, pr * P:(pr + 1) * P],
                                        w[0:SMP, pr, :, :], start=(pr == 0), stop=False, skip_group_check=True)
                else:
                    pe.wait_ge(S(f"d_v{j % 2}"), 128 * ((j + 1) // 2))
                    for b in range(NB):
                        for pr in range(2):
                            cols = slice(b * NS, (b + 1) * NS)
                            ins = pe.matmul(out[:, pr, :, cols], v_page[:, j % 2, b, pr * P:(pr + 1) * P],
                                            w[:, pr, :, cols], start=False, stop=(j == NPG), skip_group_check=True)
                ins.then_inc(S("sb_pv"), 1)

            scores(0)
            la_gate_logits_tensor(pe)
            transposes(1)
            for j in range(NPG + 1):
                exponents(j)
                if j < NPG:
                    scores(j + 1)
                    if j + 1 < NPG:
                        transposes(j + 2)
                outputs(j)

        def decode_vector(dve):
            dve.wait_ge(S("sb_pv"), len(SB_BLOCKS))
            dve.memset(dsb[0], 0.0).then_inc(S("d_q"), 1)
            dve.memset(d_sum[1], 0.0).then_inc(S("d_q"), 1)
            dve.wait_ge(S("d_q"), 2)
            for c in range(2):
                rws = slice(64 * c, 64 * c + 64)
                dve.tensor_copy(q_diag[rws, :, c, :], sqT[rws, :, T:TOK]).then_inc(S("d_q"), 1)
            for j in range(NPG + 1):
                r = decode_rows(j)
                heads = lambda t: t[0:r, :].rearrange("p (h t) -> p h t", h=H)
                dve.wait_ge(S("sb_z"), SBN + j + 1)
                if j >= 1:
                    dve.wait_ge(S("sb_x"), SBN + j)
                dve.tensor_tensor(heads(d_z), heads(ps[:, 2, 0:QC]),
                                  sb_bias[0:r, :].unsqueeze(2).broadcast_to([r, H, SMP]), ALU.add)\
                    .then_inc(S("d_z"), 1)
                dve.wait_ge(S("d_z"), j + 1)
                dve.tensor_scalar(d_l[0:r, :], d_z[0:r, :], 40.0, None, ALU.min).then_inc(S("sb_zc"), 1)
                dve.wait_ge(S("sb_l"), SBN + j + 1)
                if j >= 2:
                    dve.wait_ge(S("d_sum"), j - 1)
                dve.tensor_tensor(d_sp[j % 2][0:r, :], d_z[0:r, :], d_l[0:r, :], ALU.max).then_inc(S("sb_sp"), 1)
                dve.wait_ge(S("sb_sp"), SBN + j + 1)
                if j == 0:
                    dve.tensor_tensor(heads(d_sp[0]), heads(d_sp[0]),
                                      upper8[0:r, 0:SMP].unsqueeze(1).broadcast_to([r, H, SMP]), ALU.mult)\
                        .then_inc(S("sb_spm"), 1)
                    dve.wait_ge(S("sb_spm"), SB_DIAG + 1)
                    dve.tensor_copy(d_sum[0], d_sum[1]).then_inc(*did("dve"))
                    dve.wait_ge(*so_far("dve"))
                    dve.tensor_copy(d_sum[0][0:r, :], d_sp[0][0:r, :]).then_inc(S("d_sum"), 1)
                else:
                    dve.wait_ge(S("d_sum"), j)
                    dve.tensor_tensor(d_sum[j % 2], d_sum[(j - 1) % 2], d_sp[j % 2], ALU.add)\
                        .then_inc(S("d_sum"), 1)
                la_gates_vector(dve, j)

        def decode_act(act):
            def weights(j):
                r = decode_rows(j)
                act.wait_ge(S("sb_x"), SBN + j + 1)
                if j >= 1:
                    act.wait_ge(S("sb_pv"), SBN + j)
                act.activation(d_w[0:r, :], ps[0:r, 3, 0:QC], ACT.Exp).then_inc(S("sb_w"), 1)

            def evacuate(j):
                for g in range(4):
                    n = 4 * (j - 1) + g
                    act.wait_ge(S("d_kt"), n + 1)
                    if g == 0 and j >= 2:
                        act.wait_ge(S("sb_z"), SBN + j)
                    act.activation(kT_page[:, 2 * g:2 * g + 2, :, :],
                                   ps[:, n % 2, :].rearrange("p (b a t) -> p b a t", b=2, a=2), ACT.Copy)\
                        .then_inc(S("d_kT"), 1)
            act.wait_ge(S("sb_sum"), SBN)
            evacuate(1)
            for j in range(NPG + 1):
                r = decode_rows(j)
                act.wait_ge(S("sb_zc"), SBN + j + 1)
                act.activation(d_l[0:r, :], d_l[0:r, :], ACT.Exp).then_inc(*did("act"))
                act.wait_ge(*so_far("act"))
                act.activation(d_l[0:r, :], d_l[0:r, :], ACT.Ln, bias=one_col[0:r, :]).then_inc(S("sb_l"), 1)
                if j >= 1 and j < NPG:
                    evacuate(j + 1)
                weights(j)
                la_gates_act(act, j)
            la_exp(act, 0)
            act.wait_ge(S("sb_pv"), SBN + NPG + 1)
            for c in range(2):
                rws = slice(64 * c, 64 * c + 64)
                act.activation(mixT[rws, 4:6, T:TOK],
                               ps[rws, 4, 0:QC].rearrange("p (a c t) -> p a c t", a=2, c=2)[:, :, c, :],
                               ACT.Copy).then_inc(S("d_o"), 1)


        class Mixer:

            def __init__(self, dk, q, k, b, v, gate, gscale, kt0, norm, state, s0, out_p, out_s):
                self.dk, self.q, self.k, self.b, self.v, self.gate = dk, q, k, b, v, gate
                self.gscale, self.kt0, self.norm, self.state, self.s0 = gscale, kt0, norm, state, s0
                self.out_p, self.out_s = out_p, out_s
                self.nd = H * dk // P

            def head(self, h):
                per = P // self.dk
                return h // per, slice(self.dk * (h % per), self.dk * (h % per) + self.dk)

        la_b = at(PR, 3, TOK)
        la_reset = at(PR + 3 * TOK, TOK)

        def la_g(a):
            return mixT[:, (1, 7, 1)[a], :]

        def la_tmp(a):
            return mixT[:, (0, 6, 0)[a], :]

        la_x = at(WR, 2, 9, 2 * P)
        la_att = at(WR + 4608, 2, H, P)
        la_kn = at(WR + 5632, 2, GW)
        la_o_sq = at(WR + 6144, GW)
        la_o_n = at(WR + 6400, 2, GW)
        hg_state = at(WR + 6912, GW)
        gla_state = at(WR + 7168, GW)
        la_ss = at(WR + 7424, 2, H)
        la_gl = at(WR + 7432, 2 * NB)
        la_big = at(WR + 7448, NB, HD)
        la_inter = at(WR + 7960, GW)
        la_dlast = at(WR + 8216, 2, 2)
        hg_s0 = at(NR + 2 * NT * GW, 2, NB, HD)
        gla_s0 = at(NR + 2 * NT * GW + 1024, 1, NB, HD)

        HG = Mixer(HD, hqT, hfT, la_b[:, 0:2, :], hi_n, hg_n, 1.0, 0, PAR["hg_norm"], hg_state, hg_s0,
                   O["hgrn_prompt"], O["hgrn_sample"])
        GL = Mixer(32, gqT.unsqueeze(1), gkT.unsqueeze(1), la_b[:, 2:3, :], gv_n, gg_n, 1.0 / 16.0, 6,
                   PAR["gla_norm"], gla_state, gla_s0, O["gla_prompt"], O["gla_sample"])
        MIX = (HG, GL)
        LT = 2 * NT

        def la_tile(n):
            i = n % NT
            return MIX[n // NT], i, rows(i), i * P, i == NT - 1


        def la_gate_logits_tensor(pe):
            pe.wait_ge(S("sb_o"), 2 * H)
            for tg, (t0, tw) in enumerate(EG):
                ins = pe.matmul(ps[:, 5 + tg, 0:tw], gla_a2[0:16, :], gaT[0:16, t0:t0 + tw], start=True,
                                stop=True)
            ins.then_inc(S("gla_logit"), 1)

        def la_gate_logits_act(act):
            act.wait_ge(S("gla_logit"), 1)
            act.wait_ge(S("g_kx"), 1)
            for tg, (t0, tw) in enumerate(EG):
                ins = act.activation(la_g(2)[:, t0:t0 + tw], ps[:, 5 + tg, 0:tw], ACT.Identity,
                                     bias=PAR["gla_ab"])
            ins.then_inc(S("gla_x"), 1)

        def la_gate_clip(dve, a):
            if a == 2:
                dve.wait_ge(S("gla_x"), 1)
            x = la_g(2) if a == 2 else hfT[:, a, :]
            dve.tensor_scalar(la_tmp(a), x, -40.0, None, ALU.max).then_inc(S("g_clip"), 1)

        def la_gate_ln(act, a):
            act.wait_ge(S("g_clip"), a + 1)
            act.activation(la_tmp(a), la_tmp(a), ACT.Exp, scale=-1.0).then_inc(*did("act"))
            act.wait_ge(*so_far("act"))
            act.activation(la_tmp(a), la_tmp(a), ACT.Ln, bias=one_col).then_inc(S("g_l"), 1)

        def la_gate_log(dve, a):
            x = la_g(2) if a == 2 else hfT[:, a, :]
            dve.wait_ge(S("g_l"), a + 1)
            dve.scalar_tensor_tensor(la_g(a), la_tmp(a), -1.0, x, ALU.mult, ALU.min).then_inc(*did("dve"))
            dve.wait_ge(*so_far("dve"))
            dve.tensor_tensor_scan(la_b[:, a, :], la_reset, la_g(a), 0.0, ALU.mult, ALU.add)\
                .then_inc(*did("dve"))
            if a < 2:
                dve.tensor_tensor(hfT[:, a, :], la_g(a), hfT[:, a, :], ALU.subtract).then_inc(S("g_kx"), 1)

        def la_gate_k(act, a):
            act.wait_ge(S("g_kx"), a + 1)
            act.activation(hfT[:, a, :], hfT[:, a, :], ACT.Exp).then_inc(S("hg_k"), 1)

        def la_gates_vector(dve, j):
            if j == 1:
                dve.memset(la_reset, 1.0).then_inc(*did("dve"))
                dve.wait_ge(*so_far("dve"))
                dve.memset(la_reset[:, 0:T].rearrange("p (i t) -> p i t", t=P)[:, :, 0:1], 0.0)\
                    .then_inc(*did("dve"))
                dve.memset(la_reset[:, T:TOK].rearrange("p (i t) -> p i t", t=NS)[:, :, 0:1], 0.0)\
                    .then_inc(*did("dve"))
            if 2 <= j <= 4:
                la_gate_log(dve, j - 2)
            if 1 <= j <= 3:
                la_gate_clip(dve, j - 1)

        def la_gates_act(act, j):
            if 1 <= j <= 3:
                la_gate_ln(act, j - 1)
            if j == 2:
                la_gate_logits_act(act)
            if 4 <= j <= 5:
                la_gate_k(act, j - 4)

        def la_clear_vector(dve):
            dve.wait_ge(S("sb_z"), SBN + NPG + 1)
            dve.wait_ge(S("sb_pv"), SBN + NPG)
            dve.wait_ge(*so_far("dve"))
            dve.memset(la_att, 0.0).then_inc(S("la_zero"), 1)
            dve.memset(hg_state, 0.0).then_inc(S("la_zero"), 1)
            dve.memset(gla_state, 0.0).then_inc(S("la_zero"), 1)

        def la_load_sync(sp):
            sp.wait_ge(S("sv_out"), 32)
            sp.wait_ge(S("d_o"), 2)
            for a in range(2):
                for c in range(2):
                    sp.dma_start(hg_s0[64 * c:64 * c + 64, a, :, :],
                                 A["state_hgrn"][0, :, 2 * a + c, :, :].rearrange("b d e -> d b e"))\
                        .then_inc(S("la_s0"), 16)
            for h in range(H):
                sp.dma_start(gla_s0[32 * h:32 * h + 32, 0, :, :],
                             A["state_gla"][0, :, h, :, :].rearrange("b d e -> d b e")).then_inc(S("la_s0"), 16)

        def la_halves(m, t):
            return t.rearrange("p a (j h i) -> p a j h i", h=2, i=m)

        def la_levels(smp):
            return [(lv, m) for lv, m in enumerate(LEVELS) if not smp or m < NS]

        def la_diffs(eng, n, half, done):
            M, i, r, c0, smp = la_tile(n)
            b = M.b[:, :, c0:c0 + r]
            eng.wait_ge(S("la_zero"), 3)
            if n == 1:
                eng.wait_ge(S("d_o"), 2)
            if n >= 2:
                eng.wait_ge(S("la_o"), n - 1)
                eng.wait_ge(S("la_kT"), n - 1)
            for lv, m in la_levels(smp):
                v, x = la_halves(m, b), la_halves(m, la_x[:, (n + 1) % 2, lv, 0:M.nd * r].rearrange(
                    "p (a t) -> p a t", a=M.nd))
                for a in range(M.nd):
                    mid = v[:, a, :, 0, m - 1:m].broadcast_to([P, r // (2 * m), m])
                    if half == 1:
                        ins = eng.tensor_tensor(x[:, a, :, 1, :], v[:, a, :, 1, :], mid, ALU.subtract)
                    else:
                        ins = eng.tensor_tensor(x[:, a, :, 0, :], mid, v[:, a, :, 0, :], ALU.subtract)
            if half == 1:
                L = NS if smp else P
                for a in range(M.nd):
                    bb = b[:, a, :].rearrange("p (j t) -> p j t", t=L)
                    last = bb[:, :, L - 1:L].broadcast_to([P, r // L, L])
                    ins = eng.tensor_tensor(la_x[:, (n + 1) % 2, 8, a * r:(a + 1) * r].rearrange(
                        "p (j t) -> p j t", t=L), last, bb, ALU.subtract)
            ins.then_inc(S(done), 1)

        def la_exp(act, n):
            M, i, r, c0, smp = la_tile(n)
            w = M.nd * r
            act.wait_ge(S("la_xr"), n + 1)
            act.wait_ge(S("la_xl"), n + 1)
            lv0 = la_levels(smp)[0][0]
            for part in (slice(lv0, 7), slice(8, 9)):
                x = la_x[:, (n + 1) % 2, part, 0:w]
                act.activation(x, x, ACT.Exp, scale=M.gscale)
            if smp:
                if n >= NT:
                    act.wait_ge(S("la_snew"), H)
                act.activation(la_gl[:, 0:M.nd * NB].rearrange("p (a b) -> p a b", a=M.nd),
                               M.b[:, :, c0 + NS - 1:c0 + r:NS], ACT.Exp, scale=M.gscale)
            act.activation(la_x[:, (n + 1) % 2, 7, 0:w].rearrange("p (a t) -> p a t", a=M.nd),
                           M.b[:, :, c0:c0 + r], ACT.Exp, scale=M.gscale).then_inc(S("la_exp"), 1)

        def la_times(eng, n, half, done):
            M, i, r, c0, smp = la_tile(n)
            eng.wait_ge(S("la_exp"), n + 1)
            if n == 0:
                eng.wait_ge(S("hg_k"), 2)
            y = (M.q if half == 1 else M.k)[:, :, c0:c0 + r]
            for lv, m in la_levels(smp):
                x = la_halves(m, la_x[:, (n + 1) % 2, lv, 0:M.nd * r].rearrange("p (a t) -> p a t", a=M.nd))
                for a in range(M.nd):
                    ins = eng.tensor_tensor(x[:, a, :, half, :], x[:, a, :, half, :],
                                            la_halves(m, y)[:, a, :, half, :], ALU.mult)
            x = la_x[:, (n + 1) % 2, 7 if half == 1 else 8, 0:M.nd * r].rearrange("p (a t) -> p a t", a=M.nd)
            eng.tensor_tensor(x, x, y, ALU.mult).then_inc(S(done), 1)

        def la_group(smp, g):
            return ([(0, 64), (1, 32), (2, 16), (3, 8)], [(4, 4), (5, 2), (6, 1), (None, 0)])[g]

        def la_parts(n):
            return [(g, pr) for g in ((1,) if la_tile(n)[4] else (0, 1)) for pr in range(2)]

        LA_PARTS = [(n, g, pr) for n in range(LT) for g, pr in la_parts(n)]

        def la_part(n, g, pr):
            return LA_PARTS.index((n, g, pr)) + 1

        def la_direct(n, pr):
            return sum(g == 0 for _, g, _ in LA_PARTS[:la_part(n, 0, pr)])

        def la_tensor(pe):
            def key_transposes(n):
                M, i, r, c0, smp = la_tile(n)
                pe.wait_ge(S("la_tl"), n + 1)
                if n == 0:
                    pe.wait_ge(S("d_o"), 2)
                if n >= 1:
                    pe.wait_ge(S("la_kn"), n)
                if n == NT:
                    pe.wait_ge(S("la_snew"), H)
                for a in range(M.nd):
                    ins = pe.transpose(ps[0:r, 4, a * P:(a + 1) * P],
                                       la_x[:, (n + 1) % 2, 8, a * r:(a + 1) * r], ident)
                ins.then_inc(S("la_kT"), 1)

            def outputs(n):
                M, i, r, c0, smp = la_tile(n)
                pe.wait_ge(S("la_attD"), la_part(n, 1, 1))
                if not smp:
                    pe.wait_ge(S("la_attA"), la_direct(n, 1))
                if n >= 1:
                    pe.wait_ge(S("la_on"), n)
                    pe.wait_ge(S("la_S"), n)
                o = ps[0:r, 5, 0:GW]
                if not smp:
                    for a in range(M.nd):
                        w = GW // M.nd
                        pe.matmul(o[:, a * w:(a + 1) * w], la_x[:, (n + 1) % 2, 7, a * r:(a + 1) * r],
                                  M.state[:, a * w:(a + 1) * w], start=(a == 0), stop=False,
                                  skip_group_check=True)
                for h in range(H):
                    ins = pe.matmul(o[:, h * HD:(h + 1) * HD], la_att[0:r, n % 2, h, 0:r],
                                    M.v[0:r, i, h * HD:(h + 1) * HD], start=(smp and h == 0), stop=True,
                                    skip_group_check=True)
                ins.then_inc(S("la_o"), 1)
                pe.wait_ge(S("la_kn"), n + 1)
                if not smp:
                    for a in range(M.nd):
                        w = GW // M.nd
                        ins = pe.matmul(ps[:, 6, a * w:(a + 1) * w], la_kn[0:r, n % 2, a * P:(a + 1) * P],
                                        M.v[0:r, i, a * w:(a + 1) * w], start=(a == 0), stop=True,
                                        skip_group_check=True)
                    ins.then_inc(S("la_s"), 1)

            def output_transposes(n):
                M, i, r, c0, smp = la_tile(n)
                pe.wait_ge(S("la_on"), n + 1)
                if n >= 1:
                    pe.wait_ge(S("la_mix"), n)
                for a in range(2):
                    ins = pe.transpose(ps[:, 7, a * P:a * P + r], la_o_n[0:r, n % 2, a * P:(a + 1) * P],
                                       ident[0:r, 0:r])
                ins.then_inc(S("la_oT"), 1)

            def sample_states(n):
                M, i, r, c0, smp = la_tile(n)
                k = MIX.index(M)
                pe.wait_ge(S("la_s0"), 16 * 8)
                for h in range(H):
                    c = H * k + h
                    a, rws = M.head(h)
                    if c >= 1:
                        pe.wait_ge(S("la_bigr"), c)
                    pe.matmul(ps[0:r, 6, :], la_x[rws, (n + 1) % 2, 7, a * r:(a + 1) * r],
                              M.s0[rws, a, :, :], start=True, stop=True).then_inc(S("la_bigi"), 1)
                    pe.wait_ge(S("la_vexp"), c + 1)
                    if c >= 1:
                        pe.wait_ge(S("la_snew"), c)
                    kc = a * P + rws.start
                    pe.matmul(ps[rws, 4, :], la_kn[0:r, n % 2, kc:kc + M.dk], la_big[0:r, :, :],
                              start=True, stop=True).then_inc(S("la_bigs"), 1)

            for n in range(LT):
                smp = la_tile(n)[4]
                if n == 0:
                    la_scores(pe, n, 0, 0)
                if not smp:
                    la_scores(pe, n, 0, 1)
                key_transposes(n)
                if n >= 1:
                    output_transposes(n - 1)
                la_scores(pe, n, 1, 0)
                la_scores(pe, n, 1, 1)
                if smp:
                    pe.wait_ge(S("la_kn"), n + 1)
                    sample_states(n)
                if n + 1 < LT and not la_tile(n + 1)[4]:
                    la_scores(pe, n + 1, 0, 0)
                outputs(n)
            output_transposes(LT - 1)

        def la_scores(pe, n, g, pr):
            M, i, r, c0, smp = la_tile(n)
            pe.wait_ge(S("la_tr"), n + 1)
            pe.wait_ge(S("la_tl"), n + 1)
            part = la_part(n, g, pr)
            if part > 2:
                pe.wait_ge(S("la_attD"), part - 2)
                m, before, _ = LA_PARTS[part - 3]
                if before == 0:
                    pe.wait_ge(S("la_attA"), la_direct(m, pr))
            for slot, (lv, m) in enumerate(la_group(smp, g)):
                for h in (2 * pr, 2 * pr + 1):
                    a, rws = M.head(h)
                    out = ps[:, h, slot * P:slot * P + P]
                    if lv is None:
                        ins = pe.matmul(out[0:r, 0:r], M.k[rws, a, c0:c0 + r], M.q[rws, a, c0:c0 + r],
                                        start=True, stop=True, skip_group_check=True)
                        continue
                    x = la_x[rws, (n + 1) % 2, lv, a * r:(a + 1) * r]
                    if m >= 32:
                        for j in range(P // (2 * m)):
                            s0 = 2 * m * j
                            ins = pe.matmul(out[s0:s0 + m, s0 + m:s0 + 2 * m], x[:, s0:s0 + m],
                                            x[:, s0 + m:s0 + 2 * m], start=True, stop=True,
                                            skip_group_check=True)
                    else:
                        ins = pe.matmul(out[0:r, 0:r], x, x, start=True, stop=True, skip_group_check=True)
            ins.then_inc(S("la_att"), 1)

        def la_mask(dve, step, n, g, pr):
            M, i, r, c0, smp = la_tile(n)
            dve.wait_ge(S("la_att"), la_part(n, g, pr))
            if n >= 2 and (g, pr) == la_parts(n)[0]:
                dve.wait_ge(S("la_o"), n - 1)
            heads = slice(2 * pr, 2 * pr + 2)
            if smp:
                step(dve.memset(la_att[:, n % 2, heads, :], 0.0))
            elif g == 0:
                dve.wait_ge(S("la_attA"), la_direct(n, pr))
            for slot, (lv, m) in enumerate(la_group(smp, g)):
                if m >= 32:
                    continue
                mask = ident if lv is None else up_mask[:, lv, :]
                step(dve.copy_predicated(la_att[0:r, n % 2, heads, 0:r],
                                         mask[0:r, 0:r].bitcast(U32).unsqueeze(1).broadcast_to([r, 2, r]),
                                         ps[0:r, heads, slot * P:slot * P + r]))
            dve.nop().then_inc(S("la_attD"), 1)

        def la_state(dve, n):
            M, i, r, c0, smp = la_tile(n)
            if smp:
                return
            dve.wait_ge(S("la_s"), sum(not la_tile(j)[4] for j in range(n + 1)))
            dve.wait_ge(S("la_o"), n + 1)
            dve.wait_ge(S("la_exp"), n + 1)
            dve.wait_ge(S("la_dl"), sum(not la_tile(j)[4] for j in range(n + 1)))
            for h in range(H):
                a, rws = M.head(h)
                blk = M.state[rws, h * HD:(h + 1) * HD]
                ins = dve.scalar_tensor_tensor(blk, blk, la_dlast[rws, n % 2, a:a + 1],
                                               ps[rws, 6, h * HD:(h + 1) * HD], ALU.mult, ALU.add)
            ins.then_inc(S("la_S"), 1)

        def la_normalise(dve, n):
            M, i, r, c0, smp = la_tile(n)
            o = ps[0:r, 5, 0:GW]
            if smp:
                dve.wait_ge(S("la_o"), n + 1)
                dve.tensor_tensor(la_inter[0:r, :], o, la_inter[0:r, :], ALU.add).then_inc(S("la_osum"), 1)
                o = la_inter[0:r, :]
            dve.wait_ge(S("la_sq"), n + 1)
            dve.tensor_reduce(la_ss[0:r, n % 2, :], la_o_sq[0:r, :].rearrange("p (h e) -> p h e", h=H), AX,
                              ALU.add).then_inc(S("la_ss"), 1)
            if smp:
                dve.wait_ge(S("la_osum"), n // NT + 1)
            else:
                dve.wait_ge(S("la_o"), n + 1)
            if n >= 2:
                dve.wait_ge(S("la_oT"), n - 1)
            on = la_o_n[0:r, n % 2, :]
            dve.tensor_tensor(on, o, M.gate[0:r, i, :], ALU.mult).then_inc(*did("dve"))
            dve.wait_ge(*so_far("dve"))
            dve.wait_ge(S("la_rs"), n + 1)
            dve.tensor_tensor(on.rearrange("p (h e) -> p h e", h=H), on.rearrange("p (h e) -> p h e", h=H),
                              la_ss[0:r, n % 2, :].unsqueeze(2).broadcast_to([r, H, HD]), ALU.mult)\
                .then_inc(S("la_on"), 1)

        def la_sample_vector(dve, n):
            M, i, r, c0, smp = la_tile(n)
            k = MIX.index(M)
            sm = seqmask[0:r, :].unsqueeze(2).broadcast_to([r, NB, HD])
            for h in range(H):
                c = H * k + h
                a, rws = M.head(h)
                dve.wait_ge(S("la_bigi"), c + 1)
                if c >= 1:
                    dve.wait_ge(S("la_bigs"), c)
                if h == 0 and k == 1:
                    dve.wait_ge(*so_far("dve"))
                dve.tensor_tensor(la_big[0:r, :, :], ps[0:r, 6, :].rearrange("p (b e) -> p b e", b=NB), sm,
                                  ALU.mult).then_inc(*did("dve"))
                dve.wait_ge(*so_far("dve"))
                dve.tensor_reduce(la_inter[0:r, h * HD:(h + 1) * HD],
                                  la_big[0:r, :, :].rearrange("p b e -> p e b"), AX, ALU.add)\
                    .then_inc(S("la_bigr"), 1)
                dve.wait_ge(S("la_bigr"), c + 1)
                dve.tensor_tensor(la_big[0:r, :, :],
                                  M.v[0:r, i, h * HD:(h + 1) * HD].unsqueeze(1).broadcast_to([r, NB, HD]), sm,
                                  ALU.mult).then_inc(S("la_vexp"), 1)
                gl = la_gl[rws, a * NB:(a + 1) * NB].unsqueeze(2).broadcast_to([M.dk, NB, HD])
                dve.wait_ge(S("la_exp"), n + 1)
                dve.wait_ge(S("la_bigs"), c + 1)
                dve.tensor_tensor(M.s0[rws, a, :, :], M.s0[rws, a, :, :], gl, ALU.mult)\
                    .then_inc(*did("dve"))
                dve.wait_ge(*so_far("dve"))
                dve.tensor_tensor(M.s0[rws, a, :, :], M.s0[rws, a, :, :],
                                  ps[rws, 4, :].rearrange("p (b e) -> p b e", b=NB), ALU.add)\
                    .then_inc(S("la_snew"), 1)

        def la_vector(dve):
            step = chain(dve, "dve")
            la_diffs(dve, 0, 1, "la_xr")
            la_times(dve, 0, 1, "la_tr")
            for n in range(LT):
                smp = la_tile(n)[4]
                if not smp:
                    la_mask(dve, step, n, 0, 0)
                if n + 1 < LT:
                    la_diffs(dve, n + 1, 1, "la_xr")
                if not smp:
                    la_mask(dve, step, n, 0, 1)
                la_mask(dve, step, n, 1, 0)
                if n + 1 < LT:
                    la_times(dve, n + 1, 1, "la_tr")
                la_mask(dve, step, n, 1, 1)
                if smp:
                    la_sample_vector(dve, n)
                    dve.nop().then_inc(S("la_S"), 1)
                la_state(dve, n)
                la_normalise(dve, n)

        def la_gpsimd(pool):
            la_diffs(pool, 0, 0, "la_xl")
            la_times(pool, 0, 0, "la_tl")
            for n in range(LT):
                if n + 1 < LT:
                    la_diffs(pool, n + 1, 0, "la_xl")
                    la_times(pool, n + 1, 0, "la_tl")
                if la_tile(n)[1] == NT - 2:
                    M = la_tile(n)[0]
                    pool.wait_ge(S("la_S"), n + 1)
                    for h in range(H):
                        a, rws = M.head(h)
                        pool.dma_start(M.out_p[0, 0, h], M.state[rws, h * HD:(h + 1) * HD])\
                            .then_inc(S("states_out"), 16)
            for M in MIX:
                pool.wait_ge(S("la_snew"), H * (MIX.index(M) + 1))
                for h in range(H):
                    a, rws = M.head(h)
                    pool.dma_start(M.out_s[0, :, h].rearrange("b d e -> d b e"), M.s0[rws, a, :, :])\
                        .then_inc(S("states_out"), 16)

        def la_act(act):
            def last_decay(n):
                M, i, r, c0, smp = la_tile(n)
                if smp:
                    return
                if n >= 2:
                    act.wait_ge(S("la_S"), n - 1)
                act.activation(la_dlast[:, n % 2, 0:M.nd].unsqueeze(2), M.b[:, :, c0 + r - 1:c0 + r], ACT.Exp,
                               scale=M.gscale).then_inc(S("la_dl"), 1)

            def direct(n):
                M, i, r, c0, smp = la_tile(n)
                if smp:
                    return
                for pr in range(2):
                    direct_pair(n, pr)

            def direct_pair(n, pr):
                act.wait_ge(S("la_att"), la_part(n, 0, pr))
                if n >= 2:
                    act.wait_ge(S("la_o"), n - 1)
                act.wait_ge(S("la_zero"), 3)
                for slot, m in ((0, 64), (1, 32)):
                    for j in range(P // (2 * m)):
                        s0 = 2 * m * j
                        ins = act.activation(la_att[s0:s0 + m, n % 2, 2 * pr:2 * pr + 2, s0 + m:s0 + 2 * m],
                                             ps[s0:s0 + m, 2 * pr:2 * pr + 2,
                                                slot * P + s0 + m:slot * P + s0 + 2 * m], ACT.Copy)
                ins.then_inc(S("la_attA"), 1)

            def mix_out(n):
                M, i, r, c0, smp = la_tile(n)
                act.wait_ge(S("la_oT"), n + 1)
                act.activation(mixT[:, M.kt0:M.kt0 + 2, c0:c0 + r],
                               ps[:, 7, 0:GW].rearrange("p (a t) -> p a t", a=2)[:, :, 0:r], ACT.Copy,
                               scale=M.norm).then_inc(S("la_mix"), 1)

            for n in range(LT):
                M, i, r, c0, smp = la_tile(n)
                last_decay(n)
                direct(n)
                if n + 1 < LT:
                    la_exp(act, n + 1)
                act.wait_ge(S("la_kT"), n + 1)
                if n >= 2:
                    act.wait_ge(S("la_o"), n - 1)
                    act.wait_ge(S("la_S"), n - 1)
                act.activation(la_kn[0:r, n % 2, 0:M.nd * P], ps[0:r, 4, 0:M.nd * P], ACT.Copy)\
                    .then_inc(S("la_kn"), 1)
                if n >= 1:
                    mix_out(n - 1)
                if smp:
                    act.wait_ge(S("la_osum"), n // NT + 1)
                act.wait_ge(S("la_o"), n + 1)
                if n >= 1:
                    act.wait_ge(S("la_ss"), n)
                act.activation(la_o_sq[0:r, :], la_inter[0:r, :] if smp else ps[0:r, 5, 0:GW], ACT.Square)\
                    .then_inc(S("la_sq"), 1)
                act.wait_ge(S("la_ss"), n + 1)
                ss = la_ss[0:r, n % 2, :]
                act.activation(ss, ss, ACT.Ln, scale=1.0 / HD, bias=eps_col[0:r, :]).then_inc(*did("act"))
                act.wait_ge(*so_far("act"))
                act.activation(ss, ss, ACT.Exp, scale=-0.5).then_inc(S("la_rs"), 1)
            mix_out(LT - 1)


        rwR, rwK, rwV = at(NR, 2, TOK), at(NR + 2 * TOK, 2, TOK), at(NR + 4 * TOK, 2, TOK)
        rwX = at(NR + 6 * TOK, TOK)
        rw_bonus = at(NR + 7 * TOK, 2, TOK)
        _o = NR + 9 * TOK
        rw_state = at(_o, GW)
        rw_stmp = at(_o + 256, GW)
        rw_inter = at(_o + 512, 2, GW)
        rw_big = at(_o + 1024, NB, HD)
        RP = PR + 8 * TOK
        rwKQ, rwAH, rwLW = at(RP, 2, TOK), at(RP + 2 * TOK, 2, TOK), at(RP + 4 * TOK, 2, TOK)
        rw_s0 = at(RP + 6 * TOK, 2, NB, HD)
        rwB, rwA = at(PR, 2, TOK), at(PR + 2 * TOK, 2, TOK)
        rwT1, rwT2 = at(PR + 4 * TOK, 2, TOK), at(PR + 6 * TOK, 2, TOK)
        rw_d = at(PR, 2, PADW)
        GR = RP + RWT * PADW
        rw_reset = at(GR, TOK)
        rw_s0_in = at(GR + TOK, 2, NB, P)
        rw_mats = at(WR, 4, 4, H, P)
        rw_dv = at(WR, 2, PADW)
        rw_sh9 = at(WR + 8192, RWT, 1 + NB)
        rw_pc = at(WR + 8256, 2, NT - 1 + NB)
        rw_col = at(WR + 8288, 8)
        rw_ms = at(WR + 8296, 2, H)
        rw_x = at(PR, 2, H, P)
        rw_t = at(PR + 1024, 2, H, P)
        rw_xt = at(PR + 2048, 4, H, P)
        rw_nat = at(PR + 4096, 4, 3, GW)
        rw_rh = at(PR + 7168, GW)
        rw_u = at(PR + 7424, GW)
        rw_yc = at(PR + 7680, GW)
        rw_sq = at(PR + 7936, GW)
        rw_mz = at(PR + 8192, GW)
        rw_shift_out = at(GR + TOK, RWT * P)
        LOG_DECAY = -math.exp(-0.5)
        LN_SCALE = 2.0 ** 30

        def rw_shifted(ct):
            return (rwR, rwR, rwK, rwK, rwV, rwV)[ct][:, ct % 2, :] if ct < 6 else rwX

        SHIFT_ORDER = (6, 2, 3, 0, 1, 4, 5)

        def rw_prep_vector(dve):
            step = chain(dve, "dve")
            dve.wait_ge(S("la_mix"), LT)
            dve.wait_ge(S("states_out"), 16 * 16)
            step(dve.tensor_copy(rw_sh9[:, :, 0:1], rwP[:, :, T:T + 1]))
            smp_view = rwP[:, :, 1 + T:].rearrange("p c (b t) -> p c b t", b=NB)
            dve.tensor_copy(rw_sh9[:, :, 1:].unsqueeze(3), smp_view[:, :, :, NS:NS + 1])\
                .then_inc(S("rw_sh9"), 1)
            step(dve.memset(rw_reset, 1.0))
            step(dve.memset(rw_reset[:, 0:T].rearrange("p (i t) -> p i t", t=P)[:, :, 0:1], 0.0))
            step(dve.memset(rw_reset[:, T:TOK].rearrange("p (i t) -> p i t", t=NS)[:, :, 0:1], 0.0))
            step(dve.memset(rw_col[:, 0:1], 0.5 * math.log(LN_SCALE)))
            step(dve.memset(rw_col[:, 1:2], RW_GN_EPS))
            dve.tensor_scalar(PAR["one_k_a"], PAR["k_a"], -1.0, 1.0, ALU.mult, ALU.add)\
                .then_inc(*did("dve"))
            for n, ct in enumerate(SHIFT_ORDER):
                dst, mu = rw_shifted(ct), PAR["mu"][:, ct:ct + 1]
                if ct in (4, 5):
                    d = rw_dv[:, ct - 4, 0:PADW - 1]
                    dve.wait_ge(S("rw_m0"), ct - 3)
                else:
                    d = rw_d[:, n % 2, 0:PADW - 1]
                    step(dve.tensor_tensor(d, rwP[:, ct, 0:PADW - 1], rwP[:, ct, 1:PADW], ALU.subtract))
                dve.scalar_tensor_tensor(dst[:, 0:T], d[:, 0:T], mu, rwP[:, ct, 1:1 + T], ALU.mult, ALU.add)
                tail = lambda t: t.rearrange("p (b t) -> p b t", b=NB)
                dve.scalar_tensor_tensor(tail(dst[:, T:TOK]), tail(d[:, T:PADW - 1])[:, :, 1:], mu,
                                         tail(rwP[:, ct, 1 + T:PADW])[:, :, 1:], ALU.mult, ALU.add)\
                    .then_inc(S("rw_xs"), 1)
            dve.wait_ge(S("rw_xs"), RWT)
            dve.wait_ge(*so_far("dve"))
            for a in range(2):
                step(dve.tensor_scalar(rwT1[:, a, :], rwK[:, a, :], PAR["k_k"][:, a:a + 1], None, ALU.mult))
                dve.tensor_tensor(rwT2[:, a, :], rwT1[:, a, :], rwT1[:, a, :], ALU.mult).then_inc(S("rw_kk2"), 1)
            dve.wait_ge(S("rw_gate"), 6)
            for a in range(2):
                step(dve.tensor_scalar(rwLW[:, a, :], rwLW[:, a, :], LOG_DECAY, None, ALU.mult))
                dve.tensor_tensor_scan(rwB[:, a, :], rw_reset, rwLW[:, a, :], 0.0, ALU.mult, ALU.add)\
                    .then_inc(*did("dve"))
            for q in range(6):
                a, (t0, tw) = q // 3, TG[q % 3]
                dve.wait_ge(S("rw_q"), 18 + q + 1)
                dve.tensor_scalar(rwT2[:, a, t0:t0 + tw], ps[:, q, 0:tw], 1e-24, None, ALU.max)\
                    .then_inc(S("rw_ss"), 1)
            dve.wait_ge(S("rw_gate"), 12)
            for a in range(2):
                step(dve.tensor_scalar(rwKQ[:, a, :], rwA[:, a, :], PAR["k_a"][:, a:a + 1],
                                       PAR["one_k_a"][:, a:a + 1], ALU.mult, ALU.add))
                step(dve.tensor_tensor(rwK[:, a, :], rwK[:, a, :], rwKQ[:, a, :], ALU.mult))
                dve.scalar_tensor_tensor(rwAH[:, a, :], rwR[:, a, :], PAR["r_k"][:, a:a + 1], rwK[:, a, :],
                                         ALU.mult, ALU.mult).then_inc(S("rw_rkrk"), 1)
            for q in range(6):
                a, (t0, tw) = q // 3, TG[q % 3]
                dve.wait_ge(S("rw_q"), 24 + q + 1)
                dve.tensor_tensor(rw_bonus[:, a, t0:t0 + tw], ps[:, q, 0:tw], rwV[:, a, t0:t0 + tw], ALU.mult)\
                    .then_inc(*did("dve"))
            dve.wait_ge(S("rw_rn"), 2)
            dve.wait_ge(*so_far("dve"))
            for a in range(2):
                step(dve.tensor_tensor(rwT1[:, a, :], rwT1[:, a, :], rwT2[:, a, :], ALU.mult))
                dve.tensor_tensor(rwT2[:, a, :], rwB[:, a, :], rwLW[:, a, :], ALU.subtract)\
                    .then_inc(S("rw_bprev"), 1)
            for a in range(2):
                step(dve.tensor_tensor(rwAH[:, a, :], rwT1[:, a, :], rwA[:, a, :], ALU.mult))
                dve.wait_ge(S("rw_e"), 3 * a + 1)
                dve.scalar_tensor_tensor(rwKQ[:, a, :], rwT1[:, a, :], -1.0, rwT2[:, a, :], ALU.mult, ALU.mult)
                dve.wait_ge(S("rw_e"), 3 * a + 2)
                dve.tensor_tensor(rwAH[:, a, :], rwAH[:, a, :], rwLW[:, a, :], ALU.mult)
                dve.tensor_tensor(rwK[:, a, :], rwK[:, a, :], rwLW[:, a, :], ALU.mult)
                dve.wait_ge(S("rw_e"), 3 * a + 3)
                dve.tensor_copy(rw_pc[:, a, 0:NT - 1], rwB[:, a, P - 1:T:P])
                dve.tensor_copy(rw_pc[:, a, NT - 1:], rwB[:, a, T + NS - 1:TOK:NS])
                dve.tensor_tensor(rwR[:, a, :], rwR[:, a, :], rwB[:, a, :], ALU.mult).then_inc(S("rw_ready"), 1)
            dve.memset(rw_state, 0.0).then_inc(*did("dve"))
            dve.wait_ge(S("rw_ready"), 2)
            dve.wait_ge(*so_far("dve"))

        def rw_prep_act(act):
            act.wait_ge(S("rw_shp"), 1)
            act.activation(rw_shift_out[0:1 + NB, 0:512], ps[0:1 + NB, 6, :], ACT.Copy)
            act.activation(rw_shift_out[0:1 + NB, 512:RWT * P], ps[0:1 + NB, 7, 0:RWT * P - 512], ACT.Copy)\
                .then_inc(S("rw_shout"), 1)
            act.wait_ge(S("rw_xs"), 1)
            act.activation(rwX[0:32, :], rwX[0:32, :], ACT.Tanh).then_inc(S("rw_lr"), 1)
            act.activation(rwX[64:128, :], rwX[64:128, :], ACT.Sigmoid).then_inc(S("rw_lr"), 1)
            act.wait_ge(S("rw_xs"), RWT)
            for q in range(18):
                kind, a, (t0, tw) = q // 6, q % 6 // 3, TG[q % 3]
                act.wait_ge(S("rw_q"), q + 1)
                src = ps[:, q % 6, 0:tw]
                if kind == 0:
                    ins = act.activation(rwLW[:, a, t0:t0 + tw], src, ACT.Sigmoid, bias=PAR["w0"][:, a:a + 1])
                elif kind == 1:
                    ins = act.activation(rwA[:, a, t0:t0 + tw], src, ACT.Sigmoid, bias=PAR["a0"][:, a:a + 1])
                else:
                    ins = act.activation(mixT[:, 2 + a, t0:t0 + tw], src, ACT.Copy)
                ins.then_inc(S("rw_gate"), 1)
            act.preload_act_table_set("natural_log_exp_and_others")
            act.wait_ge(S("rw_ss"), 6)
            for a in range(2):
                act.activation(rwT2[:, a, :], rwT2[:, a, :], ACT.Ln, scale=LN_SCALE).then_inc(*did("act"))
                act.wait_ge(*so_far("act"))
                act.activation(rwT2[:, a, :], rwT2[:, a, :], ACT.Exp, scale=-0.5, bias=rw_col[:, 0:1])\
                    .then_inc(S("rw_rn"), 1)
            act.wait_ge(S("rw_bprev"), 2)
            for a in range(2):
                act.activation(rwT2[:, a, :], rwT2[:, a, :], ACT.Exp).then_inc(S("rw_e"), 1)
                act.activation(rwLW[:, a, :], rwB[:, a, :], ACT.Exp, scale=-1.0).then_inc(S("rw_e"), 1)
                act.activation(rwB[:, a, :], rwB[:, a, :], ACT.Exp).then_inc(S("rw_e"), 1)

        def rw_prep_tensor(pe):
            pe.wait_ge(S("la_mix"), LT)
            pe.wait_ge(S("rw_sh9"), 1)
            for ct in range(RWT):
                ins = pe.transpose(ps[0:1 + NB, 6 + ct // 4, (ct % 4) * P:(ct % 4) * P + P], rw_sh9[:, ct, :],
                                   ident)
            ins.then_inc(S("rw_shp"), 1)
            for q in range(30):
                kind, a, (t0, tw) = q // 6, q % 6 // 3, TG[q % 3]
                if kind == 0:
                    pe.wait_ge(S("rw_lr"), 1)
                    lhs, rhs = w2all[0:32, a * P:(a + 1) * P], rwX[0:32, t0:t0 + tw]
                elif kind == 1:
                    pe.wait_ge(S("rw_gate"), q - 5)
                    lhs, rhs = w2all[32:64, a * P:(a + 1) * P], rwX[32:64, t0:t0 + tw]
                elif kind == 2:
                    pe.wait_ge(S("rw_gate"), q - 5)
                    pe.wait_ge(S("rw_lr"), 2)
                    lhs, rhs = w2all[64:128, a * P:(a + 1) * P], rwX[64:128, t0:t0 + tw]
                elif kind == 3:
                    pe.wait_ge(S("rw_gate"), q - 5)
                    pe.wait_ge(S("rw_kk2"), a + 1)
                    lhs, rhs = headones, rwT2[:, a, t0:t0 + tw]
                else:
                    pe.wait_ge(S("rw_ss"), q - 23)
                    pe.wait_ge(S("rw_rkrk"), a + 1)
                    lhs, rhs = headones, rwAH[:, a, t0:t0 + tw]
                pe.matmul(ps[:, q % 6, 0:tw], lhs, rhs, start=True, stop=True).then_inc(S("rw_q"), 1)
            pe.wait_ge(S("rw_s0_in"), 64)
            pe.wait_ge(S("rw_shout"), 1)
            for a in range(2):
                for b in range(NB):
                    ins = pe.transpose(ps[:, 6 + a, b * HD:(b + 1) * HD], rw_s0_in[0:HD, a, b, :],
                                       ident[0:HD, 0:HD])
            ins.then_inc(S("rw_s0p"), 1)

        def rw_gpsimd(pool):
            pool.wait_ge(S("la_mix"), LT)
            pool.wait_ge(S("states_out"), 16 * 16)
            for a in range(2):
                pool.tensor_tensor(rw_dv[:, a, 0:PADW - 1], rwP[:, 4 + a, 0:PADW - 1], rwP[:, 4 + a, 1:PADW],
                                   ALU.subtract).then_inc(S("rw_m0"), 1)
            pool.wait_ge(S("rw_xs"), RWT)
            for sl in range(4):
                pool.memset(rw_mats[:, sl, :, :, :], 0.0).then_inc(S("rw_m0"), 1)
            pool.wait_ge(S("rw_m0"), 6)
            for sl in range(4):
                pool.tensor_copy(rw_mats[:, sl, 0, :, :], ident.unsqueeze(1).broadcast_to([P, H, P]))\
                    .then_inc(S("rw_m0"), 1)
            pool.wait_ge(S("rw_shout"), 1)
            pool.dma_start(O["rwkv_shift_prompt"][0], rw_shift_out[0:1, :]).then_inc(S("shift_out"), 16)
            pool.dma_start(O["rwkv_shift_sample"][0], rw_shift_out[1:1 + NB, :]).then_inc(S("shift_out"), 16)
            pool.wait_ge(S("shift_out"), 32)
            for h in range(H):
                c = h % 2
                pool.dma_start(rw_s0_in[0:HD, h // 2, :, 64 * c:64 * c + 64],
                               A["state_rwkv"][0, :, h, :, :].rearrange("b v k -> v b k"))\
                    .then_inc(S("rw_s0_in"), 16)
            pool.wait_ge(S("rw_fin_p"), 1)
            for h in range(H):
                c, a = h % 2, h // 2
                pool.dma_start(O["rwkv_prompt"][0, 0, h],
                               rw_stmp[64 * c:64 * c + 64, a * P + 64 * c:a * P + 64 * c + 64])\
                    .then_inc(S("states_out"), 16)
            pool.wait_ge(S("rw_fin_s"), 4)
            for h in range(H):
                c = h % 2
                pool.dma_start(O["rwkv_sample"][0, :, h, :, :].rearrange("b v k -> v b k"),
                               rw_s0_in[0:HD, h // 2, :, 64 * c:64 * c + 64]).then_inc(S("rw_states_out"), 16)

        def rw_schedule():
            items = []
            pairs = [(0, 1), (2, 3), (4, 5), (6, 7), (NT - 1,)]
            for p, pair in enumerate(pairs):
                prev = pairs[p - 1] if p else ()
                fill = [(k, prev[j]) for k, j in (("rhs", 0), ("solve", 0), ("out", 0), ("rhs", 1), ("turn", 0),
                                                  ("solve", 1), ("out", 1), ("turn", 1))] if p else []
                items += [("front", n) for n in pair]
                for lv in range(6, -1, -1) if len(pair) == 2 else (6, 5, 4):
                    items += [("join_a", n, lv) for n in pair]
                    items += [fill.pop(0)] if fill else []
                    items += [("join_b", n, lv) for n in pair]
                    if len(fill) > 6 or len(pair) == 1:
                        items += [fill.pop(0)] if fill else []
                items += fill
            return items

        RW_ITEMS = rw_schedule()

        def rw_upto(kind, *key):
            last = max(j for j, it in enumerate(RW_ITEMS) if it[0] == kind and it[1:1 + len(key)] == key)
            return sum(it[0] == kind for it in RW_ITEMS[:last + 1])

        def rw_last_level(n):
            return 4 if n == NT - 1 else 0

        def rw_before(kind, at_item):
            return sum(it[0] == kind for it in RW_ITEMS[:RW_ITEMS.index(at_item)])

        def rw_tensor(pe):
            for item in RW_ITEMS:
                kind, n = item[0], item[1]
                r, c0 = rows(n), n * P
                cols = slice(c0, c0 + r)
                sl, e = n % 4, n % 2
                nat = rw_nat[0:r, sl, :, :]
                if kind == "front":
                    if n == 0:
                        pe.wait_ge(S("rw_ready"), 2)
                    else:
                        pe.wait_ge(S("rw_mats"), n)
                        pe.wait_ge(S("rw_nat"), n)
                        if rw_before("join_b", item):
                            pe.wait_ge(S("rw_xx"), rw_before("join_b", item))
                    for h in range(H):
                        a, rws = h // 2, slice(64 * (h % 2), 64 * (h % 2) + 64)
                        for ty, (lhs, rhs) in enumerate(((rwAH, rwKQ), (rwK, rwKQ), (rwAH, rwR), (rwK, rwR))):
                            ins = pe.matmul(ps[0:r, h, ty * P:ty * P + r], lhs[rws, a, cols], rhs[rws, a, cols],
                                            start=True, stop=True, skip_group_check=True)
                    ins.then_inc(S("rw_mp"), 1)
                    for y, src in enumerate((rwK, rwAH, rwV)):
                        for a in range(2):
                            ins = pe.transpose(ps[0:r, 4 + y // 2, (y % 2) * GW + a * P:(y % 2) * GW + (a + 1) * P],
                                               src[:, a, cols], ident)
                    ins.then_inc(S("rw_np"), 1)
                elif kind == "join_a":
                    lv = item[2]
                    first = lv == 6
                    if first:
                        pe.wait_ge(S("rw_mats"), n + 1)
                        pe.wait_ge(S("rw_nat"), min(NT, (n // 2) * 2 + 2))
                        pe.wait_ge(S("rw_mats"), min(NT, (n // 2) * 2 + 2))
                    else:
                        pe.wait_ge(S("rw_xx"), rw_upto("join_b", n, lv + 1))
                    for h in range(H):
                        x = ident[0:r, 0:r] if first else (rw_t if lv == 5 else rw_x)[0:r, e, h, 0:r]
                        ins = pe.matmul(ps[0:r, 3 * e, h * P:h * P + r], rw_mats[0:r, sl, 0, h, 0:r], x,
                                        start=(h == 0), stop=True, skip_group_check=True)
                    ins.then_inc(S("rw_ja"), 1)
                elif kind == "join_b":
                    lv = item[2]
                    pe.wait_ge(S("rw_t1"), rw_upto("join_a", n, lv))
                    for h in range(H):
                        t1 = rw_t[0:r, e, h, 0:r]
                        if lv != 6 and lv != rw_last_level(n):
                            pe.matmul(ps[0:r, 3 * e + 1, h * P:h * P + r], rw_xt[0:r, sl, h, 0:r], t1,
                                      start=(h == 0), stop=True, skip_group_check=True)
                        xt = ident[0:r, 0:r] if lv == 6 else rw_xt[0:r, sl, h, 0:r]
                        ins = pe.matmul(ps[0:r, 3 * e + 2, h * P:h * P + r], t1, xt, start=(h == 0), stop=True,
                                        skip_group_check=True)
                    ins.then_inc(S("rw_jb"), 1)
                elif kind == "rhs":
                    pe.wait_ge(S("rw_nat"), n + 1)
                    if n >= 1:
                        pe.wait_ge(S("rw_S"), n)
                        pe.wait_ge(S("rw_u"), n)
                    else:
                        pe.wait_ge(S("rw_s0"), 1)
                    for a in range(2):
                        pe.matmul(ps[0:r, 6, a * P:(a + 1) * P], rwKQ[:, a, cols], rw_state[:, a * P:(a + 1) * P],
                                  start=(a == 0), stop=False, skip_group_check=True)
                    for h in range(H):
                        hc = slice(h * HD, (h + 1) * HD)
                        ins = pe.matmul(ps[0:r, 6, hc], rw_mats[0:r, sl, 1, h, 0:r], nat[:, 2, hc], start=False,
                                        stop=True, skip_group_check=True)
                    ins.then_inc(S("rw_c1"), 1)
                elif kind == "solve":
                    pe.wait_ge(S("rw_rh"), n + 1)
                    pe.wait_ge(S("rw_xx"), rw_upto("join_b", n, rw_last_level(n)))
                    for h in range(H):
                        hc = slice(h * HD, (h + 1) * HD)
                        ins = pe.matmul(ps[0:r, 6, GW + h * HD:GW + (h + 1) * HD], rw_xt[0:r, sl, h, 0:r],
                                        rw_rh[0:r, hc], start=(h == 0), stop=True, skip_group_check=True)
                    ins.then_inc(S("rw_c2"), 1)
                elif kind == "out":
                    pe.wait_ge(S("rw_u"), n + 1)
                    if n >= 1:
                        pe.wait_ge(S("rw_mz"), n)
                    for a in range(2):
                        pe.matmul(ps[0:r, 7, a * P:(a + 1) * P], rwR[:, a, cols], rw_state[:, a * P:(a + 1) * P],
                                  start=(a == 0), stop=False, skip_group_check=True)
                    for h in range(H):
                        hc = slice(h * HD, (h + 1) * HD)
                        pe.matmul(ps[0:r, 7, hc], rw_mats[0:r, sl, 2, h, 0:r], rw_u[0:r, hc], start=False,
                                  stop=False, skip_group_check=True)
                        pe.matmul(ps[0:r, 7, hc], rw_mats[0:r, sl, 3, h, 0:r], nat[:, 2, hc], start=False,
                                  stop=True, skip_group_check=True)
                    for a in range(2):
                        ac = slice(a * P, (a + 1) * P)
                        pe.matmul(ps[:, 7, GW + a * P:GW + (a + 1) * P], nat[:, 1, ac], rw_u[0:r, ac],
                                  start=False, stop=False, skip_group_check=True)
                        ins = pe.matmul(ps[:, 7, GW + a * P:GW + (a + 1) * P], nat[:, 0, ac], nat[:, 2, ac],
                                        start=False, stop=True, skip_group_check=True)
                    ins.then_inc(S("rw_c3"), 1)
                elif kind == "turn":
                    pe.wait_ge(S("rw_yn"), n + 1)
                    pe.wait_ge(S("rw_S"), n + 1)
                    for a in range(2):
                        ins = pe.transpose(ps[:, 7, a * P:a * P + r], rw_yc[0:r, a * P:(a + 1) * P],
                                           ident[0:r, 0:r])
                    ins.then_inc(S("rw_c6"), 1)

        def rw_vector(dve):
            step = chain(dve, "dve")
            dve.wait_ge(S("rw_m0"), 10)
            for item in RW_ITEMS:
                kind, n = item[0], item[1]
                r, c0 = rows(n), n * P
                cols = slice(c0, c0 + r)
                sl, e = n % 4, n % 2
                if kind == "front":
                    smp = n == NT - 1
                    if n >= 4:
                        dve.wait_ge(S("rw_c3"), n - 3)
                    if smp:
                        step(dve.memset(rw_mats[0:r, sl, :, :, 0:r], 0.0))
                        step(dve.tensor_copy(rw_mats[0:r, sl, 0, :, 0:r],
                                             ident[0:r, 0:r].unsqueeze(1).broadcast_to([r, H, r])))
                    dve.wait_ge(S("rw_mp"), n + 1)
                    for ty in range(4):
                        mask = ((upper8 if smp else upper) if ty < 2 else (upper8_eq if smp else upper_eq))
                        ins = dve.copy_predicated(rw_mats[0:r, sl, ty, :, 0:r],
                                                  mask[0:r, 0:r].bitcast(U32).unsqueeze(1).broadcast_to([r, H, r]),
                                                  ps[0:r, 0:H, ty * P:ty * P + r])
                    ins.then_inc(S("rw_mats"), 1)
                elif kind == "join_a":
                    lv = item[2]
                    dve.wait_ge(S("rw_ja"), rw_upto("join_a", n, lv))
                    heads = lambda t: t.rearrange("p (h t) -> p h t", h=H)[:, :, 0:r]
                    dve.tensor_tensor(rw_t[0:r, e, :, 0:r], heads(ps[0:r, 3 * e, :]),
                                      low_eq[0:r, lv, 0:r].unsqueeze(1).broadcast_to([r, H, r]), ALU.mult)\
                        .then_inc(S("rw_t1"), 1)
                elif kind == "out":
                    dve.wait_ge(S("rw_c3"), n + 1)
                    y = ps[0:r, 7, 0:GW].rearrange("p (h e) -> p h e", h=H)
                    step(dve.tensor_tensor(rw_stmp, rw_state, ps[:, 7, GW:2 * GW], ALU.add))
                    for a in range(2):
                        ac = slice(a * P, (a + 1) * P)
                        ins = dve.scalar_tensor_tensor(rw_state[:, ac], rw_stmp[:, ac], rw_pc[:, a, n:n + 1],
                                                       headones, ALU.mult, ALU.mult)
                    ins.then_inc(S("rw_S"), 1)
                    rw_norm(dve, step, n, r, y)
                elif kind == "turn":
                    rw_mix(dve, step, n, r, cols)

        def rw_norm(dve, step, n, r, y):
            step(dve.tensor_reduce(rw_ms[0:r, 0, :], y, AX, ALU.add))
            if n >= 1:
                dve.wait_ge(S("rw_c6"), n)
            yc = rw_yc[0:r, :].rearrange("p (h e) -> p h e", h=H)
            dve.scalar_tensor_tensor(yc, rw_ms[0:r, 0, :].unsqueeze(2).broadcast_to([r, H, HD]), -1.0 / HD, y,
                                     ALU.mult, ALU.add).then_inc(S("rw_yc"), 1)
            dve.wait_ge(S("rw_ysq"), n + 1)
            dve.tensor_reduce(rw_ms[0:r, 1, :], rw_sq[0:r, :].rearrange("p (h e) -> p h e", h=H), AX,
                              ALU.add).then_inc(S("rw_var"), 1)
            dve.wait_ge(S("rw_yrs"), n + 1)
            dve.tensor_tensor(yc, yc, rw_ms[0:r, 1, :].unsqueeze(2).broadcast_to([r, H, HD]), ALU.mult)\
                .then_inc(S("rw_yn"), 1)

        def rw_mix(dve, step, n, r, cols):
            dve.wait_ge(S("rw_mz"), n + 1)
            z = rw_mz.rearrange("p (a t) -> p a t", a=2)[:, :, 0:r]
            step(dve.tensor_tensor(z, z, rw_bonus[:, :, cols], ALU.add))
            dve.tensor_tensor(mixT[:, 2:4, cols], z, mixT[:, 2:4, cols], ALU.mult).then_inc(S("rw_done"), 1)

        def rw_act_norm(act, n, r):
            act.wait_ge(S("rw_yc"), n + 1)
            act.activation(rw_sq[0:r, :], rw_yc[0:r, :], ACT.Square).then_inc(S("rw_ysq"), 1)
            act.wait_ge(S("rw_var"), n + 1)
            v = rw_ms[0:r, 1, :]
            act.activation(v, v, ACT.Ln, scale=1.0 / HD, bias=rw_col[0:r, 1:2]).then_inc(*did("act"))
            act.wait_ge(*so_far("act"))
            act.activation(v, v, ACT.Exp, scale=-0.5).then_inc(S("rw_yrs"), 1)

        def rw_act_turn(act, n, r):
            act.wait_ge(S("rw_c6"), n + 1)
            if n >= 1:
                act.wait_ge(S("rw_done"), n)
            for a in range(2):
                ins = act.activation(rw_mz[:, a * P:a * P + r], ps[:, 7, a * P:a * P + r], ACT.Identity,
                                     scale=PAR["ln_w"][:, a:a + 1], bias=PAR["ln_b"][:, a:a + 1])
            ins.then_inc(S("rw_mz"), 1)

        def rw_act(act):
            act.wait_ge(S("rw_s0p"), 1)
            act.activation(rw_s0.rearrange("p a b e -> p a (b e)"), ps[:, 6:8, :], ACT.Copy)\
                .then_inc(S("rw_s0"), 1)
            act.wait_ge(S("rw_ready"), 2)
            for item in RW_ITEMS:
                kind, n = item[0], item[1]
                r = rows(n)
                sl, e = n % 4, n % 2
                if kind == "front":
                    act.wait_ge(S("rw_np"), n + 1)
                    if n >= 4:
                        act.wait_ge(S("rw_c3"), n - 3)
                    act.activation(rw_nat[0:r, sl, 0:2, :],
                                   ps[0:r, 4, :].rearrange("p (y c) -> p y c", y=2), ACT.Copy)
                    act.activation(rw_nat[0:r, sl, 2, :], ps[0:r, 5, 0:GW], ACT.Copy).then_inc(S("rw_nat"), 1)
                elif kind == "join_b":
                    lv = item[2]
                    act.wait_ge(S("rw_jb"), rw_upto("join_b", n, lv))
                    heads = lambda t: t.rearrange("p (h t) -> p h t", h=H)[:, :, 0:r]
                    if lv != 6 and lv != rw_last_level(n):
                        act.activation(rw_x[0:r, e, :, 0:r], heads(ps[0:r, 3 * e + 1, :]), ACT.Copy)
                    act.activation(rw_xt[0:r, sl, :, 0:r], heads(ps[0:r, 3 * e + 2, :]), ACT.Copy)\
                        .then_inc(S("rw_xx"), 1)
                elif kind == "rhs":
                    act.wait_ge(S("rw_c1"), n + 1)
                    if n >= 1:
                        act.wait_ge(S("rw_c2"), n)
                    act.activation(rw_rh[0:r, :], ps[0:r, 6, 0:GW], ACT.Copy).then_inc(S("rw_rh"), 1)
                elif kind == "solve":
                    act.wait_ge(S("rw_c2"), n + 1)
                    if n >= 1:
                        act.wait_ge(S("rw_c3"), n)
                    act.activation(rw_u[0:r, :], ps[0:r, 6, GW:2 * GW], ACT.Copy).then_inc(S("rw_u"), 1)
                elif kind == "out":
                    rw_act_norm(act, n, r)
                elif kind == "turn":
                    rw_act_turn(act, n, r)

        def rws_tensor(pe):
            n, r, cols = NT - 1, SMP, slice(T, TOK)
            sl = n % 4
            nat = rw_nat[0:r, sl, :, :]
            pe.wait_ge(S("rw_mz"), NT - 1)
            pe.wait_ge(S("rw_u"), NT - 1)
            for c in range(2 * H):
                h = c % H
                rws = slice(64 * (h % 2), 64 * (h % 2) + 64)
                if c >= 2:
                    pe.wait_ge(S("rws_sel"), c - 1)
                pe.matmul(ps[0:r, 6 + c % 2, :], (rwKQ, rwR)[c // H][rws, h // 2, cols],
                          rw_s0[rws, h // 2, :, :], start=True, stop=True).then_inc(S("rws_big"), 1)
            pe.wait_ge(S("rws_sel"), 2 * H)
            pe.wait_ge(S("rw_nat"), NT)
            for h in range(H):
                hc = slice(h * HD, (h + 1) * HD)
                ins = pe.matmul(ps[0:r, 6, hc], rw_mats[0:r, sl, 1, h, 0:r], nat[:, 2, hc], start=(h == 0),
                                stop=True, skip_group_check=True)
            ins.then_inc(S("rws_c1"), 1)
            pe.wait_ge(S("rws_rh"), 1)
            pe.wait_ge(S("rw_xx"), rw_upto("join_b", n, rw_last_level(n)))
            for h in range(H):
                hc = slice(h * HD, (h + 1) * HD)
                ins = pe.matmul(ps[0:r, 6, GW + h * HD:GW + (h + 1) * HD], rw_xt[0:r, sl, h, 0:r], rw_rh[0:r, hc],
                                start=(h == 0), stop=True, skip_group_check=True)
            ins.then_inc(S("rws_c2"), 1)
            pe.wait_ge(S("rws_u"), 1)
            for h in range(H):
                hc = slice(h * HD, (h + 1) * HD)
                pe.matmul(ps[0:r, 7, hc], rw_mats[0:r, sl, 2, h, 0:r], rw_u[0:r, hc], start=(h == 0), stop=False,
                          skip_group_check=True)
                ins = pe.matmul(ps[0:r, 7, hc], rw_mats[0:r, sl, 3, h, 0:r], nat[:, 2, hc], start=False,
                                stop=True, skip_group_check=True)
            ins.then_inc(S("rws_y"), 1)
            for h in range(H):
                rws = slice(64 * (h % 2), 64 * (h % 2) + 64)
                for y in range(2):
                    pe.wait_ge(S("rws_exp"), 2 * h + y + 1)
                    pe.matmul(ps[rws, h, :], nat[:, 1 - y, h * HD:(h + 1) * HD], rw_big[0:r, :, :],
                              start=(y == 0), stop=(y == 1)).then_inc(S("rws_inc"), 1)
            pe.wait_ge(S("rw_yn"), NT)
            for a in range(2):
                ins = pe.transpose(ps[:, 7, a * P:a * P + r], rw_yc[0:r, a * P:(a + 1) * P], ident[0:r, 0:r])
            ins.then_inc(S("rw_c6"), 1)
            pe.wait_ge(S("rw_S"), NT - 1)
            for a in range(2):
                ins = pe.transpose(ps[:, 6, a * P:(a + 1) * P], rw_state[:, a * P:(a + 1) * P], ident)
            ins.then_inc(S("rw_finp"), 1)
            for g in range(4):
                pe.wait_ge(S("rws_new"), H)
                for j in range(4):
                    b = 4 * (g % 2) + j
                    ins = pe.transpose(ps[0:HD, g, j * P:(j + 1) * P], rw_s0[:, g // 2, b, :], ident)
                ins.then_inc(S("rw_fins"), 1)

        def rws_vector(dve):
            n, r, cols = NT - 1, SMP, slice(T, TOK)
            step = chain(dve, "dve")
            sm = seqmask[0:r, :].unsqueeze(2).broadcast_to([r, NB, HD])
            for c in range(2 * H):
                h = c % H
                dve.wait_ge(S("rws_big"), c + 1)
                if c >= 1:
                    dve.wait_ge(S("rws_sel"), c)
                step(dve.tensor_tensor(rw_big[0:r, :, :], ps[0:r, 6 + c % 2, :].rearrange(
                    "p (b e) -> p b e", b=NB), sm, ALU.mult))
                dve.tensor_reduce(rw_inter[0:r, c // H, h * HD:(h + 1) * HD],
                                  rw_big[0:r, :, :].rearrange("p b e -> p e b"), AX, ALU.add)\
                    .then_inc(S("rws_sel"), 1)
            dve.wait_ge(S("rws_sel"), 2 * H)
            dve.wait_ge(S("rws_c1"), 1)
            dve.wait_ge(S("rw_c2"), NT - 1)
            dve.tensor_tensor(rw_rh[0:r, :], ps[0:r, 6, 0:GW], rw_inter[0:r, 0, :], ALU.add)\
                .then_inc(S("rws_rh"), 1)
            dve.wait_ge(S("rws_y"), 1)
            step(dve.tensor_tensor(rw_inter[0:r, 1, :], ps[0:r, 7, 0:GW], rw_inter[0:r, 1, :], ALU.add))
            for h in range(H):
                rws, a = slice(64 * (h % 2), 64 * (h % 2) + 64), h // 2
                for y, src in enumerate((rw_u[0:r, :], rw_nat[0:r, n % 4, 2, :])):
                    if h or y:
                        dve.wait_ge(S("rws_inc"), 2 * h + y)
                    dve.tensor_tensor(rw_big[0:r, :, :],
                                      src[:, h * HD:(h + 1) * HD].unsqueeze(1).broadcast_to([r, NB, HD]), sm,
                                      ALU.mult).then_inc(S("rws_exp"), 1)
                dve.wait_ge(S("rws_inc"), 2 * h + 2)
                step(dve.tensor_tensor(rw_s0[rws, a, :, :], rw_s0[rws, a, :, :],
                                       ps[rws, h, :].rearrange("p (b e) -> p b e", b=NB), ALU.add))
                dve.tensor_tensor(rw_s0[rws, a, :, :], rw_s0[rws, a, :, :],
                                  rw_pc[rws, a, NT - 1:].unsqueeze(2).broadcast_to([64, NB, HD]), ALU.mult)\
                    .then_inc(S("rws_new"), 1)
            rw_norm(dve, step, n, r, rw_inter[0:r, 1, :].rearrange("p (h e) -> p h e", h=H))
            rw_mix(dve, step, n, r, cols)

        def rws_act(act):
            n, r = NT - 1, SMP
            act.wait_ge(S("rws_c2"), 1)
            act.wait_ge(S("rw_c3"), NT - 1)
            act.activation(rw_u[0:r, :], ps[0:r, 6, GW:2 * GW], ACT.Copy).then_inc(S("rws_u"), 1)
            rw_act_norm(act, n, r)
            rw_act_turn(act, n, r)
            act.wait_ge(S("rw_finp"), 1)
            act.activation(rw_stmp, ps[:, 6, 0:GW], ACT.Copy).then_inc(S("rw_fin_p"), 1)
            for g in range(4):
                act.wait_ge(S("rw_fins"), g + 1)
                act.activation(rw_s0_in[0:HD, g // 2, 4 * (g % 2):4 * (g % 2) + 4, :],
                               ps[0:HD, g, :].rearrange("p (b k) -> p b k", b=4), ACT.Copy)\
                    .then_inc(S("rw_fin_s"), 1)


        CH = 256
        NCH = FF // CH
        FT = CH // P
        x1 = at(PR, NT, D)
        H2 = PR + NT * D
        _o = H2 + 2 * KD * TOK
        w_out = at(_o, KD, D)
        y_acc = at(_o, NT, D)
        _o += KD * D
        x_again = at(_o, 2, D)
        h2 = at(_o + 2 * D, 2, D)
        post_gain = at(_o + 4 * D, D)
        d_junk = at(_o + 5 * D, D // 2).bitcast(BF16)
        d_ss = at(MIXER_CONSTS - 2 * NT, 2 * NT)
        end_gain = at(MIXER_CONSTS + P + 2048, D)
        end_junk = at(MIXER_CONSTS + P + 3072, D // 2).bitcast(BF16)
        WS = PR - 4 * 2048

        place = ExitStack()
        with place:
            below_w = place.enter_context(nc.sbuf_tensor("below_w_split", [P, WS], F32))
            w_split = place.enter_context(nc.sbuf_tensor("w_split", [P, 4, FT, 1024], F32R))
            place.enter_context(nc.sbuf_tensor("below_h2_split", [P, NT * D], F32))
            h2_split = place.enter_context(nc.sbuf_tensor("h2_split", [P, 2, KD, TOK], F32R))
            place.enter_context(nc.sbuf_tensor("below_u_split", [P, NT * D], F32))
            u_split = place.enter_context(nc.sbuf_tensor("u_split", [P, 2, FT, TOK], F32R))
            above_u = place.enter_context(nc.sbuf_tensor("above_u_split", [P, 2 * EG[0][1]], F32))
        up_hi, up_lo, dn_hi, dn_lo = (w_split[:, n, :, :] for n in range(4))
        h2_hi, h2_lo = h2_split[:, 0, :, :], h2_split[:, 1, :, :]
        u_hi, u_lo = u_split[:, 0, :, :], u_split[:, 1, :, :]
        w_raw = below_w[:, MIXER_CONSTS + P:MIXER_CONSTS + P + 2048].rearrange("p (g c) -> p g c", g=2)
        u_raw = above_u[:, :].rearrange("p (g c) -> p g c", g=2)
        h2_raw = above_u[:, 2 * EG[0][1] - 512:2 * EG[0][1]]
        w_raw = below_w[:, MIXER_CONSTS + P:MIXER_CONSTS + P + 2048].rearrange("p (g c) -> p g c", g=2)
        u_raw = above_u[:, :].rearrange("p (g c) -> p g c", g=2)
        h2_raw = above_u[:, 2 * EG[0][1] - 512:2 * EG[0][1]]

        W_LOADS = [t_loads(g) + sum(n_slot(n) == g for n in range(len(N_GROUPS)))
                   for g in range(WSLOTS)]

        def mlp_out_sync(sp):
            sp.wait_ge(S("rw_done"), NT)
            sp.wait_ge(S("rw_fin_s"), 4)
            sp.wait_ge(S("states_out"), 16 * (16 + H))
            for k0, k1, c0, done in ((0, KD // 2, 0, "w_in2"), (KD // 2, KD, 0, "w_in3"), (0, KD, 512, "w_out")):
                sp.dma_start(w_out[:, k0:k1, c0:c0 + 512],
                             A["w_out"][0].rearrange("(k p) c -> p k c", p=P)[:, k0:k1, c0:c0 + 512])\
                    .then_inc(S(done), 16)
            sp.wait_ge(S("rw_states_out"), 16 * H)
            sp.wait_ge(S("shift_out"), 32)
            sp.dma_start(post_gain, A["norm_mix_post"][0].partition_broadcast(P)).then_inc(S("params"), 16)
            for i in range(NT):
                if i >= 2:
                    sp.wait_ge(S("m_x1"), i - 1)
                sp.dma_start(x_again[0:rows(i), i % 2, :], x_rows(i)).then_inc(S(f"x_in{i % 2}"), 16)
                if i == 2:
                    for g in range(FT):
                        load_up(sp, 0, g)
            sp.wait_ge(S("m_x1"), NT)
            sp.wait_ge(S("up_split"), FT)
            for g in range(FT):
                load_down(sp, 0, g)
            sp.dma_start(end_gain, A["norm_ffn_post"][0].partition_broadcast(P)).then_inc(S("params"), 16)
            with sp.Fori(1, NCH) as c:
                for g in range(FT):
                    sp.wait_ge(S("dn_split"), c * FT + (g - 1))
                    load_up(sp, c, g)
                for g in range(FT):
                    sp.wait_ge(S("up_split"), c * FT + (g + 1))
                    load_down(sp, c, g)

        def load_up(sp, c, g):
            sp.dma_start(w_raw[:, g, :].rearrange("p (k f) -> p k f", k=KD),
                         A["w_up"][0].rearrange("(k p) (n f) -> p k n f", p=P, f=P)
                         [:, :, bass.ds(c * FT + g, 1), :].rearrange("p k n f -> p k (n f)"))\
                .then_inc(S(f"w_in{g}"), 16)

        def load_down(sp, c, g):
            sp.dma_start(w_raw[:, g, :], A["w_down"][0].rearrange("(n p) c -> p n c", p=P)
                         [:, bass.ds(c * FT + g, 1), :].rearrange("p n c -> p (n c)"))\
                .then_inc(S(f"w_in{g}"), 16)

        def out_tensor(pe):
            def transposes(i):
                r = rows(i)
                pe.wait_ge(S("xh"), NT + i + 1)
                if i >= 1:
                    pe.wait_ge(S("hT"), 2 * NT + 2 * i)
                for half in range(2):
                    for k in range(4):
                        c = (4 * half + k) * P
                        ins = pe.transpose(ps[:, 4 + half, k * P:k * P + r], h2[0:r, i % 2, c:c + P],
                                           ident[0:r, 0:r])
                    ins.then_inc(S("xT"), 1)
            pe.wait_ge(S("rw_done"), NT)
            pe.wait_ge(S("rw_fin_s"), 4)
            for i in range(NT):
                r = rows(i)
                if i >= 2:
                    pe.wait_ge(S("m_x1"), i - 1)
                for half in range(2):
                    for k in range(KD):
                        if i == 0 and half == 0 and k in (0, KD // 2):
                            pe.wait_ge(S("w_in2" if k == 0 else "w_in3"), 16 * (W_LOADS[2 + (k > 0)] + 1))
                        if i == 0 and half == 1 and k == 0:
                            pe.wait_ge(S("w_out"), 16)
                        ins = pe.matmul(ps[0:r, 2 * (i % 2) + half, :], mixT[:, k, i * P:i * P + r],
                                        w_out[:, k, half * 512:half * 512 + 512], start=(k == 0),
                                        stop=(k == KD - 1))
                ins.then_inc(S("m_o"), 1)
                if i >= 1:
                    transposes(i - 1)
            transposes(NT - 1)

        def out_act(act):
            def rms(col, src, r, want, n):
                s = d_ss[0:r, col:col + 1]
                act.wait_ge(S(want), n)
                act.activation(d_junk[0:r, :], src, ACT.Square, accum_out=s).then_inc(*did("act"))
                act.wait_ge(*so_far("act"))
                act.activation(s, s, ACT.Ln, scale=1.0 / D, bias=eps_col[0:r, :]).then_inc(*did("act"))
                act.wait_ge(*so_far("act"))
                return act.activation(s, s, ACT.Exp, scale=-0.5)
            for i in range(NT):
                r = rows(i)
                rms(2 * i, ps[0:r, 2 * (i % 2):2 * (i % 2) + 2, :].rearrange("p a c -> p (a c)"), r, "m_o",
                    i + 1 if i < NT - 1 else NT).then_inc(S("rs"), 1)
                rms(2 * i + 1, x1[0:r, i, :], r, "m_x1", i + 1).then_inc(S("m_rs2"), 1)

        def out_vector(dve):
            def evac(i):
                r = rows(i)
                for half in range(2):
                    dve.wait_ge(S("xT"), 2 * NT + 2 * i + half + 1)
                    src = ps[:, 4 + half, :].rearrange("p (k t) -> p k t", k=4)[:, :, 0:r]
                    g = gain_ffn[:, 4 * half:4 * half + 4].unsqueeze(2).broadcast_to([P, 4, r])
                    hi, lo = (t[:, 4 * half:4 * half + 4, i * P:i * P + r] for t in (h2_hi, h2_lo))
                    raw = h2_raw.rearrange("p (k t) -> p k t", k=4)[:, :, 0:r]
                    dve.wait_ge(S("hT"), 2 * NT + 2 * i + half)
                    step(dve.tensor_tensor(raw, src, g, ALU.mult))
                    step(dve.tensor_copy(hi, raw))
                    dve.tensor_tensor(lo, raw, hi.bitcast(F32), ALU.subtract).then_inc(S("hT"), 1)
            step = chain(dve, "dve")
            for i in range(NT):
                r = rows(i)
                dve.wait_ge(S("rs"), NT + i + 1)
                if i == 0:
                    dve.wait_ge(S("params"), 16 * (N_PAR_DMA + 1))
                o = ps[0:r, 2 * (i % 2):2 * (i % 2) + 2, :].rearrange("p a c -> p (a c)")
                step(dve.scalar_tensor_tensor(x1[0:r, i, :], o, d_ss[0:r, 2 * i:2 * i + 1], post_gain[0:r, :],
                                              ALU.mult, ALU.mult))
                dve.wait_ge(S(f"x_in{i % 2}"), 16 * (3 + i // 2 + 1))
                dve.tensor_tensor(x1[0:r, i, :], x1[0:r, i, :], x_again[0:r, i % 2, :], ALU.add)\
                    .then_inc(S("m_x1"), 1)
                if i >= 1:
                    evac(i - 1)
                dve.wait_ge(S("m_rs2"), i + 1)
                dve.tensor_scalar(h2[0:r, i % 2, :], x1[0:r, i, :], d_ss[0:r, 2 * i + 1:2 * i + 2], None,
                                  ALU.mult).then_inc(S("xh"), 1)
            evac(NT - 1)

        NUP = 3 * FT
        UP_TILES = [(ft, tg) for tg in range(3) for ft in range(FT)]

        def mlp_tensor(pe):
            def chunk(c, first):
                for q, (ft, tg) in enumerate(UP_TILES):
                    t0, tw = EG[tg]
                    if q < FT:
                        pe.wait_ge(S("up_split"), c * FT + (q + 1))
                    if not first or q >= 2:
                        pe.wait_ge(S("up_relu"), c * NUP + (q - 1))
                    for k in range(KD):
                        ins = three(pe, ps[:, q % 2, 0:tw], up_hi[:, ft, k * P:k * P + P],
                                    up_lo[:, ft, k * P:k * P + P], h2_hi[:, k, t0:t0 + tw],
                                    h2_lo[:, k, t0:t0 + tw], k == 0, k == KD - 1)
                    ins.then_inc(S("up_ps"), 1)
                for i in range(NT):
                    r = rows(i)
                    if i == 0:
                        pe.wait_ge(S("dn_split"), c * FT + FT)
                    if i * P in [t0 for t0, _ in EG]:
                        tg = [t0 for t0, _ in EG].index(i * P)
                        pe.wait_ge(S("u_split"), c * NUP + FT * (tg + 1))
                    if not first or i >= 3:
                        pe.wait_ge(S("dn_out"), c * NT + (i - 1))
                    for half in range(2):
                        cols = slice(half * 512, half * 512 + 512)
                        for k in range(FT):
                            x_hi, x_lo = (t[:, k, i * P:i * P + r] for t in (u_hi, u_lo))
                            ins = three(pe, ps[0:r, 2 + 2 * (i % 3) + half, :], x_hi, x_lo, dn_hi[:, k, cols],
                                        dn_lo[:, k, cols], k == 0, k == FT - 1)
                    ins.then_inc(S("dn_ps"), 1)
            pe.wait_ge(S("hT"), 4 * NT)
            pe.wait_ge(S("m_x1"), NT)
            chunk(0, True)
            with pe.Fori(1, NCH) as c:
                chunk(c, False)

        def mlp_act(act):
            def high(name, raw, hi, c, g, n):
                act.wait_ge(S(f"w_in{g}"), n * 16 + 16 * W_LOADS[g])
                act.activation(hi[:, g, :], raw[:, g, :], ACT.Copy).then_inc(S(name + "_hi"), 1)

            def chunk(c, first):
                if not first:
                    act.wait_ge(S("up_ps"), c * NUP)
                for g in range(FT):
                    high("up", w_raw, up_hi, c, g, c * 2 + 1)
                if not first:
                    act.wait_ge(S("dn_ps"), c * NT)
                for g in range(FT):
                    high("dn", w_raw, dn_hi, c, g, c * 2 + 2)
                for q, (ft, tg) in enumerate(UP_TILES):
                    t0, tw = EG[tg]
                    act.wait_ge(S("up_ps"), c * NUP + (q + 1))
                    if not first or q >= 2:
                        act.wait_ge(S("u_split"), c * NUP + (q - 1))
                    u = u_raw[:, q % 2, 0:tw]
                    act.activation(u, ps[:, q % 2, 0:tw], ACT.Relu).then_inc(S("up_relu"), 1)
                    act.wait_ge(S("up_relu"), c * NUP + (q + 1))
                    act.activation(u_hi[:, ft, t0:t0 + tw], u, ACT.Square)
                    act.activation(u, u, ACT.Square).then_inc(S("up_out"), 1)
            chunk(0, True)
            with act.Fori(1, NCH) as c:
                chunk(c, False)
            for i in range(NT):
                r = rows(i)
                s = d_ss[0:r, 2 * i:2 * i + 1]
                act.wait_ge(S("dn_out"), (NCH - 1) * NT + i + 2)
                act.activation(end_junk[0:r, :], y_acc[0:r, i, :], ACT.Square, accum_out=s)\
                    .then_inc(*did("act"))
                act.wait_ge(*so_far("act"))
                act.activation(s, s, ACT.Ln, scale=1.0 / D, bias=eps_col[0:r, :]).then_inc(*did("act"))
                act.wait_ge(*so_far("act"))
                act.activation(s, s, ACT.Exp, scale=-0.5).then_inc(S("rs"), 1)

        def mlp_vector(dve):
            def low(name, raw, hi, lo, c):
                for g in range(FT):
                    dve.wait_ge(S(name + "_hi"), c * FT + (g + 1))
                    dve.tensor_tensor(lo[:, g, :], raw[:, g, :], hi[:, g, :].bitcast(F32), ALU.subtract)\
                        .then_inc(S(name + "_split"), 1)

            def low_u(c):
                for q, (ft, tg) in enumerate(UP_TILES):
                    t0, tw = EG[tg]
                    hi, lo = u_hi[:, ft, t0:t0 + tw], u_lo[:, ft, t0:t0 + tw]
                    dve.wait_ge(S("up_out"), c * NUP + (q + 1))
                    dve.tensor_tensor(lo, u_raw[:, q % 2, 0:tw], hi.bitcast(F32), ALU.subtract)\
                        .then_inc(S("u_split"), 1)

            def finish(i):
                r = rows(i)
                y = y_acc[0:r, i, :]
                dve.wait_ge(S("rs"), 2 * NT + i + 1)
                dve.scalar_tensor_tensor(y, y, d_ss[0:r, 2 * i:2 * i + 1], end_gain[0:r, :], ALU.mult,
                                         ALU.mult).then_inc(S("xh"), 1)

            def accumulate(n, tiles):
                for i in tiles:
                    r = rows(i)
                    dve.wait_ge(S("dn_ps"), n * NT + (i + 1 - NT))
                    if i == 0:
                        dve.wait_ge(S("dn_out"), n * NT + (1 - NT))
                    p = ps[0:r, 2 + 2 * (i % 3):4 + 2 * (i % 3), :].rearrange("p a c -> p (a c)")
                    dve.tensor_tensor(y_acc[0:r, i, :], y_acc[0:r, i, :], p, ALU.add).then_inc(S("dn_out"), 1)

            low("up", w_raw, up_hi, up_lo, 0)
            low("dn", w_raw, dn_hi, dn_lo, 0)
            low_u(0)
            with dve.Fori(1, NCH) as c:
                accumulate(c, range(0, 3))
                low("up", w_raw, up_hi, up_lo, c)
                accumulate(c, range(3, NT))
                low("dn", w_raw, dn_hi, dn_lo, c)
                low_u(c)
            dve.wait_ge(S("params"), 16 * (N_PAR_DMA + 2))
            for i in range(NT):
                accumulate(NCH, [i])
                if i >= 1:
                    finish(i - 1)
            finish(NT - 1)

        def residual_gpsimd(pool):
            for i in range(NT):
                y = y_acc[0:rows(i), i, :]
                pool.wait_ge(S("xh"), 2 * NT + i + 1)
                pool.tensor_tensor(y, y, x1[0:rows(i), i, :], ALU.add).then_inc(S("y_ready"), 1)

        def y_out_sync(sp):
            for i in range(NT):
                sp.wait_ge(S("y_ready"), i + 1)
                dst = (O["y_prompt"][0, i * P:(i + 1) * P, :] if i < NT - 1
                       else O["y_sample"].rearrange("b t d -> (b t) d"))
                sp.dma_start(dst, y_acc[0:rows(i), i, :]).then_inc(S("y_out"), 16)
            sp.wait_ge(S("y_out"), 16 * NT)

        @block.sync
        def _(sp):
            norm_in_sync(sp)
            project_sync(sp)
            decode_load_sync(sp)
            la_load_sync(sp)
            mlp_out_sync(sp)
            y_out_sync(sp)

        @block.scalar
        def _(act):
            norm_in_act(act)
            project_act(act)
            sb_act(act)
            decode_act(act)
            la_act(act)
            rw_prep_act(act)
            rw_act(act)
            rws_act(act)
            out_act(act)
            mlp_act(act)

        @block.gpsimd
        def _(pool):
            make_identity(pool)
            norm_in_gpsimd(pool)
            make_constants(pool)
            caches_out_gpsimd(pool)
            sb_gpsimd(pool)
            decode_load_gpsimd(pool)
            la_gpsimd(pool)
            rw_gpsimd(pool)
            pool.wait_ge(S("m_x1"), NT)
            pool.memset(y_acc, 0.0).then_inc(S("dn_out"), 1)
            residual_gpsimd(pool)
            pool.wait_ge(S("rw_states_out"), 16 * H)
            pool.wait_ge(S("states_out"), 16 * (16 + H))
            pool.wait_ge(S("sk_out"), 32)
            pool.wait_ge(S("sv_out"), 32)

        @block.tensor
        def _(pe):
            norm_in_tensor(pe)
            project_tensor(pe)
            sb_tensor(pe)
            decode_tensor(pe)
            la_tensor(pe)
            rw_prep_tensor(pe)
            rw_tensor(pe)
            rws_tensor(pe)
            out_tensor(pe)
            mlp_tensor(pe)

        @block.vector
        def _(dve):
            norm_in_vector(dve)
            project_vector(dve)
            sb_vector(dve)
            decode_vector(dve)
            la_clear_vector(dve)
            la_vector(dve)
            rw_prep_vector(dve)
            rw_vector(dve)
            rws_vector(dve)
            out_vector(dve)
            mlp_vector(dve)


INPUTS = ("x_prompt", "x_sample", "cache_sb_k", "cache_sb_v", "page_table", "state_hgrn", "state_rwkv",
          "state_rwkv_shift", "state_gla", "norm_mix_pre", "norm_mix_post", "norm_ffn_pre", "norm_ffn_post",
          "w_in", "w_out", "w_up", "w_down", "hg_norm", "rw_mu", "rw_w0", "rw_w2", "rw_a0", "rw_a2",
          "rw_g2", "rw_k_k", "rw_k_a", "rw_r_k", "rw_ln_w", "rw_ln_b", "sb_bias", "gla_a2", "gla_a_b", "gla_norm")
OUTPUTS = (("y_prompt", (1, T, D)), ("y_sample", (NB, NS, D)),
           ("sb_k_prompt", (1, 1, T, H, HD)), ("sb_v_prompt", (1, 1, T, H, HD)),
           ("sb_k_sample", (1, NB, NS, H, HD)), ("sb_v_sample", (1, NB, NS, H, HD)),
           ("hgrn_prompt", (1, 1, H, HD, HD)), ("hgrn_sample", (1, NB, H, HD, HD)),
           ("rwkv_prompt", (1, 1, H, HD, HD)), ("rwkv_sample", (1, NB, H, HD, HD)),
           ("rwkv_shift_prompt", (1, 1, 896)), ("rwkv_shift_sample", (1, NB, 896)),
           ("gla_prompt", (1, 1, H, 32, HD)), ("gla_sample", (1, NB, H, 32, HD)))


def kernel(**inputs):
    import numpy as np
    from concourse import bacc
    from concourse.bass_utils import run_bass_kernel_spmd

    nc = bacc.Bacc("TRN2", target_bir_lowering=False, num_devices=1)
    arrays, A, O = {}, {}, {}
    for name in INPUTS:
        a = np.ascontiguousarray(inputs[name])
        arrays[f"in_{name}"] = a
        A[name] = nc.dram_tensor(f"in_{name}", a.shape, mybir.dt.from_np(a.dtype), kind="ExternalInput").ap()
    for name, shape in OUTPUTS:
        O[name] = nc.dram_tensor(f"out_{name}", shape, F32, kind="ExternalOutput").ap()
    build(nc, A, O)
    r = run_bass_kernel_spmd(nc, [arrays], core_ids=[0])
    return tuple(r.results[0][f"out_{name}"] for name, _ in OUTPUTS)
```
